# Optimizing a Trainium2 kernel written in Bass

```python
import jax, jax.numpy as jnp
from jax import lax
import numpy as np

D_MODEL = 1024
BATCH = 1
SEQ = 256
DEPTH = 1
DEC_BATCH = 8
DEC_SEQ = 8
PAST_LEN = 2048
PAGE_SIZE = 128

CHUNK = 128
A_GROUPS = 8
A_GROUP_DIM = D_MODEL // 8
A_WIDTH = A_GROUPS * A_GROUP_DIM
POOL_WINDOWS = (2, 4, 8, 16)
POOL_GROUPS = len(POOL_WINDOWS)
POOL_GROUP_DIM = D_MODEL // 8
POOL_WIDTH = POOL_GROUPS * POOL_GROUP_DIM
POOL_HIST = max(POOL_WINDOWS) - 1
MEM_LEN = 256
MEM_HEADS = 4
MEM_HEAD_DIM = D_MODEL // 8
MEM_WIDTH = MEM_HEADS * MEM_HEAD_DIM
N_BRANCHES = 3
OFF_P = 2 * A_WIDTH
OFF_Q = OFF_P + POOL_WIDTH
OFF_G = OFF_Q + MEM_WIDTH
C_IN = OFF_G + N_BRANCHES * D_MODEL
N_EXPERTS = 32
TOP_K = 4
D_FF = D_MODEL
SWIGLU_LIMIT = 7.0
SWIGLU_ALPHA = 1.702
EXPERT_BLOCK = 128
LN_EPS = 1e-5
DN_ALPHA = (2 * DEPTH) ** 0.25
DN_BETA = (8 * DEPTH) ** -0.25

kernel_name = 'gated_hybrid_chunkmlp_pool_memattn_moe'

def layer_norm(x, g, b):
    xf = x.astype(jnp.float32)
    mu = jnp.mean(xf, axis=-1, keepdims=True)
    xc = xf - mu
    var = jnp.mean(xc * xc, axis=-1, keepdims=True)
    return (xc * lax.rsqrt(var + LN_EPS) * g + b).astype(x.dtype)

def spatial_gating(v, w_s, b_s):
    L = v.shape[2]
    mask = jnp.tril(jnp.ones((L, L), dtype=bool))
    w = jnp.where(mask, w_s[:, :L, :L], 0.0).astype(v.dtype)
    out = jnp.einsum('gts,ncsge->nctge', w, v)
    return out + b_s[:, :L].T.astype(v.dtype)[None, None, :, :, None]

def pool_mix(p_ext, pos0, w_pool, ls_pool):
    N = p_ext.shape[0]
    L = p_ext.shape[1] - POOL_HIST
    pf = p_ext.astype(jnp.float32)
    cs = jnp.concatenate([jnp.zeros_like(pf[:, :1]), jnp.cumsum(pf, axis=1)], axis=1)
    pos = pos0 + jnp.arange(L)
    tok = pf[:, POOL_HIST:]
    outs = []
    for g, w in enumerate(POOL_WINDOWS):
        c0, c1 = g * POOL_GROUP_DIM, (g + 1) * POOL_GROUP_DIM
        wsum = cs[:, POOL_HIST + 1:, c0:c1] - cs[:, POOL_HIST + 1 - w:POOL_HIST + 1 - w + L, c0:c1]
        cnt = jnp.minimum(w, pos + 1).astype(jnp.float32)[None, :, None]
        outs.append(wsum / cnt - tok[:, :, c0:c1])
    d = jnp.stack(outs, axis=2).astype(p_ext.dtype)
    y = jnp.einsum('nlgc,gcd->nlgd', d, w_pool).reshape(N, L, POOL_WIDTH)
    return y * ls_pool

def mem_attend(q, k, v):
    s = jnp.einsum('nlhd,nmhd->nhlm', q, k).astype(jnp.float32) * (MEM_HEAD_DIM ** -0.5)
    pr = jax.nn.softmax(s, axis=-1).astype(v.dtype)
    return jnp.einsum('nhlm,nmhd->nlhd', pr, v)

def token_mix(x, pool_prev, mem_k, mem_v, pos0, w_in, b_in, ln_v_g, ln_v_b, w_s, b_s,
              w_a_out, w_pool, ls_pool, w_b_out, w_m_out, w_o):
    N, L, _ = x.shape
    proj = x @ w_in + b_in
    z = jax.nn.gelu(proj[..., :OFF_P])
    u, v = z[..., :A_WIDTH], z[..., A_WIDTH:]
    p = proj[..., OFF_P:OFF_Q]
    q = proj[..., OFF_Q:OFF_G]
    gates = jax.nn.sigmoid(proj[..., OFF_G:].reshape(N, L, N_BRANCHES, D_MODEL))
    v = layer_norm(v, ln_v_g, ln_v_b)
    cl = min(L, CHUNK)
    mixed = spatial_gating(v.reshape(N, L // cl, cl, A_GROUPS, A_GROUP_DIM), w_s, b_s)
    br_a = (u * mixed.reshape(N, L, A_WIDTH)) @ w_a_out
    p_ext = jnp.concatenate([pool_prev.astype(p.dtype), p], axis=1)
    br_b = pool_mix(p_ext, pos0, w_pool, ls_pool) @ w_b_out
    o = mem_attend(q.reshape(N, L, MEM_HEADS, MEM_HEAD_DIM), mem_k.astype(q.dtype), mem_v.astype(q.dtype))
    br_m = o.reshape(N, L, MEM_WIDTH) @ w_m_out
    h = gates[:, :, 0] * br_a + gates[:, :, 1] * br_b + gates[:, :, 2] * br_m
    return h @ w_o, p_ext[:, -POOL_HIST:], v

def moe_ffn(x2d, w_r, b_r, w1, b1, w2, b2):
    T, D = x2d.shape
    logits = (x2d @ w_r + b_r).astype(jnp.float32)
    top_v, top_e = lax.top_k(logits, TOP_K)
    gate = jax.nn.softmax(top_v, axis=-1).astype(x2d.dtype)
    n_assign = T * TOP_K
    e_flat = top_e.reshape(n_assign)
    tok_flat = jnp.arange(n_assign, dtype=jnp.int32) // TOP_K
    g_flat = gate.reshape(n_assign)
    order = jnp.argsort(e_flat)
    e_sorted = e_flat[order]
    counts = jnp.bincount(e_flat, length=N_EXPERTS)
    padded = (counts + EXPERT_BLOCK - 1) // EXPERT_BLOCK * EXPERT_BLOCK
    pad_end = jnp.cumsum(padded)
    pad_start = pad_end - padded
    start = jnp.cumsum(counts) - counts
    dest = pad_start[e_sorted] + jnp.arange(n_assign, dtype=pad_end.dtype) - start[e_sorted]
    n_blocks = -(-n_assign // EXPERT_BLOCK) + N_EXPERTS
    n_slots = n_blocks * EXPERT_BLOCK
    slot_tok = jnp.full((n_slots,), T, jnp.int32).at[dest].set(tok_flat[order])
    slot_g = jnp.zeros((n_slots,), x2d.dtype).at[dest].set(g_flat[order])
    blk_start = jnp.arange(n_blocks, dtype=pad_end.dtype) * EXPERT_BLOCK
    blk_e = jnp.minimum(jnp.searchsorted(pad_end, blk_start, side='right'), N_EXPERTS - 1)
    x_pad = jnp.concatenate([x2d, jnp.zeros((1, D), x2d.dtype)], axis=0)
    xs = x_pad[slot_tok].reshape(n_blocks, EXPERT_BLOCK, D)

    def expert_block(args):
        xb, e = args
        h = xb @ w1[e] + b1[e]
        g = jnp.minimum(h[:, :D_FF], SWIGLU_LIMIT)
        lin = jnp.clip(h[:, D_FF:], -SWIGLU_LIMIT, SWIGLU_LIMIT)
        act = g * jax.nn.sigmoid(SWIGLU_ALPHA * g) * (lin + 1.0)
        return act @ w2[e] + b2[e]

    out = lax.map(expert_block, (xs, blk_e)).reshape(n_slots, D)
    y = jnp.zeros((T + 1, D), x2d.dtype).at[slot_tok].add(out * slot_g[:, None])
    return y[:T]

def setup_inputs(seed: int = 0) -> dict:
    key = jax.random.key(seed)
    ks = jax.random.split(key, 32)

    def nrm(k, shape, scale):
        return jax.random.normal(k, shape, jnp.float32) * scale

    tri = jnp.tril(jnp.ones((CHUNK, CHUNK), jnp.float32))
    return {
        'x_prompt': nrm(ks[0], (BATCH, SEQ, D_MODEL), 1.0),
        'x_sample': nrm(ks[1], (DEC_BATCH, DEC_SEQ, D_MODEL), 1.0),
        'state_pool': nrm(ks[2], (DEPTH, DEC_BATCH, POOL_HIST, POOL_WIDTH), 1.0),
        'cache_mem_k': nrm(ks[3], (DEPTH, DEC_BATCH, MEM_LEN, MEM_HEADS, MEM_HEAD_DIM), 1.0),
        'cache_mem_v': nrm(ks[4], (DEPTH, DEC_BATCH, MEM_LEN, MEM_HEADS, MEM_HEAD_DIM), 1.0),
        'mem_prompt': nrm(ks[5], (BATCH, MEM_LEN, D_MODEL), 1.0),
        'w_in': nrm(ks[6], (DEPTH, D_MODEL, C_IN), D_MODEL ** -0.5),
        'b_in': nrm(ks[7], (DEPTH, C_IN), 0.02),
        'ln_v_g': 1.0 + nrm(ks[8], (DEPTH, A_WIDTH), 0.05),
        'ln_v_b': nrm(ks[9], (DEPTH, A_WIDTH), 0.02),
        'w_s': nrm(ks[10], (DEPTH, A_GROUPS, CHUNK, CHUNK), CHUNK ** -0.5) * tri,
        'b_s': 1.0 + nrm(ks[11], (DEPTH, A_GROUPS, CHUNK), 0.1),
        'w_a_out': nrm(ks[12], (DEPTH, A_WIDTH, D_MODEL), A_WIDTH ** -0.5),
        'w_pool': nrm(ks[13], (DEPTH, POOL_GROUPS, POOL_GROUP_DIM, POOL_GROUP_DIM), POOL_GROUP_DIM ** -0.5),
        'ls_pool': 1.0 + nrm(ks[14], (DEPTH, POOL_WIDTH), 0.1),
        'w_b_out': nrm(ks[15], (DEPTH, POOL_WIDTH, D_MODEL), POOL_WIDTH ** -0.5),
        'w_mk': nrm(ks[16], (DEPTH, D_MODEL, MEM_WIDTH), D_MODEL ** -0.5),
        'w_mv': nrm(ks[17], (DEPTH, D_MODEL, MEM_WIDTH), D_MODEL ** -0.5),
        'w_m_out': nrm(ks[18], (DEPTH, MEM_WIDTH, D_MODEL), MEM_WIDTH ** -0.5),
        'w_o': nrm(ks[19], (DEPTH, D_MODEL, D_MODEL), D_MODEL ** -0.5 * DN_BETA),
        'ln1_g': 1.0 + nrm(ks[20], (DEPTH, D_MODEL), 0.05),
        'ln1_b': nrm(ks[21], (DEPTH, D_MODEL), 0.02),
        'w_r': nrm(ks[22], (DEPTH, D_MODEL, N_EXPERTS), D_MODEL ** -0.5),
        'b_r': nrm(ks[23], (DEPTH, N_EXPERTS), 0.01),
        'w1': nrm(ks[24], (DEPTH, N_EXPERTS, D_MODEL, 2 * D_FF), D_MODEL ** -0.5),
        'b1': nrm(ks[25], (DEPTH, N_EXPERTS, 2 * D_FF), 0.02),
        'w2': nrm(ks[26], (DEPTH, N_EXPERTS, D_FF, D_MODEL), D_FF ** -0.5 * DN_BETA),
        'b2': nrm(ks[27], (DEPTH, N_EXPERTS, D_MODEL), 0.02),
        'ln2_g': 1.0 + nrm(ks[28], (DEPTH, D_MODEL), 0.05),
        'ln2_b': nrm(ks[29], (DEPTH, D_MODEL), 0.02),
    }

def reference(x_prompt, x_sample, state_pool, cache_mem_k, cache_mem_v, mem_prompt,
              w_in, b_in, ln_v_g, ln_v_b, w_s, b_s, w_a_out, w_pool, ls_pool, w_b_out,
              w_mk, w_mv, w_m_out, w_o, ln1_g, ln1_b, w_r, b_r, w1, b1, w2, b2, ln2_g, ln2_b):
    y_p, y_s = x_prompt, x_sample
    pool_p_out, pool_s_out, mk_out, mv_out, cv_out = [], [], [], [], []
    for l in range(DEPTH):
        mk_p = (mem_prompt @ w_mk[l]).reshape(BATCH, MEM_LEN, MEM_HEADS, MEM_HEAD_DIM)
        mv_p = (mem_prompt @ w_mv[l]).reshape(BATCH, MEM_LEN, MEM_HEADS, MEM_HEAD_DIM)
        shared = (w_in[l], b_in[l], ln_v_g[l], ln_v_b[l], w_s[l], b_s[l], w_a_out[l],
                  w_pool[l], ls_pool[l], w_b_out[l], w_m_out[l], w_o[l])
        zero_hist = jnp.zeros((y_p.shape[0], POOL_HIST, POOL_WIDTH), y_p.dtype)
        t_p, pool_p, _ = token_mix(y_p, zero_hist, mk_p, mv_p, 0, *shared)
        t_s, pool_s, v_s = token_mix(y_s, state_pool[l], cache_mem_k[l], cache_mem_v[l], PAST_LEN, *shared)
        y_p = layer_norm(DN_ALPHA * y_p + t_p, ln1_g[l], ln1_b[l])
        y_s = layer_norm(DN_ALPHA * y_s + t_s, ln1_g[l], ln1_b[l])
        f_p = moe_ffn(y_p.reshape(-1, D_MODEL), w_r[l], b_r[l], w1[l], b1[l], w2[l], b2[l]).reshape(y_p.shape)
        f_s = moe_ffn(y_s.reshape(-1, D_MODEL), w_r[l], b_r[l], w1[l], b1[l], w2[l], b2[l]).reshape(y_s.shape)
        y_p = layer_norm(DN_ALPHA * y_p + f_p, ln2_g[l], ln2_b[l])
        y_s = layer_norm(DN_ALPHA * y_s + f_s, ln2_g[l], ln2_b[l])
        pool_p_out.append(pool_p)
        pool_s_out.append(pool_s)
        mk_out.append(mk_p)
        mv_out.append(mv_p)
        cv_out.append(v_s)
    return (y_p, y_s, jnp.stack(pool_p_out), jnp.stack(pool_s_out), jnp.stack(mk_out), jnp.stack(mv_out), jnp.stack(cv_out))


_drawn_inputs = setup_inputs


def setup_inputs(seed=0):
    import zlib

    import numpy as np

    out = dict(_drawn_inputs(seed))
    spreads = {}
    factors = {'ln_v_b': 2.858, 'b_r': 4.106, 'b1': 8.0, 'b2': 6.425, 'ln2_b': 2.93}
    for name, (base, spread) in spreads.items():
        noise = np.random.default_rng([zlib.crc32(name.encode()), seed]).standard_normal(out[name].shape)
        drawn = base * np.exp(spread * noise) if base else spread * noise
        out[name] = __import__('jax').numpy.asarray(drawn.astype(out[name].dtype))
    for name, factor in factors.items():
        out[name] = (out[name] * factor).astype(out[name].dtype)
    return out
```

```python
from contextlib import ExitStack

import concourse.bass as bass
from concourse import mybir

F32 = mybir.dt.float32
BF16 = mybir.dt.bfloat16
I32 = mybir.dt.int32
ALU = mybir.AluOpType
ACT = mybir.ActivationFunctionType
AX = mybir.AxisListType

P = 128
D = 1024
KD = D // P
SEQ, NB, LS = 256, 8, 8
T = SEQ + NB * LS
ROWS = [128, 128, 64]
GA = 8
HEADS, MEM = 4, 256
PG, HIST = 4, 15
WINDOWS = [2, 4, 8, 16]
NE, TOPK = 32, 4
CAP = 64
PASSES = T // CAP
SCALE = float(P) ** -0.5
EPS = 1e-5
ALPHA = 2.0 ** 0.25
SW_LIMIT, SW_ALPHA = 7.0, 1.702

SLOT = 2048
RING = 12
SEG = HIST + LS
EXT = HIST + SEQ + NB * SEG


def head_slots():
    s = [("v", i) for i in range(4)] + [("u", i) for i in range(4)] + [("mem", 0)]
    s += [(w, i) for w in ("mk", "mv", "q") for i in range(2)]
    s += [(w, i) for w in ("kc", "vc") for i in range(4)] + [("p", i) for i in range(2)]
    for i in range(4):
        s += [("gA", i), ("wa", i)]
    for g, w in (("gB", "wb"), ("gM", "wm")):
        for i in range(2):
            s += [(g, 2 * i), (g, 2 * i + 1), (w, i)]
    return s + [("wo", i) for i in range(4)]


def head_tiles():
    t = [("bias", 0)] + [("xT", k) for k in range(KD)]
    t += [("v", s, j) for s in range(4) for j in range(2)] + [("u", c) for c in range(KD)]
    t += [("ws", 0), ("ws", 1), ("bd", 0)] + [("mix", g) for g in range(GA)]
    t += [("mem", i) for i in range(4)] + [(w, i) for w in ("mk", "mv", "mkp") for i in range(2)]
    t += [("q", h) for h in range(HEADS)] + [("sc", h) for h in range(HEADS)]
    for hp in range(2):
        t += [("kt", hp, b) for b in range(NB)] + [("ss", hp)]
    t += [("pt", 0), ("pt", 1), ("o", 0), ("pt", 2), ("o", 1), ("pt", 3), ("o", 2), ("o", 3)]
    t += [("pst", 0), ("pst", 1), ("so", 0), ("hist", 0)] + [("p", g) for g in range(PG)] + [("pout", 0)]
    for i in range(4):
        t += [("gA", 2 * i), ("gA", 2 * i + 1), ("wa", 2 * i), ("wa", 2 * i + 1)]
    t += [("yb", g) for g in range(PG)]
    for g, w in (("gB", "wb"), ("gM", "wm")):
        for i in range(2):
            t += [(g, 4 * i + c) for c in range(4)] + [(w, 4 * i + c) for c in range(4)]
    t += [("wo", s, j) for s in range(4) for j in range(2)] + [("x1T", k) for k in range(KD)]
    t += [("rt", 0), ("rank", 0), ("gT", 0)]
    return t + [("b2", i) for i in range(6)]


SLOTS = {key: n for n, key in enumerate(head_slots())}
TILES = {key: n for n, key in enumerate(head_tiles())}
NH = len(SLOTS)


def build(nc, a, o):
    ctx = ExitStack()
    with ctx:
        def sem(name):
            return ctx.enter_context(nc.semaphore(name))

        top = [(nc.sbuf_base + 63) // 64 * 64]

        def region(nbytes):
            at = top[0]
            top[0] += (nbytes + 31) // 32 * 32
            assert top[0] <= nc.sbuf_usable_end
            return at

        def at(name, shape, off, dt=F32):
            return nc.alloc_sbuf_tensor_at(name, shape, dt, offset=off)

        def small(name, shape, dt=F32):
            n = 4
            for x in shape[1:]:
                n *= x
            return at(name, shape, region(n), dt)

        ring = at("ring", [P, RING, SLOT], region(RING * SLOT * 4))
        x = small("x", [P, 3, D])
        rC = region(12288)
        vn = at("vn", [P, 3, D], rC)
        mkT = at("mkT", [P, HEADS, MEM], rC)
        mvp = at("mvp", [P, 2, HEADS * P], rC + 4096)
        mkp = at("mkp", [P, 2, HEADS * P], rC + 8192)
        pcur = at("pcur", [P, PG, T], rC)
        ybT = at("ybT", [P, PG, T], rC)
        dT = at("dT", [P, PG, T], rC + 5120)
        yacc = at("yacc", [P, 3, D], rC)
        rD = region(10240)
        xT = at("xT", [P, KD, T], rD)
        x1T = at("x1T", [P, KD, T], rD)
        pick = at("pick", [P, 2, 3, CAP], rD)
        pickg = at("pickg", [P, 3, 2, CAP], rD + 1536)
        rE = region(23040)
        bvb = at("bvb", [P, 3, D], rE)
        memT = at("memT", [P, KD, MEM], rE + 12288)
        kTs = at("kTs", [P, NB, 2, MEM], rE)
        QSTEP = NB * LS + LS
        qmask = at("qmask", [P, 2, NB * QSTEP], rE + 16384)
        Ps = at("Ps", [P, 2, MEM], rE + 20992)
        ext = [at(f"ext{i}", [P, PG, EXT], rE + 7296 * i) for i in range(3)]
        lnb = at("lnb", [P, 4, D], rE)
        b2s = at("b2s", [NE, D], rE + 16384)
        rF = region(10240)
        qT = at("qT", [P, HEADS, T], rF)
        oT = at("oT", [P, HEADS, T], rF + 5120)
        b1s = at("b1s", [3 * NE, 2 * D], rF, BF16)
        ypair = at("ypair", [P, D], rF + 4096)
        rG = region(8192)
        wsr = at("wsr", [P, GA, P], rG)
        Pp = at("Pp", [P, HEADS, 2, MEM], rG)
        pout = at("pout", [P, PG * P], rG)
        gm, sg, lin, gs = (at(n, [P, 512], rG + 2048 * i) for i, n in enumerate(("gm", "sg", "lin", "gs")))
        rH = region(10240)
        uT = at("uT", [P, KD, T], rH)
        b1x = at("b1x", [3 * NE, 2 * D], rH)
        rJ = region(10240)
        wsT = at("wsT", [P, GA, P], rJ)
        bd = at("bd", [NB * LS, GA, NB * LS], rJ + 4096)
        bsb = at("bsb", [P, GA, P], rJ + 6144)
        histr = at("histr", [NB * HIST, PG * P], rJ)
        PTs = at("PTs", [P, 2, 2, P], rJ + 4096)
        hT = at("hT", [P, KD, T], rJ)
        xg = at("xg", [P, KD, CAP], rJ)
        act_s = at("act_s", [P, 512], rJ + 2048)
        actT = at("actT", [P, 4, 2, CAP], rJ + 4096)
        pickT = at("pickT", [P, T], rJ + 6144)
        rK = region(5120)
        gbuf = at("gbuf", [P, 4, T], rK)
        PT = at("PT", [P, 2, 2, SEQ], rK)
        mtmp = at("mtmp", [P, 2, T], rK)
        ident = small("ident", [P, P])
        upper = small("upper", [P, P])
        ones = small("ones", [P, P])
        slotj = small("slotj", [P, CAP])
        slotj_i = at("slotj_i", [P, CAP], rJ, I32)
        bdmask = small("bdmask", [NB * LS, NB, LS])
        rep8 = small("rep8", [LS, NB, LS])
        selcol = small("selcol", [3 * NE, NE + 1])
        sel = small("sel", [3 * NE, 2, CAP], BF16)
        zeros32 = small("zeros32", [P, NE])
        pos_i = at("pos_i", [P, HIST + 1], rJ + 256, I32)
        pos_f = at("pos_f", [P, HIST + 1], rJ + 320)
        ratio = small("ratio", [P, PG, HIST + 1])
        thr = small("thr", [1, PASSES - 1])
        wpool = at("wpool", [P, PG, P], region(2048))
        brow = at("brow", [52, P], rK + 4096)
        bT = small("bT", [P, 52])
        wr = small("wr", [P, KD, NE])
        brb = small("brb", [P, NE])
        mx = small("mx", [P, 10])
        nmx = small("nmx", [P, 10])
        ssum = small("ssum", [P, 10])
        rsum = small("rsum", [P, 10])
        stats = small("stats", [P, 3, 2, 6])
        mv = small("mv", [P, 3, 2])
        rstd = small("rstd", [P, 3])
        lg = small("lg", [P, 3, NE])
        top8 = small("top8", [P, 3, 8])
        gt = at("gt", [P, 3, NE], rH + 8192)
        eq = at("eq", [P, 3, NE], rH + 8576)
        ceq = at("ceq", [P, 3, NE], rH + 8960)
        mask = small("mask", [P, 3, NE])
        nsel = small("nsel", [P, 3])
        ge = at("ge", [P, 3, NE], rH + 9344)
        gsum = small("gsum", [P, 3])
        gates = small("gates", [P, 3, NE + 1])
        gatesT = small("gatesT", [NE, T])
        slotv = small("slotv", [P, 3, NE + 1])
        cmax = small("cmax", [1, 2])
        late = small("late", [1, PASSES - 1])
        npass = small("npass", [1, 1], I32)
        ps = ctx.enter_context(nc.psum_tensor("ps", [P, 8, 512], F32))

        slot_full = [sem(f"slot_full{i}") for i in range(RING)]
        slot_free = sem("slot_free")
        bank_full = [sem(f"bank_full{i}") for i in range(8)]
        bank_free = [sem(f"bank_free{i}") for i in range(8)]
        x_in, bias_in, vparam_in, const_in, ws_in, hist_in, ln_in, b1_in, b2_in = (sem(n) for n in (
            "x_in", "bias_in", "vparam_in", "const_in", "ws_in", "hist_in", "ln_in", "b1_in", "b2_in"))
        cv_out, mkv_out, pout_out, out_done = (sem(n) for n in ("cv_out", "mkv_out", "pout_out", "out_done"))
        consts, ops_pool, ops_dve = sem("consts"), sem("ops_pool"), sem("ops_dve")
        v_gelu, v_norm, wsT_ready, a_ready = (sem(n) for n in (
            "v_gelu", "v_norm", "wsT_ready", "a_ready"))
        var_ready, std_ready = sem("var_ready"), sem("std_ready")
        sm_max, sm_done, qmask_ready, d_ready, h_added = (sem(n) for n in (
            "sm_max", "sm_done", "qmask_ready", "d_ready", "h_added"))
        x1_ready, lg_ready, ge_ready, mask_ready, gates_ready, b1_ready, npass_ready = (sem(n) for n in (
            "x1_ready", "lg_ready", "ge_ready", "mask_ready", "gates_ready", "b1_ready", "npass_ready"))
        slots_moved, pick_ready, pickg_ready, pickT_turned, pickT_ready = (sem(n) for n in (
            "slots_moved", "pick_ready", "pickg_ready", "pickT_turned", "pickT_ready"))
        xg_done, xg_ready, up_done, gm_ready, lin_ready = (sem(n) for n in (
            "xg_done", "xg_ready", "up_done", "gm_ready", "lin_ready"))
        sg_ready, gs_ready, act_ready, act_turned, actT_ready = (sem(n) for n in (
            "sg_ready", "gs_ready", "act_ready", "act_turned", "actT_ready"))
        y_done, y_ready, part_done, part_added, y_out_ready = (sem(n) for n in (
            "y_done", "y_ready", "part_done", "part_added", "y_out_ready"))

        def bank(*key):
            return ps[:, TILES[key] % 8, :]

        def full(*key):
            return bank_full[TILES[key] % 8], TILES[key] // 8 + 1

        def fills(*key):
            return bank_full[TILES[key] % 8], 1

        def frees(*key):
            return bank_free[TILES[key] % 8], 1

        def copied(*key):
            return bank_free[TILES[key] % 8], TILES[key] // 8 + 1

        def slot(*key):
            return ring[:, SLOTS[key] % RING, :]

        def loaded(*key):
            return slot_full[SLOTS[key] % RING], 16 * (SLOTS[key] // RING + 1)

        def last_use(kind, i):
            if kind in ("v", "wo"):
                return kind, i, 1
            if kind in ("mk", "mv"):
                return kind, i
            return {"mem": ("mem", 3), "kc": ("kt", 1, 2 * i + 1), "vc": ("so", 0), "wb": ("wb", 4 * i + 3),
                    "wm": ("wm", 4 * i + 3)}.get(kind, (kind, 2 * i + 1))

        def wcols(w, c0, k=KD, n=256):
            return w[:, c0:c0 + n].rearrange("(k p) n -> p k n", k=k)

        def rows(v):
            return v.unsqueeze(0).broadcast_to([P, v.shape[0]])

        OFF = {"u": 0, "v": D, "p": 2 * D, "q": 2 * D + 512, "gA": 3 * D, "gB": 4 * D, "gM": 5 * D}
        BIAS = {k: v // P for k, v in OFF.items()}
        LS_COL = 48

        def source(kind, i):
            if kind in OFF:
                return wcols(a["w_in"], OFF[kind] + 256 * i)
            if kind == "mem":
                return a["mem_prompt"].rearrange("(m p) d -> p m d", m=2)
            if kind in ("kc", "vc"):
                c = a["cache_mem_k" if kind == "kc" else "cache_mem_v"]
                return c[2 * i:2 * i + 2].rearrange("b (m p) h d -> p (b m) (h d)", m=2)
            if kind in ("wb", "wm"):
                return wcols(a["w_b_out" if kind == "wb" else "w_m_out"], 512 * i, 4, 512)
            w = {"mk": "w_mk", "mv": "w_mv", "wa": "w_a_out", "wo": "w_o"}[kind]
            return wcols(a[w], 256 * i)

        block = ctx.enter_context(nc.Block())

        def gate_used(n):
            return copied("wa", n) if n < KD else (h_added, n - KD + 1)

        GB, LB, XG, AT, YB, ST, O0 = 0, 1, 2, 3, 4, 5, 6

        @block.sync
        def _(sp):
            slots = list(SLOTS)
            for n, key in enumerate(slots):
                if n >= RING:
                    sp.wait_ge(*full(*last_use(*slots[n - RING])))
                src = source(*key)
                sp.dma_start(slot(*key).rearrange("p (k n) -> p k n", k=src.shape[1]), src)\
                    .then_inc(slot_full[n % RING], 16)

            def load(e, j):
                n = (NH + j) % RING
                if j < KD:
                    src = a["w1"][e, j * P:(j + 1) * P, :].rearrange("e p n -> p (e n)")
                    dst = ring[:, n, :]
                else:
                    r0 = 2 * (j - KD) * P
                    src = a["w2"][e, r0:r0 + 2 * P, :].rearrange("e (k p) n -> p (e k) n", k=2)
                    dst = ring[:, n, :].rearrange("p (k n) -> p k n", k=2)
                sp.dma_start(dst, src).then_inc(slot_full[n], 16)

            def expert(q, e):
                before = q * NE + e - 1
                for j in range(RING):
                    if j == KD - 1:
                        sp.wait_ge(up_done, before + 1)
                    elif j == RING - 1:
                        sp.wait_ge(y_done, before + 1)
                    else:
                        sp.wait_ge(slot_free, before * (RING - 2) + (j if j < KD else j - 1) + 1)
                    load(bass.ds(e, 1), j)

            for j in range(RING):
                sp.wait_ge(*full(*last_use(*slots[NH - RING + j])))
                load(slice(0, 1), j)
            with sp.Fori(1, NE) as e:
                expert(0, e)
            sp.wait_ge(npass_ready, 1)
            passes = sp.value_load(npass[0:1, 0:1], min_val=1, max_val=PASSES)
            with sp.If(passes > 1):
                with sp.Fori(1, passes) as q:
                    with sp.Fori(0, NE) as e:
                        expert(q, e)

        @block.gpsimd
        def _(pool):
            n = [0]

            def link(ins):
                n[0] += 1
                ins.then_inc(ops_pool, 1)
                pool.wait_ge(ops_pool, n[0])

            def select(out, op, fill, base, pattern, mult):
                return pool.affine_select(out=out, in_=out, compare_op=op, fill=fill, base=base,
                                          pattern=pattern, channel_multiplier=mult)

            link(pool.memset(ident[:, :], 0.0))
            select(ident[:, :], ALU.not_equal, 1.0, 0, [[-1, P]], 1).then_inc(consts, 1)
            pool.memset(ones[:, :], 1.0).then_inc(consts, 1)
            link(pool.memset(upper[:, :], 1.0))
            select(upper[:, :], ALU.is_gt, 0.0, 0, [[1, P]], -1).then_inc(consts, 1)
            link(pool.memset(bdmask[:, :, :], 1.0))
            link(select(bdmask[:, :, :], ALU.is_ge, 0.0, 0, [[-LS, NB], [0, LS]], 1))
            select(bdmask[:, :, :], ALU.is_ge, 0.0, LS - 1, [[LS, NB], [0, LS]], -1).then_inc(consts, 1)
            link(pool.memset(rep8[:, :, :], 0.0))
            select(rep8[:, :, :], ALU.not_equal, 1.0, 0, [[0, NB], [-1, LS]], 1).then_inc(consts, 1)
            link(pool.memset(selcol[:, :], 0.0))
            for r in range(3):
                ins = select(selcol[:, 0:NE], ALU.not_equal, 1.0, -NE * r, [[-1, NE]], 1)
                if r < 2:
                    link(ins)
            ins.then_inc(consts, 1)
            pool.iota(slotj_i[:, :], [[1, CAP]], base=0, channel_multiplier=0).then_inc(consts, 1)
            pool.iota(pos_i[:, :], [[1, HIST + 1]], base=1, channel_multiplier=0).then_inc(consts, 1)
            for i in range(PASSES - 1):
                ins = pool.memset(thr[:, i:i + 1], float(CAP * (i + 1)))
            ins.then_inc(consts, 1)
            pool.memset(zeros32[:, :], 0.0).then_inc(consts, 1)

            pool.dma_start(o["pool_s"][:, 0:HIST - LS, :], a["state_pool"][:, LS:HIST, :]).then_inc(out_done, 16)
            pool.wait_ge(*copied("ws", 0))
            pool.wait_ge(*copied("ws", 1))
            select(wsT[:, :, :], ALU.is_ge, 0.0, 0, [[0, GA], [1, P]], -1).then_inc(wsT_ready, 1)
            pool.wait_ge(v_norm, 1)
            pool.dma_start(o["cv"], vn[0:NB * LS, 2, :]).then_inc(cv_out, 16)
            pool.wait_ge(a_ready, GA)
            pool.dma_start(histr[:, :], a["state_pool"].rearrange("b t c -> (b t) c")).then_inc(hist_in, 16)
            for m in range(2):
                pool.wait_ge(*copied("mv", m))
            pool.dma_start(o["mv"].rearrange("(m p) c -> p m c", m=2), mvp[:, :, :]).then_inc(mkv_out, 16)
            for m in range(2):
                pool.wait_ge(*copied("mkp", m))
            pool.dma_start(o["mk"].rearrange("(m p) c -> p m c", m=2), mkp[:, :, :]).then_inc(mkv_out, 16)
            pool.wait_ge(*copied("pout", 0))
            pool.dma_start(o["pool_p"], pout[49:64, :]).then_inc(pout_out, 16)
            for b in range(NB):
                pool.dma_start(o["pool_s"][b, HIST - LS:HIST, :], pout[64 + LS * b:64 + LS * (b + 1), :])\
                    .then_inc(pout_out, 16)
            pool.wait_ge(d_ready, PG)
            for i, w in enumerate(("ln1_g", "ln1_b", "ln2_g", "ln2_b")):
                pool.dma_start(lnb[:, i, :], rows(a[w]))\
                    .then_inc(ln_in, 16)
            pool.dma_start(b2s[:, :], a["b2"]).then_inc(b2_in, 16)
            pool.wait_ge(*full("yb", 0))
            for r in range(3):
                pool.dma_start(b1x[r * NE:(r + 1) * NE, :], a["b1"]).then_inc(b1_in, 16)
            pool.wait_ge(b1_in, 48)
            pool.wait_ge(*full("wo", 0, 0))
            for r in range(3):
                part = slice(r * NE, (r + 1) * NE)
                for _ in range(r):
                    link(pool.tensor_copy(b1s[part, :], b1x[part, :]))
                    link(pool.tensor_tensor(b1x[part, :], b1x[part, :], b1s[part, :], ALU.subtract))
                ins = pool.tensor_copy(b1s[part, :], b1x[part, :])
            ins.then_inc(b1_ready, 1)
            pool.wait_ge(y_out_ready, 1)
            pool.dma_start(o["y_s"], x[0:64, 2, :]).then_inc(out_done, 16)
            for tt in range(2):
                pool.wait_ge(y_out_ready, tt + 2)
                pool.dma_start(o["y_p"][P * tt:P * tt + P, :], x[:, tt, :]).then_inc(out_done, 16)
            pool.wait_ge(cv_out, 16)
            pool.wait_ge(mkv_out, 32)
            pool.wait_ge(pout_out, 16 * (1 + NB))
            pool.wait_ge(out_done, 16 * 4)

        @block.scalar
        def _(act):
            act.dma_start(x[:, 0:2, :], a["x_prompt"].rearrange("(m p) d -> p m d", m=2)).then_inc(x_in, 16)
            act.dma_start(x[0:64, 2, :], a["x_sample"]).then_inc(x_in, 16)
            act.dma_start(brow[0:48, :], a["b_in"].rearrange("(c p) -> c p", p=P)).then_inc(bias_in, 16)
            act.dma_start(brow[48:52, :], a["ls_pool"].rearrange("(c p) -> c p", p=P)).then_inc(bias_in, 16)
            for i, src in enumerate((a["b_in"][D:2 * D], a["ln_v_g"], a["ln_v_b"])):
                act.dma_start(bvb[:, i, :], rows(src))\
                    .then_inc(vparam_in, 16)
            act.dma_start(wsr[:, :, :], a["w_s"].rearrange("g t s -> t g s")).then_inc(ws_in, 16)
            act.dma_start(bsb[:, :, :].rearrange("p g t -> p (g t)"),
                          rows(a["b_s"].rearrange("g t -> (g t)"))).then_inc(const_in, 16)
            act.dma_start(wpool[:, :, :], a["w_pool"].rearrange("g c d -> c g d")).then_inc(const_in, 16)
            act.dma_start(wr[:, :, :], a["w_r"].rearrange("(k p) e -> p k e", k=KD)).then_inc(const_in, 16)
            act.dma_start(brb[:, :], rows(a["b_r"])).then_inc(const_in, 16)

            for k in range(1, KD, 2):
                act.wait_ge(*full("xT", k))
                act.copy(xT[:, k, :], bank("xT", k)[:, 0:T]).then_inc(*frees("xT", k))
            def roots(nth):
                act.wait_ge(var_ready, nth)
                act.activation(rstd[:, :], rstd[:, :], ACT.Sqrt).then_inc(std_ready, 1)

            for s in range(4):
                cols = slice(256 * s, 256 * s + 256)
                act.wait_ge(*copied("v", s, 0))
                act.activation(vn[:, 0:2, cols], vn[:, 0:2, cols], ACT.Gelu_apprx_tanh).then_inc(v_gelu, 1)
                act.wait_ge(*copied("v", s, 1))
                act.activation(vn[0:64, 2, cols], vn[0:64, 2, cols], ACT.Gelu_apprx_tanh).then_inc(v_gelu, 1)
            roots(1)
            act.wait_ge(*copied("bias", 0))
            for c in range(KD):
                act.wait_ge(*full("u", c))
                act.activation(uT[:, c, :], bank("u", c)[:, 0:T], ACT.Gelu_apprx_tanh,
                               bias=bT[:, BIAS["u"] + c:BIAS["u"] + c + 1]).then_inc(*frees("u", c))
            act.wait_ge(*full("mem", 1))
            act.copy(memT[:, 2:4, :], bank("mem", 1).rearrange("p (k m) -> p k m", k=2)).then_inc(*frees("mem", 1))
            act.wait_ge(*full("mem", 3))
            act.copy(memT[:, 6:8, :], bank("mem", 3).rearrange("p (k m) -> p k m", k=2)).then_inc(*frees("mem", 3))
            for i in range(2):
                act.wait_ge(*full("mk", i))
                act.copy(mkT[:, 2 * i:2 * i + 2, :], bank("mk", i).rearrange("p (h m) -> p h m", h=2))\
                    .then_inc(*frees("mk", i))
            act.wait_ge(cv_out, 16)
            for i in range(2):
                act.wait_ge(*full("mkp", i))
                act.copy(mkp[:, i, :], bank("mkp", i)).then_inc(*frees("mkp", i))
            for h in range(HEADS):
                act.wait_ge(*full("q", h))
                act.activation(qT[:, h, :], bank("q", h)[:, 0:T], ACT.Identity,
                               bias=bT[:, BIAS["q"] + h:BIAS["q"] + h + 1]).then_inc(*frees("q", h))
            for h in range(HEADS):
                act.wait_ge(sm_max, h + 1)
                for lt in range(2):
                    j = 2 * h + lt
                    ins = act.activation(Pp[:, h, lt, :], bank("sc", h)[:, lt * MEM:(lt + 1) * MEM], ACT.Exp,
                                         bias=nmx[:, j:j + 1], scale=SCALE, accum_out=ssum[:, j:j + 1])
                ins.then_inc(*frees("sc", h))
            for hp in range(2):
                for b in range(1, NB, 2):
                    act.wait_ge(*full("kt", hp, b))
                    act.copy(kTs[:, b, :, :], bank("kt", hp, b).rearrange("p (h m) -> p h m", h=2))\
                        .then_inc(*frees("kt", hp, b))
                act.wait_ge(sm_max, HEADS + hp + 1)
                act.activation(Ps[:, hp, :], bank("ss", hp)[:, 0:MEM], ACT.Exp, bias=nmx[:, 8 + hp:9 + hp],
                               scale=SCALE, accum_out=ssum[:, 8 + hp:9 + hp]).then_inc(*frees("ss", hp))
            for kind, h in (("pt", 0), ("pt", 1), ("o", 0), ("pt", 2), ("o", 1), ("pt", 3), ("o", 2), ("o", 3)):
                act.wait_ge(*full(kind, h))
                if kind == "pt":
                    act.copy(PT[:, h % 2, :, :], bank("pt", h).rearrange("p (m l) -> p m l", m=2))\
                        .then_inc(*frees("pt", h))
                else:
                    act.copy(oT[:, h, 0:SEQ], bank("o", h)[:, 0:SEQ]).then_inc(*frees("o", h))
            act.wait_ge(mkv_out, 32)
            for g in range(PG):
                act.wait_ge(*full("p", g))
                act.activation(pcur[:, g, :], bank("p", g)[:, 0:T], ACT.Identity,
                               bias=bT[:, BIAS["p"] + g:BIAS["p"] + g + 1]).then_inc(*frees("p", g))

            def gate(kind, c, n):
                act.wait_ge(*full(kind, c))
                if n >= 4:
                    act.wait_ge(*gate_used(n - 4))
                act.activation(gbuf[:, n % 4, :], bank(kind, c)[:, 0:T], ACT.Sigmoid,
                               bias=bT[:, BIAS[kind] + c:BIAS[kind] + c + 1]).then_inc(*frees(kind, c))

            for c in range(KD):
                gate("gA", c, c)
            for g in range(PG):
                act.wait_ge(*full("yb", g))
                act.activation(ybT[:, g, :], bank("yb", g)[:, 0:T], ACT.Copy,
                               scale=bT[:, LS_COL + g:LS_COL + g + 1]).then_inc(*frees("yb", g))
            for c in range(KD):
                gate("gB", c, KD + c)
            for c in range(KD):
                gate("gM", c, 2 * KD + c)
            roots(2)
            for k in range(1, KD, 2):
                act.wait_ge(*full("x1T", k))
                act.copy(x1T[:, k, :], bank("x1T", k)[:, 0:T]).then_inc(*frees("x1T", k))
            act.wait_ge(lg_ready, 1)
            act.activation(ge[:, :, :], ge[:, :, :], ACT.Exp).then_inc(ge_ready, 1)
            for i in range(6):
                tt, dh = i // 2, i % 2
                act.wait_ge(*full("b2", i))
                act.copy(yacc[0:ROWS[tt], tt, 512 * dh:512 * dh + 512], bank("b2", i)[0:ROWS[tt], :])\
                    .then_inc(*frees("b2", i))

            def gathered(g):
                act.wait_ge(xg_done, g + 1)
                act.copy(xg[:, :, :], ps[:, XG, :].rearrange("p (k c) -> p k c", k=KD)).then_inc(xg_ready, 1)

            def pair(q, i):
                for par in range(2):
                    e = (q * NE + 2 * i) + par
                    act.wait_ge(gm_ready, e + 1)
                    act.activation(sg[:, :], gm[:, :], ACT.Sigmoid, scale=SW_ALPHA).then_inc(sg_ready, 1)
                    gathered(q * (NE + 1) + 2 * i + par + 1)
                    act.wait_ge(act_turned, e + 1)
                    act.copy(actT[:, :, :, :], ps[:, AT, :].rearrange("p (c h s) -> p c h s", c=4, h=2))\
                        .then_inc(actT_ready, 1)
                    act.wait_ge(y_done, e + 1)
                    act.copy(ypair[CAP * par:CAP * par + CAP, 0:512], ps[0:CAP, YB, :])
                    act.copy(ypair[CAP * par:CAP * par + CAP, 512:D], ps[CAP:2 * CAP, YB, :]).then_inc(y_ready, 1)

            gathered(0)
            with act.Fori(0, NE // 2) as i:
                pair(0, i)
            act.wait_ge(npass_ready, 1)
            passes = act.value_load(npass[0:1, 0:1], min_val=1, max_val=PASSES)
            with act.If(passes > 1):
                with act.Fori(1, passes) as q:
                    gathered(q * (NE + 1))
                    with act.Fori(0, NE // 2) as i:
                        pair(q, i)
            roots(3)

        GB, LB, XG, AT, YB, ST, O0 = 0, 1, 2, 3, 4, 5, 6

        @block.vector
        def _(dve):
            n = [0]

            def link(ins):
                n[0] += 1
                ins.then_inc(ops_dve, 1)
                dve.wait_ge(ops_dve, n[0])

            def layer_norm(buf, g, b, nth, ready):
                for tt in range(3):
                    r = slice(0, ROWS[tt])
                    for c in range(2):
                        ins = dve.bn_stats(stats[r, tt, c, :], buf[r, tt, 512 * c:512 * c + 512])
                link(ins)
                for tt in range(3):
                    r = slice(0, ROWS[tt])
                    ins = dve.bn_aggr(mv[r, tt, :], stats[r, tt, :, :].rearrange("p c s -> p (c s)"))
                link(ins)
                dve.tensor_scalar(rstd[:, :], mv[:, :, 1], EPS, None, ALU.add).then_inc(var_ready, 1)
                dve.wait_ge(std_ready, nth)
                link(dve.reciprocal(rstd[:, :], rstd[:, :]))
                for tt in (2, 0, 1):
                    r = slice(0, ROWS[tt])
                    link(dve.tensor_scalar(buf[r, tt, :], buf[r, tt, :], mv[r, tt, 0:1], rstd[r, tt:tt + 1],
                                           ALU.subtract, ALU.mult))
                    link(dve.tensor_tensor(buf[r, tt, :], buf[r, tt, :], g[r, :], ALU.mult))
                    dve.tensor_tensor(buf[r, tt, :], buf[r, tt, :], b[r, :], ALU.add).then_inc(ready, 1)

            dve.wait_ge(consts, 10)
            dve.tensor_copy(slotj[:, :], slotj_i[:, :])
            link(dve.tensor_copy(pos_f[:, :], pos_i[:, :]))
            for g, w in enumerate(WINDOWS):
                ins = dve.tensor_scalar(ratio[:, g, :], pos_f[:, :], float(w), None, ALU.min)
            link(ins)
            link(dve.reciprocal(ratio[:, :, :], ratio[:, :, :]))
            for g, w in enumerate(WINDOWS):
                dve.tensor_scalar(ratio[:, g, :], ratio[:, g, :], float(w), None, ALU.mult)
            dve.memset(slotv[:, :, :], -1.0)
            dve.memset(gates[:, :, :], 0.0)
            dve.memset(mv[:, :, :], 1.0)
            link(dve.memset(lg[:, :, :], 0.0))

            dve.wait_ge(*full("bias", 0))
            dve.tensor_copy(bT[:, :], bank("bias", 0)[:, 0:52]).then_inc(*frees("bias", 0))
            for k in range(0, KD, 2):
                dve.wait_ge(*full("xT", k))
                dve.tensor_copy(xT[:, k, :], bank("xT", k)[:, 0:T]).then_inc(*frees("xT", k))

            dve.wait_ge(vparam_in, 48)
            for s in range(4):
                cols = slice(256 * s, 256 * s + 256)
                dve.wait_ge(*full("v", s, 0))
                dve.tensor_tensor(vn[:, 0:2, cols], bank("v", s, 0).rearrange("p (t n) -> p t n", t=2),
                                  bvb[:, 0:1, cols].broadcast_to([P, 2, 256]), ALU.add)\
                   .then_inc(*frees("v", s, 0))
                dve.wait_ge(*full("v", s, 1))
                dve.tensor_tensor(vn[0:64, 2, cols], bank("v", s, 1)[0:64, 0:256], bvb[0:64, 0, cols], ALU.add)\
                   .then_inc(*frees("v", s, 1))
            dve.wait_ge(v_gelu, 8)
            layer_norm(vn, bvb[:, 1, :], bvb[:, 2, :], 1, v_norm)

            for i in range(2):
                dve.wait_ge(*full("ws", i))
                dve.tensor_copy(wsT[:, 4 * i:4 * i + 4, :], bank("ws", i).rearrange("p (g t) -> p g t", g=4))\
                   .then_inc(*frees("ws", i))
            dve.wait_ge(*full("bd", 0))
            dve.tensor_tensor(bd[:, :, :], bank("bd", 0)[0:64, :].rearrange("p (g t) -> p g t", g=GA),
                              bdmask[:, :, :].rearrange("p b t -> p (b t)").unsqueeze(1)
                              .broadcast_to([NB * LS, GA, NB * LS]), ALU.mult).then_inc(*frees("bd", 0))
            dve.wait_ge(const_in, 64)
            for g in range(GA):
                m, tmp = bank("mix", g), mtmp[:, g % 2, :]
                dve.wait_ge(*full("mix", g))
                if g >= 2:
                    dve.wait_ge(a_ready, g - 1)
                dve.tensor_tensor(tmp[:, 0:SEQ].rearrange("p (c t) -> p c t", c=2),
                                  m[:, 0:SEQ].rearrange("p (c t) -> p c t", c=2),
                                  bsb[:, g:g + 1, :].broadcast_to([P, 2, P]), ALU.add)
                dve.tensor_tensor(tmp[:, SEQ:T].rearrange("p (b t) -> p b t", b=NB),
                                  m[:, SEQ:T].rearrange("p (b t) -> p b t", b=NB),
                                  bsb[:, g:g + 1, 0:LS].broadcast_to([P, NB, LS]), ALU.add)\
                   .then_inc(*frees("mix", g))
                dve.wait_ge(*copied("mix", g))
                dve.wait_ge(*copied("u", g))
                dve.tensor_tensor(uT[:, g, :], uT[:, g, :], tmp, ALU.mult).then_inc(a_ready, 1)

            for i in (0, 2):
                dve.wait_ge(*full("mem", i))
                dve.tensor_copy(memT[:, 2 * i:2 * i + 2, :], bank("mem", i).rearrange("p (k m) -> p k m", k=2))\
                   .then_inc(*frees("mem", i))
            for i in range(2):
                dve.wait_ge(*full("mv", i))
                dve.tensor_copy(mvp[:, :, 256 * i:256 * i + 256], bank("mv", i).rearrange("p (m n) -> p m n", m=2))\
                   .then_inc(*frees("mv", i))
            link(dve.memset(qmask[:, :, :], 0.0))

            def row_max(j, w, scores):
                link(dve.tensor_reduce(mx[:, j:j + w], scores, AX.X, ALU.max))
                dve.tensor_scalar(nmx[:, j:j + w], mx[:, j:j + w], -SCALE, None, ALU.mult).then_inc(sm_max, 1)

            def own_queries(hp):
                for hh in range(2):
                    dve.wait_ge(*copied("q", 2 * hp + hh))
                    ins = dve.tensor_copy(
                        qmask[:, hh, :].rearrange("p (b s) -> p b s", s=QSTEP)[:, :, 0:LS],
                        qT[:, 2 * hp + hh, SEQ:T].rearrange("p (b l) -> p b l", b=NB))
                ins.then_inc(qmask_ready, 1)

            def turned_keys(hp):
                for b in range(0, NB, 2):
                    dve.wait_ge(*full("kt", hp, b))
                    dve.tensor_copy(kTs[:, b, :, :], bank("kt", hp, b).rearrange("p (h m) -> p h m", h=2))\
                       .then_inc(*frees("kt", hp, b))
                dve.wait_ge(*full("ss", hp))
                row_max(8 + hp, 1, bank("ss", hp)[:, 0:MEM])

            for h in range(HEADS):
                dve.wait_ge(*full("sc", h))
                row_max(2 * h, 2, bank("sc", h).rearrange("p (t m) -> p t m", t=2))
            own_queries(0)
            turned_keys(0)
            own_queries(1)
            for h in range(HEADS):
                dve.wait_ge(*copied("sc", h))
                link(dve.reciprocal(rsum[:, 2 * h:2 * h + 2], ssum[:, 2 * h:2 * h + 2]))
                for lt in range(2):
                    ins = dve.tensor_scalar(Pp[:, h, lt, :], Pp[:, h, lt, :], rsum[:, 2 * h + lt:2 * h + lt + 1],
                                            None, ALU.mult)
                ins.then_inc(sm_done, 1)
            turned_keys(1)
            for hp in range(2):
                dve.wait_ge(*copied("ss", hp))
                link(dve.reciprocal(rsum[:, 8 + hp:9 + hp], ssum[:, 8 + hp:9 + hp]))
                dve.tensor_scalar(Ps[:, hp, :], Ps[:, hp, :], rsum[:, 8 + hp:9 + hp], None, ALU.mult)\
                   .then_inc(sm_done, 1)
            for hp in range(2):
                dve.wait_ge(*full("pst", hp))
                dve.tensor_copy(PTs[:, hp, :, :], bank("pst", hp)[:, 0:MEM].rearrange("p (m t) -> p m t", m=2))\
                   .then_inc(*frees("pst", hp))
            dve.wait_ge(*full("so", 0))
            dve.tensor_copy(oT[:, :, SEQ:T], bank("so", 0)[:, 0:SEQ].rearrange("p (h t) -> p h t", h=HEADS))\
               .then_inc(*frees("so", 0))

            e0, e1, e2 = ext

            def own(t, lo, hi):
                return t[:, :, HIST + SEQ:EXT].rearrange("p g (b s) -> p g b s", s=SEG)[:, :, :, lo:hi]

            dve.wait_ge(*full("hist", 0))
            dve.memset(e0[:, :, 0:HIST], 0.0)
            dve.tensor_copy(own(e0, 0, HIST),
                            bank("hist", 0)[:, 0:PG * NB * HIST].rearrange("p (g b t) -> p g b t", g=PG, b=NB))\
               .then_inc(*frees("hist", 0))
            for g in range(PG):
                dve.wait_ge(*copied("p", g))
            dve.tensor_copy(e0[:, :, HIST:HIST + SEQ], pcur[:, :, 0:SEQ])
            link(dve.tensor_copy(own(e0, HIST, SEG), pcur[:, :, SEQ:T].rearrange("p g (b l) -> p g b l", b=NB)))
            dve.wait_ge(*full("pout", 0))
            dve.tensor_copy(pout[:, :], bank("pout", 0)).then_inc(*frees("pout", 0))
            sums = e0
            for step, out in enumerate((e1, e2, e1, e2)):
                w = 1 << step
                link(dve.tensor_tensor(out[:, step:PG, 2 * w - 1:EXT], sums[:, step:PG, 2 * w - 1:EXT],
                                       sums[:, step:PG, w - 1:EXT - w], ALU.add))
                sums = out
            for g in range(PG):
                s = (e1, e2)[g % 2][:, g, HIST:2 * HIST + 1]
                ins = dve.tensor_tensor(s, s, ratio[:, g, :], ALU.mult)
            link(ins)
            dve.wait_ge(mkv_out, 32)
            for g, w in enumerate(WINDOWS):
                s = (e1, e2)[g % 2]
                dve.scalar_tensor_tensor(out=dT[:, g, 0:SEQ], in0=s[:, g, HIST:HIST + SEQ], scalar=1.0 / w,
                                         in1=e0[:, g, HIST:HIST + SEQ], op0=ALU.mult, op1=ALU.subtract)
                dve.scalar_tensor_tensor(out=dT[:, g, SEQ:T].rearrange("p (b l) -> p b l", b=NB),
                                         in0=own(s, HIST, SEG)[:, g], scalar=1.0 / w,
                                         in1=own(e0, HIST, SEG)[:, g], op0=ALU.mult, op1=ALU.subtract)\
                   .then_inc(d_ready, 1)

            for c in range(KD):
                dve.wait_ge(*full("wa", c))
                dve.wait_ge(*copied("gA", c))
                dve.tensor_tensor(hT[:, c, :], bank("wa", c)[:, 0:T], gbuf[:, c % 4, :], ALU.mult)\
                   .then_inc(*frees("wa", c))
            for g, w in (("gB", "wb"), ("gM", "wm")):
                for c in range(KD):
                    dve.wait_ge(*full(w, c))
                    dve.wait_ge(*copied(g, c))
                    dve.tensor_tensor(gbuf[:, c % 4, :], bank(w, c)[:, 0:T], gbuf[:, c % 4, :], ALU.mult)\
                       .then_inc(*frees(w, c))
                    dve.wait_ge(*copied(w, c))
                    dve.tensor_tensor(hT[:, c, :], hT[:, c, :], gbuf[:, c % 4, :], ALU.add).then_inc(h_added, 1)

            for s in range(4):
                cols = slice(256 * s, 256 * s + 256)
                dve.wait_ge(*full("wo", s, 0))
                dve.scalar_tensor_tensor(out=x[:, 0:2, cols], in0=x[:, 0:2, cols], scalar=ALPHA,
                                         in1=bank("wo", s, 0).rearrange("p (t n) -> p t n", t=2),
                                         op0=ALU.mult, op1=ALU.add).then_inc(*frees("wo", s, 0))
                dve.wait_ge(*full("wo", s, 1))
                dve.scalar_tensor_tensor(out=x[0:64, 2, cols], in0=x[0:64, 2, cols], scalar=ALPHA,
                                         in1=bank("wo", s, 1)[0:64, 0:256],
                                         op0=ALU.mult, op1=ALU.add).then_inc(*frees("wo", s, 1))
            dve.wait_ge(ln_in, 64)
            dve.wait_ge(*copied("wo", 3, 0))
            dve.wait_ge(*copied("wo", 3, 1))
            layer_norm(x, lnb[:, 0, :], lnb[:, 1, :], 2, x1_ready)
            for k in range(0, KD, 2):
                dve.wait_ge(*full("x1T", k))
                dve.tensor_copy(x1T[:, k, :], bank("x1T", k)[:, 0:T]).then_inc(*frees("x1T", k))

            rt = bank("rt", 0)[:, 0:3 * NE].rearrange("p (t e) -> p t e", t=3)
            dve.wait_ge(*full("rt", 0))
            dve.tensor_tensor(lg[:, 0:2, :], rt[:, 0:2, :], brb[:, :].unsqueeze(1).broadcast_to([P, 2, NE]), ALU.add)
            dve.tensor_tensor(lg[0:64, 2, :], rt[0:64, 2, :], brb[0:64, :], ALU.add).then_inc(*frees("rt", 0))
            dve.wait_ge(*copied("rt", 0))
            for tt in range(3):
                ins = dve.max(out=top8[:, tt, :], in_=lg[:, tt, :])
            link(ins)
            fourth = top8[:, :, TOPK - 1:TOPK].broadcast_to([P, 3, NE])
            dve.tensor_tensor(ge[:, :, :], lg[:, :, :], top8[:, :, 0:1].broadcast_to([P, 3, NE]), ALU.subtract)\
               .then_inc(lg_ready, 1)
            dve.tensor_tensor(eq[:, :, :], lg[:, :, :], fourth, ALU.is_equal)
            link(dve.tensor_tensor(gt[:, :, :], lg[:, :, :], fourth, ALU.is_gt))
            link(dve.tensor_reduce(nsel[:, :], gt[:, :, :], AX.X, ALU.add))
            dve.tensor_scalar(nsel[:, :], nsel[:, :], -1.0, float(TOPK), ALU.mult, ALU.add)
            for tt in range(3):
                ins = dve.tensor_tensor_scan(ceq[:, tt, :], eq[:, tt, :], zeros32[:, :], 0.0, ALU.add, ALU.add)
            link(ins)
            link(dve.tensor_tensor(ceq[:, :, :], ceq[:, :, :], nsel[:, :].unsqueeze(2).broadcast_to([P, 3, NE]),
                                   ALU.is_le))
            link(dve.tensor_tensor(eq[:, :, :], eq[:, :, :], ceq[:, :, :], ALU.mult))
            dve.tensor_tensor(mask[:, :, :], gt[:, :, :], eq[:, :, :], ALU.add).then_inc(mask_ready, 1)
            dve.wait_ge(mask_ready, 1)
            dve.wait_ge(ge_ready, 1)
            link(dve.tensor_tensor(ge[:, :, :], ge[:, :, :], mask[:, :, :], ALU.mult))
            link(dve.tensor_reduce(gsum[:, :], ge[:, :, :], AX.X, ALU.add))
            link(dve.reciprocal(gsum[:, :], gsum[:, :]))
            dve.tensor_tensor(gates[:, :, 0:NE], ge[:, :, :], gsum[:, :].unsqueeze(2).broadcast_to([P, 3, NE]),
                              ALU.mult).then_inc(gates_ready, 1)
            rk = bank("rank", 0)[:, 0:4 * NE].rearrange("p (t e) -> p t e", t=4)
            dve.wait_ge(*full("rank", 0))
            dve.tensor_reduce(cmax[:, 0:1], rk[0:1, 3, :], AX.X, ALU.max)
            dve.scalar_tensor_tensor(out=slotv[:, 0:2, 0:NE], in0=rk[:, 0:2, :], scalar=1.0, in1=mask[:, 0:2, :],
                                     op0=ALU.add, op1=ALU.mult)
            dve.scalar_tensor_tensor(out=slotv[0:64, 2, 0:NE], in0=rk[0:64, 2, :], scalar=1.0,
                                     in1=mask[0:64, 2, :], op0=ALU.add, op1=ALU.mult).then_inc(*frees("rank", 0))
            dve.wait_ge(*copied("rank", 0))
            dve.tensor_scalar(slotv[:, 0:2, 0:NE], slotv[:, 0:2, 0:NE], -1.0, None, ALU.add)
            dve.tensor_scalar(slotv[0:64, 2, 0:NE], slotv[0:64, 2, 0:NE], -1.0, None, ALU.add)
            link(dve.tensor_scalar(late[:, :], thr[:, :], cmax[:, 0:1], None, ALU.is_lt))
            link(dve.tensor_reduce(cmax[:, 1:2], late[:, :], AX.X, ALU.add))
            dve.tensor_scalar(npass[:, :], cmax[:, 1:2], 1.0, None, ALU.add).then_inc(npass_ready, 1)
            dve.wait_ge(*full("gT", 0))
            dve.tensor_copy(gatesT[:, :], bank("gT", 0)[0:NE, 0:T]).then_inc(*frees("gT", 0))

            def picks(g, e, buf):
                for tt in range(3):
                    r = slice(0, ROWS[tt])
                    dve.tensor_scalar(pick[r, buf, tt, :], slotj[r, :], slotv[r, tt, bass.ds(e, 1)], None,
                                      ALU.is_equal)
                dve.tensor_copy(sel[:, buf, :], selcol[:, bass.ds(e, 1)].broadcast_to([3 * NE, CAP]))\
                   .then_inc(pick_ready, 1)

            def pair(q, i):
                n = q * (NE // 2) + i
                for par in range(2):
                    for tt in range(3):
                        r = slice(0, ROWS[tt])
                        ins = dve.tensor_scalar(pickg[r, tt, par, :], slotj[r, :],
                                                slotv[r, tt, bass.ds(2 * i + par, 1)],
                                                gates[r, tt, bass.ds(2 * i + par, 1)], ALU.is_equal, ALU.mult)
                ins.then_inc(pickg_ready, 1)
                for par in range(2):
                    e = 2 * n + par
                    picks(q * (NE + 1) + 2 * i + par + 1, 2 * i + par + 1, 1 - par)
                    dve.wait_ge(up_done, e + 1)
                    dve.tensor_scalar(gm[:, :], ps[:, GB, :], SW_LIMIT, None, ALU.min).then_inc(gm_ready, 1)
                    dve.tensor_scalar(lin[:, :], ps[:, LB, :], -SW_LIMIT, SW_LIMIT, ALU.max, ALU.min)\
                       .then_inc(lin_ready, 1)
                    dve.wait_ge(sg_ready, e + 1)
                    dve.tensor_tensor(gs[:, :], gm[:, :], sg[:, :], ALU.mult).then_inc(gs_ready, 1)
                    dve.wait_ge(gs_ready, e + 1)
                    dve.wait_ge(lin_ready, e + 1)
                    dve.scalar_tensor_tensor(out=act_s[:, :], in0=lin[:, :], scalar=1.0, in1=gs[:, :],
                                             op0=ALU.add, op1=ALU.mult).then_inc(act_ready, 1)
                dve.wait_ge(pickT_turned, n + 1)
                dve.tensor_copy(pickT[:, :], ps[:, ST, 0:T]).then_inc(pickT_ready, 1)
                for t in range(6):
                    tt, dh = t // 2, t % 2
                    y = yacc[0:ROWS[tt], tt, 512 * dh:512 * dh + 512]
                    dve.wait_ge(part_done, 6 * n + t + 1)
                    dve.tensor_tensor(y, ps[0:ROWS[tt], O0 + t % 2, :], y, ALU.add).then_inc(part_added, 1)

            dve.wait_ge(pout_out, 16 * (1 + NB))
            for i in range(6):
                dve.wait_ge(*copied("b2", i))
            dve.wait_ge(npass_ready, 1)
            picks(0, 0, 0)
            with dve.Fori(0, NE // 2) as i:
                pair(0, i)
            passes = dve.value_load(npass[0:1, 0:1], min_val=1, max_val=PASSES)
            with dve.If(passes > 1):
                with dve.Fori(1, passes) as q:
                    dve.wait_ge(xg_done, q * (NE + 1))
                    dve.tensor_scalar(slotv[:, 0:2, 0:NE], slotv[:, 0:2, 0:NE], -float(CAP), None, ALU.add)
                    dve.tensor_scalar(slotv[0:64, 2, 0:NE], slotv[0:64, 2, 0:NE], -float(CAP), None, ALU.add)\
                       .then_inc(slots_moved, 1)
                    dve.wait_ge(slots_moved, q)
                    picks(q * (NE + 1), 0, 0)
                    with dve.Fori(0, NE // 2) as i:
                        pair(q, i)

            dve.wait_ge(part_added, passes * (6 * (NE // 2)))
            for tt in range(3):
                r = slice(0, ROWS[tt])
                ins = dve.scalar_tensor_tensor(out=x[r, tt, :], in0=x[r, tt, :], scalar=ALPHA, in1=yacc[r, tt, :],
                                               op0=ALU.mult, op1=ALU.add)
            link(ins)
            layer_norm(x, lnb[:, 2, :], lnb[:, 3, :], 3, y_out_ready)

        @block.tensor
        def _(pe):
            def opens(*key):
                if TILES[key] >= 8:
                    pe.wait_ge(bank_free[TILES[key] % 8], TILES[key] // 8)
                return bank(*key)

            def contract(out, pairs):
                last = len(pairs) - 1
                for k, (lhsT, rhs) in enumerate(pairs):
                    ins = pe.matmul(out, lhsT, rhs, start=(k == 0), stop=(k == last))
                return ins

            def to_channels(kind, c, w, cc, rhs, nk=KD):
                out = opens(kind, c)
                return contract(out[:, 0:T], [(w[:, k, P * cc:P * cc + P], rhs[:, k, :]) for k in range(nk)])

            def to_tokens(kind, s, srcT):
                w = slot(kind, s).rearrange("p (k n) -> p k n", k=KD)
                pe.wait_ge(*loaded(kind, s))
                out = opens(kind, s, 0)
                for j in range(2):
                    ins = contract(out[:, 256 * j:256 * j + 256],
                                   [(srcT[:, k, P * j:P * j + P], w[:, k, :]) for k in range(KD)])
                ins.then_inc(*fills(kind, s, 0))
                out = opens(kind, s, 1)
                contract(out[0:64, 0:256], [(srcT[:, k, SEQ:T], w[:, k, :]) for k in range(KD)])\
                    .then_inc(*fills(kind, s, 1))

            pe.wait_ge(consts, 10)
            pe.wait_ge(bias_in, 32)
            pe.transpose(opens("bias", 0)[:, 0:52], brow[:, :], ident[0:52, 0:52]).then_inc(*fills("bias", 0))
            pe.wait_ge(x_in, 32)
            for k in range(KD):
                out = opens("xT", k)
                for tt in range(3):
                    ins = pe.transpose(out[:, P * tt:P * tt + ROWS[tt]], x[0:ROWS[tt], tt, P * k:P * k + P],
                                       ident[0:ROWS[tt], 0:ROWS[tt]])
                ins.then_inc(*fills("xT", k))
            for k in range(KD):
                pe.wait_ge(*copied("xT", k))
            for s in range(4):
                to_tokens("v", s, xT)
            for c in range(KD):
                pe.wait_ge(*loaded("u", c // 2))
                to_channels("u", c, slot("u", c // 2).rearrange("p (k n) -> p k n", k=KD), c % 2, xT)\
                    .then_inc(*fills("u", c))

            pe.wait_ge(ws_in, 16)
            for i in range(2):
                out = opens("ws", i)
                for g in range(4):
                    ins = pe.transpose(out[:, P * g:P * g + P], wsr[:, 4 * i + g, :], ident[:, :])
                ins.then_inc(*fills("ws", i))
            pe.wait_ge(wsT_ready, 1)
            pe.matmul(opens("bd", 0)[0:64, :], rep8[:, :, :].rearrange("s b t -> s (b t)"),
                      wsT[0:LS, :, 0:LS].unsqueeze(2).broadcast_to([LS, GA, NB, LS]), start=True, stop=True)\
              .then_inc(*fills("bd", 0))
            pe.wait_ge(v_norm, 3)
            pe.wait_ge(*copied("bd", 0))
            for g in range(GA):
                out = opens("mix", g)
                for j in range(2):
                    pe.matmul(out[:, P * j:P * j + P], vn[:, j, P * g:P * g + P], wsT[:, g, :], start=True, stop=True)
                pe.matmul(out[:, SEQ:T], vn[0:64, 2, P * g:P * g + P], bd[:, g, :], start=True, stop=True)\
                  .then_inc(*fills("mix", g))

            pe.wait_ge(*loaded("mem", 0))
            memr = slot("mem", 0).rearrange("p (m d) -> p m d", m=2)
            for i in range(4):
                out = opens("mem", i)
                for k in (2 * i, 2 * i + 1):
                    for m in range(2):
                        c = MEM * (k % 2) + P * m
                        ins = pe.transpose(out[:, c:c + P], memr[:, m, P * k:P * k + P], ident[:, :])
                ins.then_inc(*fills("mem", i))
            for i in range(4):
                pe.wait_ge(*copied("mem", i))
            for i in range(2):
                w = slot("mk", i).rearrange("p (k n) -> p k n", k=KD)
                pe.wait_ge(*loaded("mk", i))
                out = opens("mk", i)
                for hh in range(2):
                    ins = contract(out[:, MEM * hh:MEM * hh + MEM],
                                   [(w[:, k, P * hh:P * hh + P], memT[:, k, :]) for k in range(KD)])
                ins.then_inc(*fills("mk", i))
            for i in range(2):
                w = slot("mv", i).rearrange("p (k n) -> p k n", k=KD)
                pe.wait_ge(*loaded("mv", i))
                out = opens("mv", i)
                for m in range(2):
                    ins = contract(out[:, 256 * m:256 * m + 256],
                                   [(memT[:, k, P * m:P * m + P], w[:, k, :]) for k in range(KD)])
                ins.then_inc(*fills("mv", i))
            for i in range(2):
                pe.wait_ge(*copied("mk", i))
            for m in range(2):
                out = opens("mkp", m)
                for h in range(HEADS):
                    ins = pe.transpose(out[:, P * h:P * h + P], mkT[:, h, P * m:P * m + P], ident[:, :])
                ins.then_inc(*fills("mkp", m))

            for h in range(HEADS):
                pe.wait_ge(*loaded("q", h // 2))
                to_channels("q", h, slot("q", h // 2).rearrange("p (k n) -> p k n", k=KD), h % 2, xT)\
                    .then_inc(*fills("q", h))
            for h in range(HEADS):
                pe.wait_ge(*copied("q", h))
                out = opens("sc", h)
                for lt in range(2):
                    ins = pe.matmul(out[:, MEM * lt:MEM * lt + MEM], qT[:, h, P * lt:P * lt + P], mkT[:, h, :],
                                    start=True, stop=True)
                ins.then_inc(*fills("sc", h))

            def cache(kind, b):
                return slot(kind, b // 2).rearrange("p (c n) -> p c n", c=4)[:, 2 * (b % 2):2 * (b % 2) + 2, :]

            for hp in range(2):
                for b in range(NB):
                    pe.wait_ge(*loaded("kc", b // 2))
                    out = opens("kt", hp, b)
                    for hh in range(2):
                        for m in range(2):
                            c, h = MEM * hh + P * m, 2 * hp + hh
                            ins = pe.transpose(out[:, c:c + P], cache("kc", b)[:, m, P * h:P * h + P], ident[:, :])
                    ins.then_inc(*fills("kt", hp, b))
                for b in range(NB):
                    pe.wait_ge(*copied("kt", hp, b))
                pe.wait_ge(qmask_ready, hp + 1)
                out = opens("ss", hp)
                for b in range(NB):
                    for hh in range(2):
                        ins = pe.matmul(out[64 * hh:64 * hh + 64, 0:MEM], qmask[:, hh, 64 * b:64 * b + 64],
                                        kTs[:, b, hh, :], start=(b == 0), stop=(b == NB - 1))
                ins.then_inc(*fills("ss", hp))

            for kind, h in (("pt", 0), ("pt", 1), ("o", 0), ("pt", 2), ("o", 1), ("pt", 3), ("o", 2), ("o", 3)):
                out = opens(kind, h)
                if kind == "pt":
                    pe.wait_ge(sm_done, h + 1)
                    for m in range(2):
                        for lt in range(2):
                            c = SEQ * m + P * lt
                            ins = pe.transpose(out[:, c:c + P], Pp[:, h, lt, P * m:P * m + P], ident[:, :])
                    ins.then_inc(*fills("pt", h))
                else:
                    pe.wait_ge(*copied("pt", h))
                    for m in range(2):
                        pe.wait_ge(*copied("mv", m))
                    contract(out[:, 0:SEQ], [(mvp[:, m, P * h:P * h + P], PT[:, h % 2, m, :]) for m in range(2)])\
                        .then_inc(*fills("o", h))
            for hp in range(2):
                pe.wait_ge(sm_done, HEADS + hp + 1)
                out = opens("pst", hp)
                for m in range(2):
                    ins = pe.transpose(out[:, P * m:P * m + P], Ps[:, hp, P * m:P * m + P], ident[:, :])
                ins.then_inc(*fills("pst", hp))
            for hp in range(2):
                pe.wait_ge(*copied("pst", hp))
            out = opens("so", 0)
            for b in range(NB):
                pe.wait_ge(*loaded("vc", b // 2))
                for h in range(HEADS):
                    c = 64 * h + LS * b
                    t = 64 * (h % 2) + LS * b
                    ins = contract(out[:, c:c + LS], [(cache("vc", b)[:, m, P * h:P * h + P],
                                                       PTs[:, h // 2, m, t:t + LS]) for m in range(2)])
            ins.then_inc(*fills("so", 0))

            pe.wait_ge(hist_in, 16)
            out = opens("hist", 0)
            for g in range(PG):
                ins = pe.transpose(out[:, NB * HIST * g:NB * HIST * (g + 1)], histr[:, P * g:P * g + P],
                                   ident[0:NB * HIST, 0:NB * HIST])
            ins.then_inc(*fills("hist", 0))
            for g in range(PG):
                pe.wait_ge(*loaded("p", g // 2))
                to_channels("p", g, slot("p", g // 2).rearrange("p (k n) -> p k n", k=KD), g % 2, xT)\
                    .then_inc(*fills("p", g))
            for g in range(PG):
                pe.wait_ge(*copied("p", g))
            out = opens("pout", 0)
            for g in range(PG):
                ins = pe.transpose(out[:, P * g:P * g + P], pcur[:, g, T - P:T], ident[:, :])
            ins.then_inc(*fills("pout", 0))

            pe.wait_ge(a_ready, GA)
            for i in range(4):
                for kind, rhs in (("gA", xT), ("wa", uT)):
                    pe.wait_ge(*loaded(kind, i))
                    w = slot(kind, i).rearrange("p (k n) -> p k n", k=KD)
                    for c in (2 * i, 2 * i + 1):
                        to_channels(kind, c, w, c % 2, rhs).then_inc(*fills(kind, c))
            pe.wait_ge(const_in, 64)
            for g in range(PG):
                pe.wait_ge(d_ready, g + 1)
                pe.matmul(opens("yb", g)[:, 0:T], wpool[:, g, :], dT[:, g, :], start=True, stop=True)\
                  .then_inc(*fills("yb", g))
            for g in range(PG):
                pe.wait_ge(*copied("yb", g))
            for h in range(HEADS):
                pe.wait_ge(*copied("o", h))
            pe.wait_ge(*copied("so", 0))
            for gk, wk, rhs in (("gB", "wb", ybT), ("gM", "wm", oT)):
                for i in range(2):
                    for c in range(4 * i, 4 * i + 4):
                        pe.wait_ge(*loaded(gk, c // 2))
                        to_channels(gk, c, slot(gk, c // 2).rearrange("p (k n) -> p k n", k=KD), c % 2, xT)\
                            .then_inc(*fills(gk, c))
                    pe.wait_ge(*loaded(wk, i))
                    for c in range(4 * i, 4 * i + 4):
                        to_channels(wk, c, slot(wk, i).rearrange("p (k n) -> p k n", k=4), c % 4, rhs, 4)\
                            .then_inc(*fills(wk, c))
            pe.wait_ge(h_added, 2 * KD)
            for s in range(4):
                to_tokens("wo", s, hT)

            pe.wait_ge(x1_ready, 3)
            for k in range(KD):
                out = opens("x1T", k)
                for tt in range(3):
                    ins = pe.transpose(out[:, P * tt:P * tt + ROWS[tt]], x[0:ROWS[tt], tt, P * k:P * k + P],
                                       ident[0:ROWS[tt], 0:ROWS[tt]])
                ins.then_inc(*fills("x1T", k))
            for k in range(KD):
                pe.wait_ge(*copied("x1T", k))
            out = opens("rt", 0)
            for tt in range(3):
                ins = contract(out[0:ROWS[tt], NE * tt:NE * tt + NE],
                               [(x1T[:, k, P * tt:P * tt + ROWS[tt]], wr[:, k, :]) for k in range(KD)])
            ins.then_inc(*fills("rt", 0))
            pe.wait_ge(mask_ready, 1)
            out = opens("rank", 0)
            for tt in range(4):
                m = ROWS[tt] if tt < 3 else P
                pairs = [(ones[0:ROWS[j], 0:m], mask[0:ROWS[j], j, :]) for j in range(tt)]
                if tt < 3:
                    pairs.append((upper[0:m, 0:m], mask[0:m, tt, :]))
                ins = contract(out[0:m, NE * tt:NE * tt + NE], pairs)
            ins.then_inc(*fills("rank", 0))
            pe.wait_ge(gates_ready, 1)
            out = opens("gT", 0)
            for tt in range(3):
                ins = pe.transpose(out[0:NE, P * tt:P * tt + ROWS[tt]], gates[0:ROWS[tt], tt, 0:NE],
                                   ident[0:ROWS[tt], 0:ROWS[tt]])
            ins.then_inc(*fills("gT", 0))
            pe.wait_ge(*copied("gT", 0))
            pe.wait_ge(b2_in, 16)
            for i in range(6):
                tt, dh = i // 2, i % 2
                pe.matmul(opens("b2", i)[0:ROWS[tt], :], gatesT[:, P * tt:P * tt + ROWS[tt]],
                          b2s[:, 512 * dh:512 * dh + 512], start=True, stop=True).then_inc(*fills("b2", i))
            for key, n in TILES.items():
                if n >= len(TILES) - 8:
                    pe.wait_ge(*copied(*key))
            pe.wait_ge(b1_ready, 1)

            def gather(g, buf):
                pe.wait_ge(pick_ready, g + 1)
                for k in range(KD):
                    ins = contract(ps[:, XG, CAP * k:CAP * k + CAP],
                                   [(x[0:ROWS[tt], tt, P * k:P * k + P], pick[0:ROWS[tt], buf, tt, :])
                                    for tt in range(3)])
                ins.then_inc(xg_done, 1)

            def pair(q, i):
                n = q * (NE // 2) + i
                for par in range(2):
                    e = 2 * n + par
                    g = q * (NE + 1) + 2 * i + par
                    pe.wait_ge(xg_ready, g + 1)
                    parts = [(GB, 0), (GB, 1), (LB, 0), (LB, 1)]
                    for p, (b, hh) in enumerate(parts):
                        pe.matmul(ps[CAP * hh:CAP * hh + CAP, b, :], sel[:, par, :], b1s[:, 512 * p:512 * p + 512],
                                  start=True, stop=False)
                    for k in range(KD):
                        s = NH + k
                        pe.wait_ge(slot_full[s % RING], 16 * (e + s // RING + 1))
                        for p, (b, hh) in enumerate(parts):
                            ins = pe.matmul(ps[CAP * hh:CAP * hh + CAP, b, :], xg[:, k, :],
                                            ring[:, s % RING, 512 * p:512 * p + 512], start=False, stop=(k == KD - 1))
                        ins.then_inc(slot_free if k < KD - 1 else up_done, 1)
                    gather(g + 1, 1 - par)
                    pe.wait_ge(act_ready, e + 1)
                    for c in range(4):
                        ins = pe.transpose(ps[:, AT, P * c:P * c + P], act_s[:, P * c:P * c + P], ident[:, :])
                    ins.then_inc(act_turned, 1)
                    if par == 1:
                        pe.wait_ge(pickg_ready, n + 1)
                        for tt in range(3):
                            ins = pe.transpose(ps[:, ST, P * tt:P * tt + ROWS[tt]],
                                               pickg[0:ROWS[tt], tt, :, :].rearrange("p e s -> p (e s)"),
                                               ident[0:ROWS[tt], 0:ROWS[tt]])
                        ins.then_inc(pickT_turned, 1)
                        pe.wait_ge(y_ready, 2 * n + 1)
                    pe.wait_ge(actT_ready, e + 1)
                    for j in range(KD, RING):
                        s = NH + j
                        w = ring[:, s % RING, :].rearrange("p (k n) -> p k n", k=2)
                        pe.wait_ge(slot_full[s % RING], 16 * (e + s // RING + 1))
                        for kk in range(2):
                            f = 2 * (j - KD) + kk
                            for dh in range(2):
                                ins = pe.matmul(ps[CAP * dh:CAP * dh + CAP, YB, :], actT[:, f % 4, f // 4, :],
                                                w[:, kk, 512 * dh:512 * dh + 512], start=(f == 0), stop=(f == KD - 1))
                        ins.then_inc(slot_free if j < RING - 1 else y_done, 1)
                pe.wait_ge(pickT_ready, n + 1)
                pe.wait_ge(y_ready, 2 * n + 2)
                for t in range(6):
                    tt, dh = t // 2, t % 2
                    if t >= 2:
                        pe.wait_ge(part_added, 6 * n + t - 1)
                    pe.matmul(ps[0:ROWS[tt], O0 + t % 2, :], pickT[:, P * tt:P * tt + ROWS[tt]],
                              ypair[:, 512 * dh:512 * dh + 512], start=True, stop=True).then_inc(part_done, 1)

            gather(0, 0)
            with pe.Fori(0, NE // 2) as i:
                pair(0, i)
            pe.wait_ge(npass_ready, 1)
            passes = pe.value_load(npass[0:1, 0:1], min_val=1, max_val=PASSES)
            with pe.If(passes > 1):
                with pe.Fori(1, passes) as q:
                    gather(q * (NE + 1), 0)
                    with pe.Fori(0, NE // 2) as i:
                        pair(q, i)


_INS = ['x_prompt', 'x_sample', 'state_pool', 'cache_mem_k', 'cache_mem_v', 'mem_prompt', 'w_in', 'b_in', 'ln_v_g',
        'ln_v_b', 'w_s', 'b_s', 'w_a_out', 'w_pool', 'ls_pool', 'w_b_out', 'w_mk', 'w_mv', 'w_m_out', 'w_o', 'ln1_g',
        'ln1_b', 'w_r', 'b_r', 'w1', 'b1', 'w2', 'b2', 'ln2_g', 'ln2_b']
_OUTS = [('y_p', (SEQ, D), (1, SEQ, D)), ('y_s', (NB * LS, D), (NB, LS, D)),
         ('pool_p', (HIST, 512), (1, 1, HIST, 512)), ('pool_s', (NB, HIST, 512), (1, NB, HIST, 512)),
         ('mk', (MEM, 512), (1, 1, MEM, HEADS, P)), ('mv', (MEM, 512), (1, 1, MEM, HEADS, P)),
         ('cv', (NB * LS, D), (1, NB, LS, D))]


def kernel(**inputs):
    import numpy as _np
    import concourse.bacc as _bacc
    from concourse import mybir as _mybir
    from concourse.bass_utils import run_bass_kernel_spmd as _run

    nc = _bacc.Bacc("TRN2", target_bir_lowering=False, num_devices=1)
    arrays, ins, outs = {}, {}, {}
    for name in _INS:
        v = _np.ascontiguousarray(inputs[name])
        v = v.reshape(-1, D) if name == 'x_sample' else v.reshape(v.shape[1:])
        arrays[f"in_{name}"] = v
        ins[name] = nc.dram_tensor(f"in_{name}", v.shape, _mybir.dt.from_np(v.dtype), kind="ExternalInput").ap()
    for name, shape, _ in _OUTS:
        outs[name] = nc.dram_tensor(f"out_{name}", shape, F32, kind="ExternalOutput").ap()
    build(nc, ins, outs)
    r = _run(nc, [arrays], core_ids=[0])
    return tuple(_np.asarray(r.results[0][f"out_{name}"]).reshape(shape) for name, _, shape in _OUTS)
```

```python
from contextlib import ExitStack

import concourse.bass as bass
from concourse import mybir

F32 = mybir.dt.float32
BF16 = mybir.dt.bfloat16
I32 = mybir.dt.int32
ALU = mybir.AluOpType
ACT = mybir.ActivationFunctionType
AX = mybir.AxisListType

P = 128
D = 1024
KD = D // P
SEQ, NB, LS = 256, 8, 8
T = SEQ + NB * LS
ROWS = [128, 128, 64]
GA = 8
HEADS, MEM = 4, 256
PG, HIST = 4, 15
WINDOWS = [2, 4, 8, 16]
NE, TOPK = 32, 4
CAP = 64
PASSES = T // CAP
SCALE = float(P) ** -0.5
EPS = 1e-5
ALPHA = 2.0 ** 0.25
SW_LIMIT, SW_ALPHA = 7.0, 1.702

SLOT = 2048
RING = 12
SEG = HIST + LS
EXT = HIST + SEQ + NB * SEG


TOKEN_ORDER = [x for s in (0, 2) for x in ((s, 0), (s, 1), (s, 2), (s + 1, 0), (s + 1, 1))]
TILE_ORDER = (2, 0, 1)


def head_slots():
    s = [("v", i) for i in range(4)] + [("u", i) for i in range(4)] + [("mem", 0)]
    s += [(w, i) for w in ("mk", "mv", "q") for i in range(2)]
    s += [(w, i) for w in ("kc", "vc") for i in range(4)] + [("p", i) for i in range(2)]
    for i in range(4):
        s += [("gA", i), ("wa", i)]
    for g, w in (("gB", "wb"), ("gM", "wm")):
        for i in range(2):
            s += [(g, 2 * i), (g, 2 * i + 1), (w, i)]
    return s + [("wo", i) for i in range(4)]


def head_tiles():
    t = [("xT", k) for k in range(KD)] + [("bias", 0)]
    t += [("v",) + x for x in TOKEN_ORDER] + [("u", c) for c in range(KD)]
    t += [("ws", 0), ("ws", 1), ("bd", 0)] + [("mix", g) for g in range(GA)]
    t += [("mem", i) for i in range(4)] + [(w, i) for w in ("mk", "mv", "mkp") for i in range(2)]
    t += [("q", h) for h in range(HEADS)] + [("sc", h) for h in range(HEADS)]
    for hp in range(2):
        t += [("kt", hp, b) for b in range(NB)] + [("ss", hp)]
    t += [("pt", 0), ("pt", 1), ("o", 0), ("pt", 2), ("o", 1), ("pt", 3), ("o", 2), ("o", 3)]
    t += [("pst", 0), ("pst", 1), ("sv", 0), ("sv", 1), ("hist", 0), ("so", 0), ("so", 1)] + [("p", g) for g in range(PG)] + [("pout", 0)]
    for i in range(4):
        t += [("gA", 2 * i), ("gA", 2 * i + 1), ("wa", 2 * i), ("wa", 2 * i + 1)]
    t += [("yb", g) for g in range(PG)]
    for g, w in (("gB", "wb"), ("gM", "wm")):
        for i in range(2):
            t += [(g, 4 * i + c) for c in range(4)] + [(w, 4 * i + c) for c in range(4)]
    t += [("wo",) + x for x in TOKEN_ORDER]
    t += [("x1T", 2, 0), ("x1T", 2, 1), ("x1T", 0, 0), ("x1T", 0, 1), ("rt", 2), ("rt", 0)]
    return t + [("x1T", 1, 0), ("x1T", 1, 1), ("rt", 1), ("rank", 0)]


SLOTS = {key: n for n, key in enumerate(head_slots())}
TILES = {key: n for n, key in enumerate(head_tiles())}
NH = len(SLOTS)


def build(nc, a, o):
    ctx = ExitStack()
    with ctx:
        def sem(name):
            return ctx.enter_context(nc.semaphore(name))

        top = [(nc.sbuf_base + 63) // 64 * 64]

        def region(nbytes):
            at = top[0]
            top[0] += (nbytes + 31) // 32 * 32
            assert top[0] <= nc.sbuf_usable_end
            return at

        def at(name, shape, off, dt=F32):
            return nc.alloc_sbuf_tensor_at(name, shape, dt, offset=off)

        def small(name, shape, dt=F32):
            n = 4
            for x in shape[1:]:
                n *= x
            return at(name, shape, region(n), dt)

        ring = at("ring", [P, RING, SLOT], region(RING * SLOT * 4))
        x = small("x", [P, 3, D])
        rC = region(12288)
        vn = at("vn", [P, 3, D], rC)
        mkT = at("mkT", [P, HEADS, MEM], rC)
        mvp = at("mvp", [P, 2, HEADS * P], rC + 4096)
        mkp = at("mkp", [P, 2, HEADS * P], rC + 8192)
        pcur = at("pcur", [P, PG, T], rC)
        ybT = at("ybT", [P, PG, T], rC)
        dT = at("dT", [P, PG, T], rC + 5120)
        yacc = at("yacc", [P, 3, D], rC)
        rD = region(10240)
        xT = at("xT", [P, KD, T], rD)
        x1T = at("x1T", [P, KD, T], rD)
        pick = at("pick", [P, 3, 2, CAP], rD)
        pickg = at("pickg", [P, 3, 2, CAP], rD + 1536)
        rE = region(23040)
        bvb = at("bvb", [P, 3, D], rE)
        memT = at("memT", [P, KD, MEM], rE + 12288)
        kTs = at("kTs", [P, NB, 2, MEM], rE)
        QSTEP = NB * LS + LS
        qmask = at("qmask", [P, 2, NB * QSTEP], rE + 16384)
        Ps = at("Ps", [P, 2, MEM], rE + 20992)
        ext = [at(f"ext{i}", [P, PG, EXT], rE + 7296 * i) for i in range(3)]
        lnb = at("lnb", [P, 4, D], rE)
        b2x = at("b2x", [3 * NE, D], rE + 16384)
        b2s = at("b2s", [3 * NE, D], rE + 20480, BF16)
        rF = region(10240)
        qT = at("qT", [P, HEADS, T], rF)
        oT = at("oT", [P, HEADS, T], rF + 5120)
        sov = at("sov", [P, 2, HEADS * P], rF)
        b1s = at("b1s", [3 * NE, 2 * D], rF, BF16)
        ypair = at("ypair", [P, D], rF + 4096)
        rG = region(8192)
        wsr = at("wsr", [P, GA, P], rG)
        Pp = at("Pp", [P, HEADS, 2, MEM], rG)
        pout = at("pout", [P, PG * P], rG)
        gm, sg, lin, gs = (at(n, [P, 512], rG + 2048 * i) for i, n in enumerate(("gm", "sg", "lin", "gs")))
        rH = region(10240)
        uT = at("uT", [P, KD, T], rH)
        b1x = at("b1x", [3 * NE, 2 * D], rH)
        rJ = region(10240)
        wsT = at("wsT", [P, GA, P], rJ)
        bd = at("bd", [NB * LS, GA, NB * LS], rJ + 4096)
        bsb = at("bsb", [P, GA, P], rJ + 6144)
        histr = at("histr", [NB * HIST, PG * P], rJ)
        PTs = at("PTs", [P, 2, NB, HEADS, LS], rJ + 7680)
        hT = at("hT", [P, KD, T], rJ)
        xg = at("xg", [P, KD, 2, CAP], rJ)
        act_s = at("act_s", [P, 512], rJ + 4096)
        actT = at("actT", [P, 4, 2, CAP], rJ + 6144)
        pickT = at("pickT", [P, T], rJ + 8192)
        rK = region(5120)
        gbuf = at("gbuf", [P, 4, T], rK)
        PT = at("PT", [P, 2, 2, SEQ], rK)
        mtmp = at("mtmp", [P, 2, T], rK)
        ident = small("ident", [P, P])
        upper_f, ones_f = at("upper_f", [P, P], rK), at("ones_f", [P, P], rK + 512)
        upper = small("upper", [P, P], BF16)
        ones = small("ones", [P, P], BF16)
        slotj = small("slotj", [P, CAP])
        slotj_i = at("slotj_i", [P, CAP], rJ, I32)
        bdmask = small("bdmask", [NB * LS, NB, LS])
        rep8 = small("rep8", [LS, NB, LS])
        selcol = small("selcol", [3 * NE, NE + 2])
        sel = small("sel", [3 * NE, 2, CAP], BF16)
        zeros32 = small("zeros32", [P, NE])
        pos_i = at("pos_i", [P, HIST + 1], rJ + 256, I32)
        pos_f = at("pos_f", [P, HIST + 1], rJ + 320)
        ratio = small("ratio", [P, PG, HIST + 1])
        thr = small("thr", [1, PASSES - 1])
        wpool = at("wpool", [P, PG, P], region(2048))
        brow = at("brow", [52, P], rK + 4096)
        bT = small("bT", [P, 52])
        wr = small("wr", [P, KD, NE])
        brb = small("brb", [P, NE])
        mx = small("mx", [P, 10])
        nmx = small("nmx", [P, 10])
        ssum = small("ssum", [P, 10])
        rsum = small("rsum", [P, 10])
        stats = small("stats", [P, 3, 4, 6])
        mv = small("mv", [P, 3, 2])
        rstd = small("rstd", [P, 3])
        lg = small("lg", [P, 3, NE])
        top8 = small("top8", [P, 3, 8])
        gt = at("gt", [P, 3, NE], rH + 8192)
        eq = at("eq", [P, 3, NE], rH + 8576)
        ceq = at("ceq", [P, 3, NE], rH + 8960)
        mask = small("mask", [P, 3, NE], BF16)
        nsel = small("nsel", [P, 3])
        ge = at("ge", [P, 3, NE], rH + 9344)
        gsum = small("gsum", [P, 3])
        gates = small("gates", [P, 3, NE])
        slotv = small("slotv", [P, 3, NE + 2])
        cmax = small("cmax", [1, 2])
        late = small("late", [1, PASSES - 1])
        npass = small("npass", [1, 1], I32)
        ps = ctx.enter_context(nc.psum_tensor("ps", [P, 8, 512], F32))

        slot_full = [sem(f"slot_full{i}") for i in range(RING)]
        slot_free = sem("slot_free")
        bank_full = [sem(f"bank_full{i}") for i in range(8)]
        bank_free = [sem(f"bank_free{i}") for i in range(8)]
        x_in, bias_in, vparam_in, const_in, ws_in, hist_in, ln_in, b1_in, b2_in = (sem(n) for n in (
            "x_in", "bias_in", "vparam_in", "const_in", "ws_in", "hist_in", "ln_in", "b1_in", "b2_in"))
        cv_out, mkv_out, pout_out, hist_out, y_out = (sem(n) for n in (
            "cv_out", "mkv_out", "pout_out", "hist_out", "y_out"))
        consts, ops_pool, ops_dve = sem("consts"), sem("ops_pool"), sem("ops_dve")
        v_gelu, v_norm, wsT_ready, a_ready = (sem(n) for n in (
            "v_gelu", "v_norm", "wsT_ready", "a_ready"))
        var_ready, std_ready, rstd_ready = sem("var_ready"), sem("std_ready"), sem("rstd_ready")
        sm_max, sm_done, qmask_ready, d_ready, h_added = (sem(n) for n in (
            "sm_max", "sm_done", "qmask_ready", "d_ready", "h_added"))
        x1_left, x1_right, y_normal = (sem(n) for n in ("x1_left", "x1_right", "y_normal"))
        lg_ready, ge_ready, mask_ready, gates_ready, ebias_ready, npass_ready = (sem(n) for n in (
            "lg_ready", "ge_ready", "mask_ready", "gates_ready", "ebias_ready", "npass_ready"))
        slots_moved, pick_ready, sel_ready, pickg_ready, pickT_turned, pickT_ready = (sem(n) for n in (
            "slots_moved", "pick_ready", "sel_ready", "pickg_ready", "pickT_turned", "pickT_ready"))
        xg_done, xg_ready, up_done, gm_ready, lin_ready = (sem(n) for n in (
            "xg_done", "xg_ready", "up_done", "gm_ready", "lin_ready"))
        sg_ready, gs_ready, act_ready, act_turned, actT_ready = (sem(n) for n in (
            "sg_ready", "gs_ready", "act_ready", "act_turned", "actT_ready"))
        y_done, y_ready, part_done, part_added, yacc_begun = (sem(n) for n in (
            "y_done", "y_ready", "part_done", "part_added", "yacc_begun"))

        def bank(*key):
            return ps[:, TILES[key] % 8, :]

        def full(*key):
            return bank_full[TILES[key] % 8], TILES[key] // 8 + 1

        def fills(*key):
            return bank_full[TILES[key] % 8], 1

        def frees(*key):
            return bank_free[TILES[key] % 8], 1

        def copied(*key):
            return bank_free[TILES[key] % 8], TILES[key] // 8 + 1

        def slot(*key):
            return ring[:, SLOTS[key] % RING, :]

        def loaded(*key):
            return slot_full[SLOTS[key] % RING], 16 * (SLOTS[key] // RING + 1)

        def last_use(kind, i):
            if kind in ("v", "wo"):
                return (kind, i, 2) if i % 2 == 0 else (kind, i, 1)
            if kind in ("mk", "mv"):
                return kind, i
            return {"mem": ("mem", 3), "kc": ("kt", 1, 2 * i + 1), "vc": ("sv", i // 2), "wb": ("wb", 4 * i + 3),
                    "wm": ("wm", 4 * i + 3)}.get(kind, (kind, 2 * i + 1))

        def wcols(w, c0, k=KD, n=256):
            return w[:, c0:c0 + n].rearrange("(k p) n -> p k n", k=k)

        def rows(v):
            return v.unsqueeze(0).broadcast_to([P, v.shape[0]])

        OFF = {"u": 0, "v": D, "p": 2 * D, "q": 2 * D + 512, "gA": 3 * D, "gB": 4 * D, "gM": 5 * D}
        BIAS = {k: v // P for k, v in OFF.items()}
        LS_COL = 48

        def source(kind, i):
            if kind in OFF:
                return wcols(a["w_in"], OFF[kind] + 256 * i)
            if kind == "mem":
                return a["mem_prompt"].rearrange("(m p) d -> p m d", m=2)
            if kind in ("kc", "vc"):
                c = a["cache_mem_k" if kind == "kc" else "cache_mem_v"]
                return c[2 * i:2 * i + 2].rearrange("b (m p) h d -> p (b m) (h d)", m=2)
            if kind in ("wb", "wm"):
                return wcols(a["w_b_out" if kind == "wb" else "w_m_out"], 512 * i, 4, 512)
            w = {"mk": "w_mk", "mv": "w_mv", "wa": "w_a_out", "wo": "w_o"}[kind]
            return wcols(a[w], 256 * i)

        block = ctx.enter_context(nc.Block())

        def gate_used(n):
            return copied("wa", n) if n < KD else (h_added, n - KD + 1)

        GB, LB, XG, AT, YB, O0, ST = 0, 1, 2, 4, 5, 6, 7
        PAIRS = NE // 2

        HALF = D // 2

        def norm_half(link, buf, tt, side, g, b):
            r, c = slice(0, ROWS[tt]), slice(HALF * side, HALF * side + HALF)
            v = buf[r, tt, c]
            link(nc.vector.scalar_tensor_tensor(out=v, in0=v, scalar=mv[r, tt, 0:1], in1=g[r, c],
                                                op0=ALU.subtract, op1=ALU.mult))
            return nc.vector.scalar_tensor_tensor(out=v, in0=v, scalar=rstd[r, tt:tt + 1], in1=b[r, c],
                                                  op0=ALU.mult, op1=ALU.add)

        def turned(copy, tt, h):
            m = ROWS[tt]
            copy(x1T[:, 4 * h:4 * h + 4, P * tt:P * tt + m],
                 bank("x1T", tt, h)[:, 0:4 * m].rearrange("p (k t) -> p k t", k=4)).then_inc(*frees("x1T", tt, h))

        @block.sync
        def _(sp):
            slots = list(SLOTS)
            for m in range(2):
                sp.dma_start(x[:, m, :], a["x_prompt"][P * m:P * m + P, :]).then_inc(x_in, 16)
            sp.dma_start(x[0:64, 2, :], a["x_sample"]).then_inc(x_in, 16)
            for n, key in enumerate(slots):
                if n >= RING:
                    sp.wait_ge(*full(*last_use(*slots[n - RING])))
                src = source(*key)
                sp.dma_start(slot(*key).rearrange("p (k n) -> p k n", k=src.shape[1]), src)\
                    .then_inc(slot_full[n % RING], 16)

            def load(e, j):
                n = (NH + j) % RING
                if j < KD:
                    src = a["w1"][e, j * P:(j + 1) * P, :].rearrange("e p n -> p (e n)")
                    dst = ring[:, n, :]
                else:
                    r0 = 2 * (j - KD) * P
                    src = a["w2"][e, r0:r0 + 2 * P, :].rearrange("e (k p) n -> p (e k) n", k=2)
                    dst = ring[:, n, :].rearrange("p (k n) -> p k n", k=2)
                sp.dma_start(dst, src).then_inc(slot_full[n], 16)

            def expert(q, e):
                before = q * NE + e - 1
                for j in range(RING):
                    if j == KD - 1:
                        sp.wait_ge(up_done, before + 1)
                    elif j == RING - 1:
                        sp.wait_ge(y_done, before + 1)
                    else:
                        sp.wait_ge(slot_free, before * (RING - 2) + (j if j < KD else j - 1) + 1)
                    load(bass.ds(e, 1), j)

            for j in range(RING):
                sp.wait_ge(*full(*last_use(*slots[NH - RING + j])))
                load(slice(0, 1), j)
            with sp.Fori(1, NE) as e:
                expert(0, e)
            sp.wait_ge(npass_ready, 1)
            passes = sp.value_load(npass[0:1, 0:1], min_val=1, max_val=PASSES)
            with sp.If(passes > 1):
                with sp.Fori(1, passes) as q:
                    with sp.Fori(0, NE) as e:
                        expert(q, e)
            for tt in range(3):
                sp.wait_ge(y_normal, tt + 1)
                dst = o["y_p"][P * tt:P * tt + P, :] if tt < 2 else o["y_s"]
                sp.dma_start(dst, yacc[0:ROWS[tt], tt, :]).then_inc(y_out, 16)
            sp.wait_ge(y_out, 48)

        @block.gpsimd
        def _(pool):
            n = [0]

            def link(ins):
                n[0] += 1
                ins.then_inc(ops_pool, 1)
                pool.wait_ge(ops_pool, n[0])

            def select(out, op, fill, base, pattern, mult):
                return pool.affine_select(out=out, in_=out, compare_op=op, fill=fill, base=base,
                                          pattern=pattern, channel_multiplier=mult)

            link(pool.memset(ident[:, :], 0.0))
            select(ident[:, :], ALU.not_equal, 1.0, 0, [[-1, P]], 1).then_inc(consts, 1)
            pool.memset(ones_f[:, :], 1.0).then_inc(consts, 1)
            link(pool.memset(upper_f[:, :], 1.0))
            select(upper_f[:, :], ALU.is_gt, 0.0, 0, [[1, P]], -1).then_inc(consts, 1)
            link(pool.memset(bdmask[:, :, :], 1.0))
            link(select(bdmask[:, :, :], ALU.is_ge, 0.0, 0, [[-LS, NB], [0, LS]], 1))
            select(bdmask[:, :, :], ALU.is_ge, 0.0, LS - 1, [[LS, NB], [0, LS]], -1).then_inc(consts, 1)
            link(pool.memset(rep8[:, :, :], 0.0))
            select(rep8[:, :, :], ALU.not_equal, 1.0, 0, [[0, NB], [-1, LS]], 1).then_inc(consts, 1)
            link(pool.memset(selcol[:, :], 0.0))
            for r in range(3):
                ins = select(selcol[:, 0:NE], ALU.not_equal, 1.0, -NE * r, [[-1, NE]], 1)
                if r < 2:
                    link(ins)
            ins.then_inc(consts, 1)
            pool.iota(slotj_i[:, :], [[1, CAP]], base=0, channel_multiplier=0).then_inc(consts, 1)
            pool.iota(pos_i[:, :], [[1, HIST + 1]], base=1, channel_multiplier=0).then_inc(consts, 1)
            for i in range(PASSES - 1):
                ins = pool.memset(thr[:, i:i + 1], float(CAP * (i + 1)))
            ins.then_inc(consts, 1)
            pool.memset(zeros32[:, :], 0.0).then_inc(consts, 1)

            pool.dma_start(o["pool_s"][:, 0:HIST - LS, :], a["state_pool"][:, LS:HIST, :]).then_inc(hist_out, 16)
            pool.wait_ge(*copied("ws", 0))
            pool.wait_ge(*copied("ws", 1))
            select(wsT[:, :, :], ALU.is_ge, 0.0, 0, [[0, GA], [1, P]], -1).then_inc(wsT_ready, 1)
            pool.wait_ge(v_norm, 1)
            pool.dma_start(o["cv"], vn[0:NB * LS, 2, :]).then_inc(cv_out, 16)
            pool.wait_ge(a_ready, GA)
            pool.dma_start(histr[:, :], a["state_pool"].rearrange("b t c -> (b t) c")).then_inc(hist_in, 16)
            for m in range(2):
                pool.wait_ge(*copied("mv", m))
            pool.dma_start(o["mv"].rearrange("(m p) c -> p m c", m=2), mvp[:, :, :]).then_inc(mkv_out, 16)
            for m in range(2):
                pool.wait_ge(*copied("mkp", m))
            pool.dma_start(o["mk"].rearrange("(m p) c -> p m c", m=2), mkp[:, :, :]).then_inc(mkv_out, 16)
            pool.wait_ge(*copied("pout", 0))
            pool.dma_start(o["pool_p"], pout[49:64, :]).then_inc(pout_out, 16)
            for b in range(NB):
                pool.dma_start(o["pool_s"][b, HIST - LS:HIST, :], pout[64 + LS * b:64 + LS * (b + 1), :])\
                    .then_inc(pout_out, 16)
            pool.wait_ge(d_ready, PG)
            for i, w in enumerate(("ln1_g", "ln1_b", "ln2_g", "ln2_b")):
                pool.dma_start(lnb[:, i, :], rows(a[w]))\
                    .then_inc(ln_in, 16)
            for r in range(3):
                pool.dma_start(b2x[r * NE:(r + 1) * NE, :], a["b2"]).then_inc(b2_in, 16)
            pool.wait_ge(*full("yb", 0))
            for r in range(3):
                pool.dma_start(b1x[r * NE:(r + 1) * NE, :], a["b1"]).then_inc(b1_in, 16)

            def three_parts(parts, b):
                for r in range(3):
                    part = slice(r * NE, (r + 1) * NE)
                    for _ in range(r):
                        link(pool.tensor_copy(parts[part, :], b[part, :]))
                        link(pool.tensor_tensor(b[part, :], b[part, :], parts[part, :], ALU.subtract))
                    ins = pool.tensor_copy(parts[part, :], b[part, :])
                return ins

            pool.wait_ge(b2_in, 48)
            three_parts(b2s, b2x)
            pool.wait_ge(b1_in, 48)
            pool.wait_ge(*full("wo", 0, 0))
            three_parts(b1s, b1x).then_inc(ebias_ready, 1)

            pool.wait_ge(cv_out, 16)
            pool.wait_ge(mkv_out, 32)
            pool.wait_ge(pout_out, 16 * (1 + NB))
            pool.wait_ge(hist_out, 16)

        @block.scalar
        def _(act):
            act.dma_start(brow[0:48, :], a["b_in"].rearrange("(c p) -> c p", p=P)).then_inc(bias_in, 16)
            act.dma_start(brow[48:52, :], a["ls_pool"].rearrange("(c p) -> c p", p=P)).then_inc(bias_in, 16)
            for i, src in enumerate((a["b_in"][D:2 * D], a["ln_v_g"], a["ln_v_b"])):
                act.dma_start(bvb[:, i, :], rows(src))\
                    .then_inc(vparam_in, 16)
            act.dma_start(wsr[:, :, :], a["w_s"].rearrange("g t s -> t g s")).then_inc(ws_in, 16)
            act.dma_start(bsb[:, :, :].rearrange("p g t -> p (g t)"),
                          rows(a["b_s"].rearrange("g t -> (g t)"))).then_inc(const_in, 16)
            act.dma_start(wpool[:, :, :], a["w_pool"].rearrange("g c d -> c g d")).then_inc(const_in, 16)
            act.dma_start(wr[:, :, :], a["w_r"].rearrange("(k p) e -> p k e", k=KD)).then_inc(const_in, 16)
            act.dma_start(brb[:, :], rows(a["b_r"])).then_inc(const_in, 16)

            for k in range(1, KD, 2):
                act.wait_ge(*full("xT", k))
                act.copy(xT[:, k, :], bank("xT", k)[:, 0:T]).then_inc(*frees("xT", k))

            def root(nth, tt):
                r = slice(0, ROWS[tt])
                act.wait_ge(var_ready, nth)
                act.activation(rstd[r, tt:tt + 1], rstd[r, tt:tt + 1], ACT.Sqrt).then_inc(std_ready, 1)

            for s, tt in TOKEN_ORDER:
                r, cols = slice(0, ROWS[tt]), slice(256 * s, 256 * s + (512 if tt == 2 else 256))
                act.wait_ge(*copied("v", s, tt))
                act.activation(vn[r, tt, cols], vn[r, tt, cols], ACT.Gelu_apprx_tanh).then_inc(v_gelu, 1)
            for nth, tt in enumerate(TILE_ORDER):
                root(1 + nth, tt)
            act.wait_ge(*copied("bias", 0))
            for c in range(KD):
                act.wait_ge(*full("u", c))
                act.activation(uT[:, c, :], bank("u", c)[:, 0:T], ACT.Gelu_apprx_tanh,
                               bias=bT[:, BIAS["u"] + c:BIAS["u"] + c + 1]).then_inc(*frees("u", c))
            act.wait_ge(*full("mem", 1))
            act.copy(memT[:, 2:4, :], bank("mem", 1).rearrange("p (k m) -> p k m", k=2)).then_inc(*frees("mem", 1))
            act.wait_ge(*full("mem", 3))
            act.copy(memT[:, 6:8, :], bank("mem", 3).rearrange("p (k m) -> p k m", k=2)).then_inc(*frees("mem", 3))
            for i in range(2):
                act.wait_ge(*full("mk", i))
                act.copy(mkT[:, 2 * i:2 * i + 2, :], bank("mk", i).rearrange("p (h m) -> p h m", h=2))\
                    .then_inc(*frees("mk", i))
            act.wait_ge(cv_out, 16)
            for i in range(2):
                act.wait_ge(*full("mkp", i))
                act.copy(mkp[:, i, :], bank("mkp", i)).then_inc(*frees("mkp", i))
            for h in range(HEADS):
                act.wait_ge(*full("q", h))
                act.activation(qT[:, h, :], bank("q", h)[:, 0:T], ACT.Identity,
                               bias=bT[:, BIAS["q"] + h:BIAS["q"] + h + 1]).then_inc(*frees("q", h))
            for h in range(HEADS):
                act.wait_ge(sm_max, h + 1)
                for lt in range(2):
                    j = 2 * h + lt
                    ins = act.activation(Pp[:, h, lt, :], bank("sc", h)[:, lt * MEM:(lt + 1) * MEM], ACT.Exp,
                                         bias=nmx[:, j:j + 1], scale=SCALE, accum_out=ssum[:, j:j + 1])
                ins.then_inc(*frees("sc", h))
            for hp in range(2):
                for b in range(1, NB, 2):
                    act.wait_ge(*full("kt", hp, b))
                    act.copy(kTs[:, b, :, :], bank("kt", hp, b).rearrange("p (h m) -> p h m", h=2))\
                        .then_inc(*frees("kt", hp, b))
                act.wait_ge(sm_max, HEADS + hp + 1)
                act.activation(Ps[:, hp, :], bank("ss", hp)[:, 0:MEM], ACT.Exp, bias=nmx[:, 8 + hp:9 + hp],
                               scale=SCALE, accum_out=ssum[:, 8 + hp:9 + hp]).then_inc(*frees("ss", hp))
            for kind, h in (("pt", 0), ("pt", 1), ("o", 0), ("pt", 2), ("o", 1), ("pt", 3), ("o", 2), ("o", 3)):
                act.wait_ge(*full(kind, h))
                if kind == "pt":
                    act.copy(PT[:, h % 2, :, :], bank("pt", h).rearrange("p (m l) -> p m l", m=2))\
                        .then_inc(*frees("pt", h))
                else:
                    act.copy(oT[:, h, 0:SEQ], bank("o", h)[:, 0:SEQ]).then_inc(*frees("o", h))
            act.wait_ge(*full("sv", 0))
            act.copy(sov[:, 0, :], bank("sv", 0)).then_inc(*frees("sv", 0))
            act.wait_ge(mkv_out, 32)
            for g in range(PG):
                act.wait_ge(*full("p", g))
                act.activation(pcur[:, g, :], bank("p", g)[:, 0:T], ACT.Identity,
                               bias=bT[:, BIAS["p"] + g:BIAS["p"] + g + 1]).then_inc(*frees("p", g))

            def gate(kind, c, n):
                act.wait_ge(*full(kind, c))
                if n >= 4:
                    act.wait_ge(*gate_used(n - 4))
                act.activation(gbuf[:, n % 4, :], bank(kind, c)[:, 0:T], ACT.Sigmoid,
                               bias=bT[:, BIAS[kind] + c:BIAS[kind] + c + 1]).then_inc(*frees(kind, c))

            for c in range(KD):
                gate("gA", c, c)
            for g in range(PG):
                act.wait_ge(*full("yb", g))
                act.activation(ybT[:, g, :], bank("yb", g)[:, 0:T], ACT.Copy,
                               scale=bT[:, LS_COL + g:LS_COL + g + 1]).then_inc(*frees("yb", g))
            for c in range(KD):
                gate("gB", c, KD + c)
            for c in range(KD):
                gate("gM", c, 2 * KD + c)
            for nth, tt in enumerate(TILE_ORDER):
                root(4 + nth, tt)
            for tt, h in ((2, 0), (2, 1), (0, 0), (0, 1), (1, 1)):
                act.wait_ge(*full("x1T", tt, h))
                turned(act.copy, tt, h)
            act.wait_ge(lg_ready, 1)
            act.activation(ge[:, :, :], ge[:, :, :], ACT.Exp).then_inc(ge_ready, 1)

            def gathered(g, h):
                act.wait_ge(xg_done, 2 * g + h + 1)
                act.copy(xg[:, 4 * h:4 * h + 4, :, :],
                         ps[:, XG + h, :].rearrange("p (k e c) -> p k e c", k=4, e=2)).then_inc(xg_ready, 1)

            def pair(q, i):
                for par in range(2):
                    e = (q * NE + 2 * i) + par
                    act.wait_ge(gm_ready, e + 1)
                    act.activation(sg[:, :], gm[:, :], ACT.Sigmoid, scale=SW_ALPHA).then_inc(sg_ready, 1)
                    if par == 1:
                        for h in range(2):
                            gathered(q * (PAIRS + 1) + i + 1, h)
                    act.wait_ge(act_turned, e + 1)
                    act.copy(actT[:, :, :, :], ps[:, AT, :].rearrange("p (c h s) -> p c h s", c=4, h=2))\
                        .then_inc(actT_ready, 1)
                    act.wait_ge(y_done, e + 1)
                    act.copy(ypair[CAP * par:CAP * par + CAP, 0:512], ps[0:CAP, YB, :])
                    act.copy(ypair[CAP * par:CAP * par + CAP, 512:D], ps[CAP:2 * CAP, YB, :]).then_inc(y_ready, 1)

            for h in range(2):
                gathered(0, h)
            for nth, tt in enumerate(TILE_ORDER):
                r = slice(0, ROWS[tt])
                act.wait_ge(x1_right, nth + 1)
                act.activation(yacc[r, tt, :], x[r, tt, :], ACT.Copy, scale=ALPHA).then_inc(yacc_begun, 1)
            with act.Fori(0, PAIRS) as i:
                pair(0, i)
            act.wait_ge(npass_ready, 1)
            passes = act.value_load(npass[0:1, 0:1], min_val=1, max_val=PASSES)
            with act.If(passes > 1):
                with act.Fori(1, passes) as q:
                    for h in range(2):
                        gathered(q * (PAIRS + 1), h)
                    with act.Fori(0, PAIRS) as i:
                        pair(q, i)
            for tt in range(3):
                root(7 + tt, tt)

        @block.vector
        def _(dve):
            n = [0]

            def link(ins):
                n[0] += 1
                ins.then_inc(ops_dve, 1)
                dve.wait_ge(ops_dve, n[0])

            def moments(tt, parts, nth):
                r = slice(0, ROWS[tt])
                link(dve.bn_aggr(mv[r, tt, :], stats[r, tt, 0:parts, :].rearrange("p c s -> p (c s)")))
                dve.tensor_scalar(rstd[r, tt:tt + 1], mv[r, tt, 1:2], EPS, None, ALU.add).then_inc(var_ready, 1)

            def inverse(tt, nth):
                r = slice(0, ROWS[tt])
                dve.wait_ge(std_ready, nth)
                dve.reciprocal(rstd[r, tt:tt + 1], rstd[r, tt:tt + 1]).then_inc(rstd_ready, 1)
                dve.wait_ge(rstd_ready, nth)

            for k in range(0, KD, 2):
                dve.wait_ge(*full("xT", k))
                dve.tensor_copy(xT[:, k, :], bank("xT", k)[:, 0:T]).then_inc(*frees("xT", k))
            dve.wait_ge(*full("bias", 0))
            dve.tensor_copy(bT[:, :], bank("bias", 0)[:, 0:52]).then_inc(*frees("bias", 0))
            dve.wait_ge(consts, 10)
            dve.tensor_copy(ones[:, :], ones_f[:, :])
            dve.tensor_copy(upper[:, :], upper_f[:, :])
            dve.tensor_copy(slotj[:, :], slotj_i[:, :])
            link(dve.tensor_copy(pos_f[:, :], pos_i[:, :]))
            for g, w in enumerate(WINDOWS):
                ins = dve.tensor_scalar(ratio[:, g, :], pos_f[:, :], float(w), None, ALU.min)
            link(ins)
            link(dve.reciprocal(ratio[:, :, :], ratio[:, :, :]))
            for g, w in enumerate(WINDOWS):
                dve.tensor_scalar(ratio[:, g, :], ratio[:, g, :], float(w), None, ALU.mult)
            dve.memset(slotv[:, :, :], -1.0)
            dve.memset(gates[:, :, :], 0.0)
            link(dve.memset(lg[:, :, :], 0.0))

            dve.wait_ge(vparam_in, 48)
            for s, tt in TOKEN_ORDER:
                out = bank("v", s, tt)
                dve.wait_ge(*full("v", s, tt))
                if tt < 2:
                    cols = slice(256 * s, 256 * s + 256)
                    ins = dve.tensor_tensor(vn[:, tt, cols], out[:, 0:256], bvb[:, 0, cols], ALU.add)
                else:
                    for j in range(2):
                        part, cols = slice(64 * j, 64 * j + 64), slice(256 * (s + j), 256 * (s + j + 1))
                        ins = dve.tensor_tensor(vn[0:64, 2, cols], out[part, 0:256], bvb[part, 0, cols], ALU.add)
                ins.then_inc(*frees("v", s, tt))
            dve.wait_ge(v_gelu, len(TOKEN_ORDER))
            for nth, tt in enumerate(TILE_ORDER):
                r = slice(0, ROWS[tt])
                for c in range(2):
                    ins = dve.bn_stats(stats[r, tt, c, :], vn[r, tt, HALF * c:HALF * c + HALF])
                link(ins)
                moments(tt, 2, 1 + nth)
            for nth, tt in enumerate(TILE_ORDER):
                inverse(tt, 1 + nth)
                norm_half(link, vn, tt, 0, bvb[:, 1, :], bvb[:, 2, :])
                norm_half(link, vn, tt, 1, bvb[:, 1, :], bvb[:, 2, :]).then_inc(v_norm, 1)

            for i in range(2):
                dve.wait_ge(*full("ws", i))
                dve.tensor_copy(wsT[:, 4 * i:4 * i + 4, :], bank("ws", i).rearrange("p (g t) -> p g t", g=4))\
                   .then_inc(*frees("ws", i))
            dve.wait_ge(*full("bd", 0))
            dve.tensor_tensor(bd[:, :, :], bank("bd", 0)[0:64, :].rearrange("p (g t) -> p g t", g=GA),
                              bdmask[:, :, :].rearrange("p b t -> p (b t)").unsqueeze(1)
                              .broadcast_to([NB * LS, GA, NB * LS]), ALU.mult).then_inc(*frees("bd", 0))
            dve.wait_ge(const_in, 64)
            for g in range(GA):
                m, tmp = bank("mix", g), mtmp[:, g % 2, :]
                dve.wait_ge(*full("mix", g))
                if g >= 2:
                    dve.wait_ge(a_ready, g - 1)
                dve.tensor_tensor(tmp[:, 0:SEQ].rearrange("p (c t) -> p c t", c=2),
                                  m[:, 0:SEQ].rearrange("p (c t) -> p c t", c=2),
                                  bsb[:, g:g + 1, :].broadcast_to([P, 2, P]), ALU.add)
                dve.tensor_tensor(tmp[:, SEQ:T].rearrange("p (b t) -> p b t", b=NB),
                                  m[:, SEQ:T].rearrange("p (b t) -> p b t", b=NB),
                                  bsb[:, g:g + 1, 0:LS].broadcast_to([P, NB, LS]), ALU.add)\
                   .then_inc(*frees("mix", g))
                dve.wait_ge(*copied("mix", g))
                dve.wait_ge(*copied("u", g))
                dve.tensor_tensor(uT[:, g, :], uT[:, g, :], tmp, ALU.mult).then_inc(a_ready, 1)

            for i in (0, 2):
                dve.wait_ge(*full("mem", i))
                dve.tensor_copy(memT[:, 2 * i:2 * i + 2, :], bank("mem", i).rearrange("p (k m) -> p k m", k=2))\
                   .then_inc(*frees("mem", i))
            for i in range(2):
                dve.wait_ge(*full("mv", i))
                dve.tensor_copy(mvp[:, :, 256 * i:256 * i + 256], bank("mv", i).rearrange("p (m n) -> p m n", m=2))\
                   .then_inc(*frees("mv", i))
            link(dve.memset(qmask[:, :, :], 0.0))

            def row_max(j, w, scores):
                link(dve.tensor_reduce(mx[:, j:j + w], scores, AX.X, ALU.max))
                dve.tensor_scalar(nmx[:, j:j + w], mx[:, j:j + w], -SCALE, None, ALU.mult).then_inc(sm_max, 1)

            def own_queries(hp):
                for hh in range(2):
                    dve.wait_ge(*copied("q", 2 * hp + hh))
                    ins = dve.tensor_copy(
                        qmask[:, hh, :].rearrange("p (b s) -> p b s", s=QSTEP)[:, :, 0:LS],
                        qT[:, 2 * hp + hh, SEQ:T].rearrange("p (b l) -> p b l", b=NB))
                ins.then_inc(qmask_ready, 1)

            def turned_keys(hp):
                for b in range(0, NB, 2):
                    dve.wait_ge(*full("kt", hp, b))
                    dve.tensor_copy(kTs[:, b, :, :], bank("kt", hp, b).rearrange("p (h m) -> p h m", h=2))\
                       .then_inc(*frees("kt", hp, b))

            def sample_max(hp):
                dve.wait_ge(*full("ss", hp))
                row_max(8 + hp, 1, bank("ss", hp)[:, 0:MEM])

            for h in range(HEADS):
                dve.wait_ge(*full("sc", h))
                row_max(2 * h, 2, bank("sc", h).rearrange("p (t m) -> p t m", t=2))
            own_queries(0)
            turned_keys(0)
            sample_max(0)
            own_queries(1)
            turned_keys(1)
            for h in range(HEADS):
                dve.wait_ge(*copied("sc", h))
                link(dve.reciprocal(rsum[:, 2 * h:2 * h + 2], ssum[:, 2 * h:2 * h + 2]))
                for lt in range(2):
                    ins = dve.tensor_scalar(Pp[:, h, lt, :], Pp[:, h, lt, :], rsum[:, 2 * h + lt:2 * h + lt + 1],
                                            None, ALU.mult)
                ins.then_inc(sm_done, 1)
            sample_max(1)
            for hp in range(2):
                dve.wait_ge(*copied("ss", hp))
                link(dve.reciprocal(rsum[:, 8 + hp:9 + hp], ssum[:, 8 + hp:9 + hp]))
                dve.tensor_scalar(Ps[:, hp, :], Ps[:, hp, :], rsum[:, 8 + hp:9 + hp], None, ALU.mult)\
                   .then_inc(sm_done, 1)
            for hp in range(2):
                dve.wait_ge(*full("pst", hp))
                for m in range(2):
                    ins = dve.tensor_copy(PTs[:, m, :, 2 * hp:2 * hp + 2, :].transpose([0, 2, 1, 3]),
                                          bank("pst", hp)[:, P * m:P * m + P]
                                          .rearrange("p (h b t) -> p h b t", h=2, b=NB))
                ins.then_inc(*frees("pst", hp))
            dve.wait_ge(*full("sv", 1))
            dve.tensor_copy(sov[:, 1, :], bank("sv", 1)).then_inc(*frees("sv", 1))

            e0, e1, e2 = ext

            def own(t, lo, hi):
                return t[:, :, HIST + SEQ:EXT].rearrange("p g (b s) -> p g b s", s=SEG)[:, :, :, lo:hi]

            dve.wait_ge(*full("hist", 0))
            dve.memset(e0[:, :, 0:HIST], 0.0)
            dve.tensor_copy(own(e0, 0, HIST),
                            bank("hist", 0)[:, 0:PG * NB * HIST].rearrange("p (g b t) -> p g b t", g=PG, b=NB))\
               .then_inc(*frees("hist", 0))
            for i in range(2):
                dve.wait_ge(*full("so", i))
                for h in range(HEADS):
                    ins = dve.tensor_copy(
                        oT[:, h, SEQ + 32 * i:SEQ + 32 * i + 32].rearrange("p (b t) -> p b t", b=4),
                        bank("so", i)[:, P * h:P * h + P].rearrange("p (b c) -> p b c", b=4)[:, :, LS * h:LS * h + LS])
                ins.then_inc(*frees("so", i))
            for g in range(PG):
                dve.wait_ge(*copied("p", g))
            dve.tensor_copy(e0[:, :, HIST:HIST + SEQ], pcur[:, :, 0:SEQ])
            link(dve.tensor_copy(own(e0, HIST, SEG), pcur[:, :, SEQ:T].rearrange("p g (b l) -> p g b l", b=NB)))
            dve.wait_ge(*full("pout", 0))
            dve.tensor_copy(pout[:, :], bank("pout", 0)).then_inc(*frees("pout", 0))
            sums = e0
            for step, out in enumerate((e1, e2, e1, e2)):
                w = 1 << step
                link(dve.tensor_tensor(out[:, step:PG, 2 * w - 1:EXT], sums[:, step:PG, 2 * w - 1:EXT],
                                       sums[:, step:PG, w - 1:EXT - w], ALU.add))
                sums = out
            for g in range(PG):
                s = (e1, e2)[g % 2][:, g, HIST:2 * HIST + 1]
                ins = dve.tensor_tensor(s, s, ratio[:, g, :], ALU.mult)
            link(ins)
            dve.wait_ge(mkv_out, 32)
            for g, w in enumerate(WINDOWS):
                s = (e1, e2)[g % 2]
                dve.scalar_tensor_tensor(out=dT[:, g, 0:SEQ], in0=s[:, g, HIST:HIST + SEQ], scalar=1.0 / w,
                                         in1=e0[:, g, HIST:HIST + SEQ], op0=ALU.mult, op1=ALU.subtract)
                dve.scalar_tensor_tensor(out=dT[:, g, SEQ:T].rearrange("p (b l) -> p b l", b=NB),
                                         in0=own(s, HIST, SEG)[:, g], scalar=1.0 / w,
                                         in1=own(e0, HIST, SEG)[:, g], op0=ALU.mult, op1=ALU.subtract)\
                   .then_inc(d_ready, 1)

            for c in range(KD):
                dve.wait_ge(*full("wa", c))
                dve.wait_ge(*copied("gA", c))
                dve.tensor_tensor(hT[:, c, :], bank("wa", c)[:, 0:T], gbuf[:, c % 4, :], ALU.mult)\
                   .then_inc(*frees("wa", c))
            for g, w in (("gB", "wb"), ("gM", "wm")):
                for c in range(KD):
                    dve.wait_ge(*full(w, c))
                    dve.wait_ge(*copied(g, c))
                    dve.tensor_tensor(gbuf[:, c % 4, :], bank(w, c)[:, 0:T], gbuf[:, c % 4, :], ALU.mult)\
                       .then_inc(*frees(w, c))
                    dve.wait_ge(*copied(w, c))
                    dve.tensor_tensor(hT[:, c, :], hT[:, c, :], gbuf[:, c % 4, :], ALU.add).then_inc(h_added, 1)

            dve.wait_ge(ln_in, 64)
            for s, tt in TOKEN_ORDER:
                out = bank("wo", s, tt)
                r, n_slots = slice(0, ROWS[tt]), 2 if tt == 2 else 1
                dve.wait_ge(*full("wo", s, tt))
                for j in range(n_slots):
                    cols = slice(256 * (s + j), 256 * (s + j + 1))
                    src = out[64 * j:64 * j + 64, 0:256] if tt == 2 else out[:, 0:256]
                    ins = dve.scalar_tensor_tensor(out=x[r, tt, cols], in0=x[r, tt, cols], scalar=ALPHA, in1=src,
                                                   op0=ALU.mult, op1=ALU.add)
                ins.then_inc(*frees("wo", s, tt))
                dve.wait_ge(*copied("wo", s, tt))
                for j in range(n_slots):
                    ins = dve.bn_stats(stats[r, tt, s + j, :], x[r, tt, 256 * (s + j):256 * (s + j + 1)])
                if s + n_slots == 4:
                    nth = TILE_ORDER.index(tt)
                    link(ins)
                    moments(tt, 4, 4 + nth)
                    inverse(tt, 4 + nth)
                    norm_half(link, x, tt, 0, lnb[:, 0, :], lnb[:, 1, :]).then_inc(x1_left, 1)
                    norm_half(link, x, tt, 1, lnb[:, 0, :], lnb[:, 1, :]).then_inc(x1_right, 1)

            for tt in TILE_ORDER:
                r = slice(0, ROWS[tt])
                if tt == 1:
                    dve.wait_ge(*full("x1T", 1, 0))
                    turned(dve.tensor_copy, 1, 0)
                dve.wait_ge(*full("rt", tt))
                dve.tensor_tensor(lg[r, tt, :], bank("rt", tt)[r, 0:NE], brb[r, :], ALU.add).then_inc(*frees("rt", tt))
                dve.wait_ge(*copied("rt", tt))
                ins = dve.max(out=top8[:, tt, :], in_=lg[:, tt, :])
            link(ins)
            fourth = top8[:, :, TOPK - 1:TOPK].broadcast_to([P, 3, NE])
            dve.tensor_tensor(ge[:, :, :], lg[:, :, :], top8[:, :, 0:1].broadcast_to([P, 3, NE]), ALU.subtract)\
               .then_inc(lg_ready, 1)
            dve.tensor_tensor(eq[:, :, :], lg[:, :, :], fourth, ALU.is_equal)
            link(dve.tensor_tensor(gt[:, :, :], lg[:, :, :], fourth, ALU.is_gt))
            link(dve.tensor_reduce(nsel[:, :], gt[:, :, :], AX.X, ALU.add))
            dve.tensor_scalar(nsel[:, :], nsel[:, :], -1.0, float(TOPK), ALU.mult, ALU.add)
            for tt in range(3):
                ins = dve.tensor_tensor_scan(ceq[:, tt, :], eq[:, tt, :], zeros32[:, :], 0.0, ALU.add, ALU.add)
            link(ins)
            link(dve.tensor_tensor(ceq[:, :, :], ceq[:, :, :], nsel[:, :].unsqueeze(2).broadcast_to([P, 3, NE]),
                                   ALU.is_le))
            link(dve.tensor_tensor(eq[:, :, :], eq[:, :, :], ceq[:, :, :], ALU.mult))
            dve.tensor_tensor(mask[:, :, :], gt[:, :, :], eq[:, :, :], ALU.add).then_inc(mask_ready, 1)
            dve.wait_ge(mask_ready, 1)
            dve.wait_ge(ge_ready, 1)
            link(dve.tensor_tensor(ge[:, :, :], ge[:, :, :], mask[:, :, :], ALU.mult))
            link(dve.tensor_reduce(gsum[:, :], ge[:, :, :], AX.X, ALU.add))
            link(dve.reciprocal(gsum[:, :], gsum[:, :]))
            dve.tensor_tensor(gates[:, :, 0:NE], ge[:, :, :], gsum[:, :].unsqueeze(2).broadcast_to([P, 3, NE]),
                              ALU.mult).then_inc(gates_ready, 1)
            rk = bank("rank", 0)[:, 0:4 * NE].rearrange("p (t e) -> p t e", t=4)
            dve.wait_ge(*full("rank", 0))
            dve.tensor_reduce(cmax[:, 0:1], rk[0:1, 3, :], AX.X, ALU.max)
            dve.scalar_tensor_tensor(out=slotv[:, 0:2, 0:NE], in0=rk[:, 0:2, :], scalar=1.0, in1=mask[:, 0:2, :],
                                     op0=ALU.add, op1=ALU.mult)
            dve.scalar_tensor_tensor(out=slotv[0:64, 2, 0:NE], in0=rk[0:64, 2, :], scalar=1.0,
                                     in1=mask[0:64, 2, :], op0=ALU.add, op1=ALU.mult).then_inc(*frees("rank", 0))
            dve.wait_ge(*copied("rank", 0))
            dve.tensor_scalar(slotv[:, 0:2, 0:NE], slotv[:, 0:2, 0:NE], -1.0, None, ALU.add)
            link(dve.tensor_scalar(slotv[0:64, 2, 0:NE], slotv[0:64, 2, 0:NE], -1.0, None, ALU.add))

            def picks(i):
                for tt in range(3):
                    r = slice(0, ROWS[tt])
                    for par in range(2):
                        ins = dve.tensor_scalar(pick[r, tt, par, :], slotj[r, :],
                                                slotv[r, tt, bass.ds(2 * i + par, 1)], None, ALU.is_equal)
                ins.then_inc(pick_ready, 1)

            def choose(e, par):
                dve.tensor_copy(sel[:, par, :], selcol[:, bass.ds(e, 1)].broadcast_to([3 * NE, CAP]))\
                   .then_inc(sel_ready, 1)

            def pair(q, i):
                n = q * PAIRS + i
                dve.wait_ge(xg_done, 2 * (q * (PAIRS + 1) + i + 1))
                picks(i + 1)
                for par in range(2):
                    for tt in range(3):
                        r = slice(0, ROWS[tt])
                        ins = dve.tensor_scalar(pickg[r, tt, par, :], slotj[r, :],
                                                slotv[r, tt, bass.ds(2 * i + par, 1)],
                                                gates[r, tt, bass.ds(2 * i + par, 1)], ALU.is_equal, ALU.mult)
                ins.then_inc(pickg_ready, 1)
                for par in range(2):
                    e = 2 * n + par
                    dve.wait_ge(up_done, e + 1)
                    dve.tensor_scalar(gm[:, :], ps[:, GB, :], SW_LIMIT, None, ALU.min).then_inc(gm_ready, 1)
                    dve.tensor_scalar(lin[:, :], ps[:, LB, :], -SW_LIMIT, SW_LIMIT, ALU.max, ALU.min)\
                       .then_inc(lin_ready, 1)
                    dve.wait_ge(sg_ready, e + 1)
                    dve.tensor_tensor(gs[:, :], gm[:, :], sg[:, :], ALU.mult).then_inc(gs_ready, 1)
                    dve.wait_ge(gs_ready, e + 1)
                    dve.wait_ge(lin_ready, e + 1)
                    dve.scalar_tensor_tensor(out=act_s[:, :], in0=lin[:, :], scalar=1.0, in1=gs[:, :],
                                             op0=ALU.add, op1=ALU.mult).then_inc(act_ready, 1)
                    choose(2 * i + par + 2, par)
                dve.wait_ge(pickT_turned, n + 1)
                dve.tensor_copy(pickT[:, :], ps[:, ST, 0:T]).then_inc(pickT_ready, 1)
                for t in range(6):
                    tt, dh = t // 2, t % 2
                    y = yacc[0:ROWS[tt], tt, 512 * dh:512 * dh + 512]
                    dve.wait_ge(part_done, 6 * n + t + 1)
                    dve.tensor_tensor(y, ps[0:ROWS[tt], O0 + t % 2, :], y, ALU.add).then_inc(part_added, 1)

            dve.wait_ge(pout_out, 16 * (1 + NB))
            picks(0)
            for par in range(2):
                choose(par, par)
            link(dve.tensor_scalar(late[:, :], thr[:, :], cmax[:, 0:1], None, ALU.is_lt))
            link(dve.tensor_reduce(cmax[:, 1:2], late[:, :], AX.X, ALU.add))
            dve.tensor_scalar(npass[:, :], cmax[:, 1:2], 1.0, None, ALU.add).then_inc(npass_ready, 1)
            dve.wait_ge(npass_ready, 1)
            dve.wait_ge(yacc_begun, 3)
            with dve.Fori(0, PAIRS) as i:
                pair(0, i)
            passes = dve.value_load(npass[0:1, 0:1], min_val=1, max_val=PASSES)
            with dve.If(passes > 1):
                with dve.Fori(1, passes) as q:
                    dve.wait_ge(xg_done, q * (2 * PAIRS + 2))
                    dve.tensor_scalar(slotv[:, 0:2, 0:NE], slotv[:, 0:2, 0:NE], -float(CAP), None, ALU.add)
                    dve.tensor_scalar(slotv[0:64, 2, 0:NE], slotv[0:64, 2, 0:NE], -float(CAP), None, ALU.add)\
                       .then_inc(slots_moved, 1)
                    dve.wait_ge(slots_moved, q)
                    picks(0)
                    for par in range(2):
                        choose(par, par)
                    with dve.Fori(0, PAIRS) as i:
                        pair(q, i)

            dve.wait_ge(part_added, passes * (6 * PAIRS))
            for step in (0, 1, (0,), 2, (1,), (2,)):
                tt = step[0] if isinstance(step, tuple) else step
                r = slice(0, ROWS[tt])
                if step == tt:
                    for c in range(2):
                        ins = dve.bn_stats(stats[r, tt, c, :], yacc[r, tt, HALF * c:HALF * c + HALF])
                    link(ins)
                    moments(tt, 2, 7 + tt)
                else:
                    inverse(tt, 7 + tt)
                    norm_half(link, yacc, tt, 0, lnb[:, 2, :], lnb[:, 3, :])
                    norm_half(link, yacc, tt, 1, lnb[:, 2, :], lnb[:, 3, :]).then_inc(y_normal, 1)

        @block.tensor
        def _(pe):
            def opens(*key):
                if TILES[key] >= 8:
                    pe.wait_ge(bank_free[TILES[key] % 8], TILES[key] // 8)
                return bank(*key)

            def contract(out, pairs):
                last = len(pairs) - 1
                for k, (lhsT, rhs) in enumerate(pairs):
                    ins = pe.matmul(out, lhsT, rhs, start=(k == 0), stop=(k == last))
                return ins

            def to_channels(kind, c, w, cc, rhs, nk=KD):
                out = opens(kind, c)
                return contract(out[:, 0:T], [(w[:, k, P * cc:P * cc + P], rhs[:, k, :]) for k in range(nk)])

            def to_tokens(kind, srcT):
                def w(s):
                    pe.wait_ge(*loaded(kind, s))
                    return slot(kind, s).rearrange("p (k n) -> p k n", k=KD)

                for s, tt in TOKEN_ORDER:
                    out = opens(kind, s, tt)
                    if tt < 2:
                        ws = w(s)
                        ins = contract(out[:, 0:256], [(srcT[:, k, P * tt:P * tt + P], ws[:, k, :])
                                                       for k in range(KD)])
                    else:
                        both = w(s), w(s + 1)
                        for k in range(KD):
                            for j in range(2):
                                ins = pe.matmul(out[64 * j:64 * j + 64, 0:256], srcT[:, k, SEQ:T], both[j][:, k, :],
                                                start=(k == 0), stop=(k == KD - 1))
                    ins.then_inc(*fills(kind, s, tt))

            pe.wait_ge(consts, 10)
            pe.wait_ge(x_in, 48)
            for k in range(KD):
                out = opens("xT", k)
                for tt in range(3):
                    ins = pe.transpose(out[:, P * tt:P * tt + ROWS[tt]], x[0:ROWS[tt], tt, P * k:P * k + P],
                                       ident[0:ROWS[tt], 0:ROWS[tt]])
                ins.then_inc(*fills("xT", k))
            for k in range(KD):
                pe.wait_ge(*copied("xT", k))
            pe.wait_ge(bias_in, 32)
            pe.transpose(opens("bias", 0)[:, 0:52], brow[:, :], ident[0:52, 0:52]).then_inc(*fills("bias", 0))
            to_tokens("v", xT)
            for c in range(KD):
                pe.wait_ge(*loaded("u", c // 2))
                to_channels("u", c, slot("u", c // 2).rearrange("p (k n) -> p k n", k=KD), c % 2, xT)\
                    .then_inc(*fills("u", c))

            pe.wait_ge(ws_in, 16)
            for i in range(2):
                out = opens("ws", i)
                for g in range(4):
                    ins = pe.transpose(out[:, P * g:P * g + P], wsr[:, 4 * i + g, :], ident[:, :])
                ins.then_inc(*fills("ws", i))
            pe.wait_ge(wsT_ready, 1)
            pe.matmul(opens("bd", 0)[0:64, :], rep8[:, :, :].rearrange("s b t -> s (b t)"),
                      wsT[0:LS, :, 0:LS].unsqueeze(2).broadcast_to([LS, GA, NB, LS]), start=True, stop=True)\
              .then_inc(*fills("bd", 0))
            pe.wait_ge(v_norm, 3)
            pe.wait_ge(*copied("bd", 0))
            for g in range(GA):
                out = opens("mix", g)
                for j in range(2):
                    pe.matmul(out[:, P * j:P * j + P], vn[:, j, P * g:P * g + P], wsT[:, g, :], start=True, stop=True)
                pe.matmul(out[:, SEQ:T], vn[0:64, 2, P * g:P * g + P], bd[:, g, :], start=True, stop=True)\
                  .then_inc(*fills("mix", g))

            pe.wait_ge(*loaded("mem", 0))
            memr = slot("mem", 0).rearrange("p (m d) -> p m d", m=2)
            for i in range(4):
                out = opens("mem", i)
                for k in (2 * i, 2 * i + 1):
                    for m in range(2):
                        c = MEM * (k % 2) + P * m
                        ins = pe.transpose(out[:, c:c + P], memr[:, m, P * k:P * k + P], ident[:, :])
                ins.then_inc(*fills("mem", i))
            for i in range(4):
                pe.wait_ge(*copied("mem", i))
            for i in range(2):
                w = slot("mk", i).rearrange("p (k n) -> p k n", k=KD)
                pe.wait_ge(*loaded("mk", i))
                out = opens("mk", i)
                for hh in range(2):
                    ins = contract(out[:, MEM * hh:MEM * hh + MEM],
                                   [(w[:, k, P * hh:P * hh + P], memT[:, k, :]) for k in range(KD)])
                ins.then_inc(*fills("mk", i))
            for i in range(2):
                w = slot("mv", i).rearrange("p (k n) -> p k n", k=KD)
                pe.wait_ge(*loaded("mv", i))
                out = opens("mv", i)
                for m in range(2):
                    ins = contract(out[:, 256 * m:256 * m + 256],
                                   [(memT[:, k, P * m:P * m + P], w[:, k, :]) for k in range(KD)])
                ins.then_inc(*fills("mv", i))
            for i in range(2):
                pe.wait_ge(*copied("mk", i))
            for m in range(2):
                out = opens("mkp", m)
                for h in range(HEADS):
                    ins = pe.transpose(out[:, P * h:P * h + P], mkT[:, h, P * m:P * m + P], ident[:, :])
                ins.then_inc(*fills("mkp", m))

            for h in range(HEADS):
                pe.wait_ge(*loaded("q", h // 2))
                to_channels("q", h, slot("q", h // 2).rearrange("p (k n) -> p k n", k=KD), h % 2, xT)\
                    .then_inc(*fills("q", h))
            for h in range(HEADS):
                pe.wait_ge(*copied("q", h))
                out = opens("sc", h)
                for lt in range(2):
                    ins = pe.matmul(out[:, MEM * lt:MEM * lt + MEM], qT[:, h, P * lt:P * lt + P], mkT[:, h, :],
                                    start=True, stop=True)
                ins.then_inc(*fills("sc", h))

            def cache(kind, b):
                return slot(kind, b // 2).rearrange("p (c n) -> p c n", c=4)[:, 2 * (b % 2):2 * (b % 2) + 2, :]

            for hp in range(2):
                for b in range(NB):
                    pe.wait_ge(*loaded("kc", b // 2))
                    out = opens("kt", hp, b)
                    for hh in range(2):
                        for m in range(2):
                            c, h = MEM * hh + P * m, 2 * hp + hh
                            ins = pe.transpose(out[:, c:c + P], cache("kc", b)[:, m, P * h:P * h + P], ident[:, :])
                    ins.then_inc(*fills("kt", hp, b))
                for b in range(NB):
                    pe.wait_ge(*copied("kt", hp, b))
                pe.wait_ge(qmask_ready, hp + 1)
                out = opens("ss", hp)
                for b in range(NB):
                    for hh in range(2):
                        ins = pe.matmul(out[64 * hh:64 * hh + 64, 0:MEM], qmask[:, hh, 64 * b:64 * b + 64],
                                        kTs[:, b, hh, :], start=(b == 0), stop=(b == NB - 1))
                ins.then_inc(*fills("ss", hp))

            for kind, h in (("pt", 0), ("pt", 1), ("o", 0), ("pt", 2), ("o", 1), ("pt", 3), ("o", 2), ("o", 3)):
                out = opens(kind, h)
                if kind == "pt":
                    pe.wait_ge(sm_done, h + 1)
                    for m in range(2):
                        for lt in range(2):
                            c = SEQ * m + P * lt
                            ins = pe.transpose(out[:, c:c + P], Pp[:, h, lt, P * m:P * m + P], ident[:, :])
                    ins.then_inc(*fills("pt", h))
                else:
                    pe.wait_ge(*copied("pt", h))
                    for m in range(2):
                        pe.wait_ge(*copied("mv", m))
                    contract(out[:, 0:SEQ], [(mvp[:, m, P * h:P * h + P], PT[:, h % 2, m, :]) for m in range(2)])\
                        .then_inc(*fills("o", h))
            for hp in range(2):
                pe.wait_ge(sm_done, HEADS + hp + 1)
                out = opens("pst", hp)
                for m in range(2):
                    ins = pe.transpose(out[:, P * m:P * m + P], Ps[:, hp, P * m:P * m + P], ident[:, :])
                ins.then_inc(*fills("pst", hp))
            for hp in range(2):
                pe.wait_ge(*copied("pst", hp))
            for i in range(2):
                out = opens("sv", i)
                for m in range(2):
                    for j in range(4):
                        b = 4 * i + j
                        pe.wait_ge(*loaded("vc", b // 2))
                        ins = pe.matmul(out[32 * j:32 * j + 32, :], PTs[:, m, b, :, :].rearrange("p h t -> p (h t)"),
                                        cache("vc", b)[:, m, :], start=(m == 0), stop=(m == 1))
                ins.then_inc(*fills("sv", i))

            pe.wait_ge(hist_in, 16)
            out = opens("hist", 0)
            for g in range(PG):
                ins = pe.transpose(out[:, NB * HIST * g:NB * HIST * (g + 1)], histr[:, P * g:P * g + P],
                                   ident[0:NB * HIST, 0:NB * HIST])
            ins.then_inc(*fills("hist", 0))
            for i in range(2):
                pe.wait_ge(*copied("sv", i))
                out = opens("so", i)
                for h in range(HEADS):
                    ins = pe.transpose(out[:, P * h:P * h + P], sov[:, i, P * h:P * h + P], ident[:, :])
                ins.then_inc(*fills("so", i))
            for g in range(PG):
                pe.wait_ge(*loaded("p", g // 2))
                to_channels("p", g, slot("p", g // 2).rearrange("p (k n) -> p k n", k=KD), g % 2, xT)\
                    .then_inc(*fills("p", g))
            for g in range(PG):
                pe.wait_ge(*copied("p", g))
            out = opens("pout", 0)
            for g in range(PG):
                ins = pe.transpose(out[:, P * g:P * g + P], pcur[:, g, T - P:T], ident[:, :])
            ins.then_inc(*fills("pout", 0))

            pe.wait_ge(a_ready, GA)
            for i in range(4):
                for kind, rhs in (("gA", xT), ("wa", uT)):
                    pe.wait_ge(*loaded(kind, i))
                    w = slot(kind, i).rearrange("p (k n) -> p k n", k=KD)
                    for c in (2 * i, 2 * i + 1):
                        to_channels(kind, c, w, c % 2, rhs).then_inc(*fills(kind, c))
            pe.wait_ge(const_in, 64)
            for g in range(PG):
                pe.wait_ge(d_ready, g + 1)
                pe.matmul(opens("yb", g)[:, 0:T], wpool[:, g, :], dT[:, g, :], start=True, stop=True)\
                  .then_inc(*fills("yb", g))
            for g in range(PG):
                pe.wait_ge(*copied("yb", g))
            for h in range(HEADS):
                pe.wait_ge(*copied("o", h))
            for i in range(2):
                pe.wait_ge(*copied("so", i))
            for gk, wk, rhs in (("gB", "wb", ybT), ("gM", "wm", oT)):
                for i in range(2):
                    for c in range(4 * i, 4 * i + 4):
                        pe.wait_ge(*loaded(gk, c // 2))
                        to_channels(gk, c, slot(gk, c // 2).rearrange("p (k n) -> p k n", k=KD), c % 2, xT)\
                            .then_inc(*fills(gk, c))
                    pe.wait_ge(*loaded(wk, i))
                    for c in range(4 * i, 4 * i + 4):
                        to_channels(wk, c, slot(wk, i).rearrange("p (k n) -> p k n", k=4), c % 4, rhs, 4)\
                            .then_inc(*fills(wk, c))
            pe.wait_ge(h_added, 2 * KD)
            to_tokens("wo", hT)

            for key in [key for key in TILES if key[0] in ("x1T", "rt")]:
                tt = key[1]
                m, nth = ROWS[tt], TILE_ORDER.index(tt) + 1
                out = opens(*key)
                if key[0] == "x1T":
                    pe.wait_ge((x1_left, x1_right)[key[2]], nth)
                    for k in range(4):
                        c = 512 * key[2] + P * k
                        ins = pe.transpose(out[:, m * k:m * k + m], x[0:m, tt, c:c + P], ident[0:m, 0:m])
                else:
                    for h in range(2):
                        pe.wait_ge(*copied("x1T", tt, h))
                    ins = contract(out[0:m, 0:NE], [(x1T[:, k, P * tt:P * tt + m], wr[:, k, :]) for k in range(KD)])
                ins.then_inc(*fills(*key))
            pe.wait_ge(mask_ready, 1)
            out = opens("rank", 0)
            for tt in range(4):
                m = ROWS[tt] if tt < 3 else P
                pairs = [(ones[0:ROWS[j], 0:m], mask[0:ROWS[j], j, :]) for j in range(tt)]
                if tt < 3:
                    pairs.append((upper[0:m, 0:m], mask[0:m, tt, :]))
                ins = contract(out[0:m, NE * tt:NE * tt + NE], pairs)
            ins.then_inc(*fills("rank", 0))
            for key, n in TILES.items():
                if n >= len(TILES) - 8:
                    pe.wait_ge(*copied(*key))

            def gather(g, h):
                pe.wait_ge(pick_ready, g + 1)
                for k in range(4):
                    c = 512 * h + P * k
                    ins = contract(ps[:, XG + h, P * k:P * k + P],
                                   [(x[0:ROWS[tt], tt, c:c + P],
                                     pick[0:ROWS[tt], tt, :, :].rearrange("p e s -> p (e s)")) for tt in range(3)])
                ins.then_inc(xg_done, 1)

            def pair(q, i):
                n = q * PAIRS + i
                g = q * (PAIRS + 1) + i
                for par in range(2):
                    e = 2 * n + par
                    if par == 0:
                        pe.wait_ge(xg_ready, 2 * g + 2)
                    pe.wait_ge(sel_ready, 2 * g + par + 1)
                    parts = [(GB, 0), (GB, 1), (LB, 0), (LB, 1)]
                    for p, (b, hh) in enumerate(parts):
                        pe.matmul(ps[CAP * hh:CAP * hh + CAP, b, :], sel[:, par, :], b1s[:, 512 * p:512 * p + 512],
                                  start=True, stop=False)
                    for k in range(KD):
                        s = NH + k
                        if k == KD // 2:
                            if par == 1:
                                pe.wait_ge(y_ready, e)
                            for dh in range(2):
                                pe.matmul(ps[CAP * dh:CAP * dh + CAP, YB, :], sel[:, par, :],
                                          b2s[:, 512 * dh:512 * dh + 512], start=True, stop=False)
                        pe.wait_ge(slot_full[s % RING], 16 * (e + s // RING + 1))
                        for p, (b, hh) in enumerate(parts):
                            ins = pe.matmul(ps[CAP * hh:CAP * hh + CAP, b, :], xg[:, k, par, :],
                                            ring[:, s % RING, 512 * p:512 * p + 512], start=False, stop=(k == KD - 1))
                        ins.then_inc(slot_free if k < KD - 1 else up_done, 1)
                    gather(g + 1, par)
                    pe.wait_ge(act_ready, e + 1)
                    for c in range(4):
                        ins = pe.transpose(ps[:, AT, P * c:P * c + P], act_s[:, P * c:P * c + P], ident[:, :])
                    ins.then_inc(act_turned, 1)
                    if par == 1:
                        pe.wait_ge(pickg_ready, n + 1)
                        for tt in range(3):
                            ins = pe.transpose(ps[:, ST, P * tt:P * tt + ROWS[tt]],
                                               pickg[0:ROWS[tt], tt, :, :].rearrange("p e s -> p (e s)"),
                                               ident[0:ROWS[tt], 0:ROWS[tt]])
                        ins.then_inc(pickT_turned, 1)
                    pe.wait_ge(actT_ready, e + 1)
                    for j in range(KD, RING):
                        s = NH + j
                        w = ring[:, s % RING, :].rearrange("p (k n) -> p k n", k=2)
                        pe.wait_ge(slot_full[s % RING], 16 * (e + s // RING + 1))
                        for kk in range(2):
                            f = 2 * (j - KD) + kk
                            for dh in range(2):
                                ins = pe.matmul(ps[CAP * dh:CAP * dh + CAP, YB, :], actT[:, f % 4, f // 4, :],
                                                w[:, kk, 512 * dh:512 * dh + 512], start=False, stop=(f == KD - 1))
                        ins.then_inc(slot_free if j < RING - 1 else y_done, 1)
                pe.wait_ge(pickT_ready, n + 1)
                pe.wait_ge(y_ready, 2 * n + 2)
                for t in range(6):
                    tt, dh = t // 2, t % 2
                    if t >= 2:
                        pe.wait_ge(part_added, 6 * n + t - 1)
                    pe.matmul(ps[0:ROWS[tt], O0 + t % 2, :], pickT[:, P * tt:P * tt + ROWS[tt]],
                              ypair[:, 512 * dh:512 * dh + 512], start=True, stop=True).then_inc(part_done, 1)

            for h in range(2):
                gather(0, h)
            pe.wait_ge(ebias_ready, 1)
            with pe.Fori(0, PAIRS) as i:
                pair(0, i)
            pe.wait_ge(npass_ready, 1)
            passes = pe.value_load(npass[0:1, 0:1], min_val=1, max_val=PASSES)
            with pe.If(passes > 1):
                with pe.Fori(1, passes) as q:
                    for h in range(2):
                        gather(q * (PAIRS + 1), h)
                    with pe.Fori(0, PAIRS) as i:
                        pair(q, i)


_INS = ['x_prompt', 'x_sample', 'state_pool', 'cache_mem_k', 'cache_mem_v', 'mem_prompt', 'w_in', 'b_in', 'ln_v_g',
        'ln_v_b', 'w_s', 'b_s', 'w_a_out', 'w_pool', 'ls_pool', 'w_b_out', 'w_mk', 'w_mv', 'w_m_out', 'w_o', 'ln1_g',
        'ln1_b', 'w_r', 'b_r', 'w1', 'b1', 'w2', 'b2', 'ln2_g', 'ln2_b']
_OUTS = [('y_p', (SEQ, D), (1, SEQ, D)), ('y_s', (NB * LS, D), (NB, LS, D)),
         ('pool_p', (HIST, 512), (1, 1, HIST, 512)), ('pool_s', (NB, HIST, 512), (1, NB, HIST, 512)),
         ('mk', (MEM, 512), (1, 1, MEM, HEADS, P)), ('mv', (MEM, 512), (1, 1, MEM, HEADS, P)),
         ('cv', (NB * LS, D), (1, NB, LS, D))]


def kernel(**inputs):
    import numpy as _np
    import concourse.bacc as _bacc
    from concourse import mybir as _mybir
    from concourse.bass_utils import run_bass_kernel_spmd as _run

    nc = _bacc.Bacc("TRN2", target_bir_lowering=False, num_devices=1)
    arrays, ins, outs = {}, {}, {}
    for name in _INS:
        v = _np.ascontiguousarray(inputs[name])
        v = v.reshape(-1, D) if name == 'x_sample' else v.reshape(v.shape[1:])
        arrays[f"in_{name}"] = v
        ins[name] = nc.dram_tensor(f"in_{name}", v.shape, _mybir.dt.from_np(v.dtype), kind="ExternalInput").ap()
    for name, shape, _ in _OUTS:
        outs[name] = nc.dram_tensor(f"out_{name}", shape, F32, kind="ExternalOutput").ap()
    build(nc, ins, outs)
    r = _run(nc, [arrays], core_ids=[0])
    return tuple(_np.asarray(r.results[0][f"out_{name}"]).reshape(shape) for name, _, shape in _OUTS)
```

```python
from contextlib import ExitStack

import concourse.bass as bass
from concourse import mybir

F32 = mybir.dt.float32
F32R = mybir.dt.float32r
BF16 = mybir.dt.bfloat16
I32 = mybir.dt.int32
ALU = mybir.AluOpType
ACT = mybir.ActivationFunctionType
AX = mybir.AxisListType

P = 128
D = 1024
KD = D // P
SEQ, NB, LS = 256, 8, 8
T = SEQ + NB * LS
ROWS = [128, 128, 64]
GA = 8
HEADS, MEM = 4, 256
PG, HIST = 4, 15
WINDOWS = [2, 4, 8, 16]
NE, TOPK = 32, 4
CAP = 64
PASSES = T // CAP
SCALE = float(P) ** -0.5
EPS = 1e-5
ALPHA = 2.0 ** 0.25
SW_LIMIT, SW_ALPHA = 7.0, 1.702

SLOT = 2048
RING = 12
HR = 6
SEG = HIST + LS
EXT = HIST + SEQ + NB * SEG


TOKEN_ORDER = [x for s in (0, 2) for x in ((s, 0), (s, 1), (s, 2), (s + 1, 0), (s + 1, 1))]
TILE_ORDER = (2, 0, 1)


def head_slots():
    s = [("v", i) for i in range(4)] + [("u", i) for i in range(4)] + [("mem", 0)]
    s += [(w, i) for w in ("mk", "mv", "q", "p") for i in range(2)]
    s += [(w, i) for w in ("kc", "vc") for i in range(4)]
    for i in range(4):
        s += [("gA", i), ("wa", i)]
    for g, w in (("gB", "wb"), ("gM", "wm")):
        for i in range(2):
            s += [(g, 2 * i), (g, 2 * i + 1), (w, i)]
    return s + [("wo", i) for i in range(4)]


def head_tiles():
    t = [("xT", k) for k in range(KD)] + [("bias", 0)]
    t += [("v", c) for c in range(KD)] + [("u", 0)] + [("vt", tt, h) for tt in TILE_ORDER for h in range(2)]
    t += [("u", c) for c in range(1, KD)]
    t += [("ws", 0), ("ws", 1)] + [("mem", i) for i in range(4)] + [("bd", 0)] + [("mix", g) for g in range(GA)]
    t += [(w, i) for w in ("mk", "mv", "mkp") for i in range(2)]
    t += [(w, c) for w in ("q", "p", "sc") for c in range(HEADS)]
    for hp in range(2):
        t += [("kt", hp, b) for b in range(NB)] + [("ss", hp)]
    t += [("pt", 0), ("pt", 1), ("o", 0), ("pt", 2), ("o", 1), ("pt", 3), ("o", 2), ("o", 3)]
    t += [("pst", 0), ("pst", 1), ("sv", 0), ("sv", 1), ("hist", 0), ("so", 0), ("so", 1), ("pout", 0)]
    for i in range(4):
        t += [("gA", 2 * i), ("gA", 2 * i + 1), ("wa", 2 * i), ("wa", 2 * i + 1)]
    t += [("yb", g) for g in range(PG)]
    for g, w in (("gB", "wb"), ("gM", "wm")):
        for i in range(2):
            t += [(g, 4 * i + c) for c in range(4)] + [(w, 4 * i + c) for c in range(4)]
    t += [("wo",) + x for x in TOKEN_ORDER]
    t += [("x1T", 2, 0), ("x1T", 2, 1), ("x1T", 0, 0), ("rt", 2), ("x1T", 0, 1)]
    return t + [("x1T", 1, 0), ("x1T", 1, 1), ("rt", 0), ("rt", 1), ("rank", 0)]


SLOTS = {key: n for n, key in enumerate(head_slots())}
TILES = {key: n for n, key in enumerate(head_tiles())}
NH = len(SLOTS)
SPLITS = [key for key in SLOTS if key[0] not in ("mem", "kc", "vc")]
EXPERT_SLOTS = [(NH + j) % HR for j in range(HR)] + list(range(HR, RING))
HEAD_LOADS = [len(range(i, NH, HR)) if i < HR else 0 for i in range(RING)]


def build(nc, a, o):
    ctx = ExitStack()
    with ctx:
        def sem(name):
            return ctx.enter_context(nc.semaphore(name))

        top = [(nc.sbuf_base + 63) // 64 * 64]

        def region(nbytes):
            at = top[0]
            top[0] += (nbytes + 31) // 32 * 32
            assert top[0] <= nc.sbuf_usable_end
            return at

        def at(name, shape, off, dt=F32):
            return nc.alloc_sbuf_tensor_at(name, shape, dt, offset=off)

        def small(name, shape, dt=F32):
            n = 4
            for x in shape[1:]:
                n *= x
            return at(name, shape, region(n), dt)

        r0 = region(RING * SLOT * 4)
        ring = at("ring", [P, RING, SLOT], r0)
        ring_lo = at("ring_lo", [P, HR, SLOT], r0, F32R)
        rS = r0 + HR * SLOT * 4
        w_hi = at("w_hi", [P, 2, SLOT], rS, F32R)
        xT_lo = at("xT_lo", [P, KD, T], rS + 16384, F32R)
        vT = at("vT", [P, KD, T], rS + 26624)
        aT_hi = at("aT_hi", [P, KD, T], rS + 26624, F32R)
        hT_hi = at("hT_hi", [P, KD, T], rS + 26624, F32R)
        memT_lo = at("memT_lo", [P, KD, MEM], rS + 36864, F32R)
        oT_lo = at("oT_lo", [P, HEADS, T], rS + 36864, F32R)
        pcur = at("pcur", [P, PG, T], rS + 41984)
        x = small("x", [P, 3, D])
        rC = region(12288)
        vn = at("vn", [P, 3, D], rC)
        mkT = at("mkT", [P, HEADS, MEM], rC)
        mvp = at("mvp", [P, 2, HEADS * P], rC + 4096)
        mkp = at("mkp", [P, 2, HEADS * P], rC + 8192)
        ybT_hi = at("ybT_hi", [P, PG, T], rC, F32R)
        dT = at("dT", [P, PG, T], rC + 5120)
        ybT_lo = at("ybT_lo", [P, PG, T], rC + 5120, F32R)
        yacc = at("yacc", [P, 3, D], rC)
        rD = region(10240)
        xT_hi = at("xT_hi", [P, KD, T], rD, F32R)
        x1T = at("x1T", [P, KD, T], rD)
        pick = at("pick", [P, 3, 2, CAP], rD)
        pickg = at("pickg", [P, 3, 2, CAP], rD + 1536)
        rE = region(23040)
        bvb = at("bvb", [P, 2, D], rE)
        memT_hi = at("memT_hi", [P, KD, MEM], rE + 12288, F32R)
        kTs = at("kTs", [P, NB, 2, MEM], rE)
        QSTEP = NB * LS + LS
        qmask = at("qmask", [P, 2, NB * QSTEP], rE + 16384)
        Ps = at("Ps", [P, 2, MEM], rE + 20992)
        ext = [at(f"ext{i}", [P, PG, EXT], rE + 7296 * i) for i in range(3)]
        lnb = at("lnb", [P, 4, D], rE)
        b2x = at("b2x", [3 * NE, D], rE + 16384)
        b2s = at("b2s", [3 * NE, D], rE + 20480, BF16)
        rF = region(10240)
        qT = at("qT", [P, HEADS, T], rF)
        oT_hi = at("oT_hi", [P, HEADS, T], rF + 5120, F32R)
        sov = at("sov", [P, 2, HEADS * P], rF)
        b1s = at("b1s", [3 * NE, 2 * D], rF, BF16)
        ypair = at("ypair", [P, D], rF + 4096)
        rG = region(8192)
        wsr = at("wsr", [P, GA, P], rG)
        Pp = at("Pp", [P, HEADS, 2, MEM], rG)
        pout = at("pout", [P, PG * P], rG)
        gm, sg, lin, gs = (at(n, [P, 512], rG + 2048 * i) for i, n in enumerate(("gm", "sg", "lin", "gs")))
        rH = region(10240)
        uT = at("uT", [P, KD, T], rH)
        aT_lo = at("aT_lo", [P, KD, T], rH, F32R)
        b1x = at("b1x", [3 * NE, 2 * D], rH)
        rJ = region(10240)
        wsT = at("wsT", [P, GA, P], rJ)
        bd = at("bd", [NB * LS, GA, NB * LS], rJ + 4096)
        bsb = at("bsb", [P, GA, P], rJ + 6144)
        histr = at("histr", [NB * HIST, PG * P], rJ)
        PTs = at("PTs", [P, 2, NB, HEADS, LS], rJ + 7680)
        hT = at("hT", [P, KD, T], rJ)
        hT_lo = at("hT_lo", [P, KD, T], rJ, F32R)
        xg = at("xg", [P, KD, 2, CAP], rJ)
        act_s = at("act_s", [P, 512], rJ + 4096)
        actT = at("actT", [P, 4, 2, CAP], rJ + 6144)
        pickT = at("pickT", [P, T], rJ + 8192)
        rK = region(8192)
        gbuf = at("gbuf", [P, 4, T], rK)
        PT = at("PT", [P, 2, 2, SEQ], rK)
        mtmp = at("mtmp", [P, 2, T], rK)
        spare = at("spare0", [P, SLOT], rK), at("spare1", [P, SLOT], rH)
        ident = small("ident", [P, P])
        upper_f, ones_f = at("upper_f", [P, P], rK), at("ones_f", [P, P], rK + 512)
        upper = small("upper", [P, P], BF16)
        ones = small("ones", [P, P], BF16)
        slotj = small("slotj", [P, CAP])
        slotj_i = at("slotj_i", [P, CAP], rJ, I32)
        bdmask = small("bdmask", [NB * LS, NB, LS])
        rep8 = small("rep8", [LS, NB, LS])
        selcol = small("selcol", [3 * NE, NE + 2])
        sel = small("sel", [3 * NE, 2, CAP], BF16)
        zeros32 = small("zeros32", [P, NE])
        pos_i = at("pos_i", [P, HIST + 1], rJ + 256, I32)
        pos_f = at("pos_f", [P, HIST + 1], rJ + 320)
        ratio = small("ratio", [P, PG, HIST + 1])
        thr = small("thr", [1, PASSES - 1])
        wpool = at("wpool", [P, PG, P], region(2048))
        brow = at("brow", [52, P], rK + 4096)
        bT = small("bT", [P, 52])
        wr = small("wr", [P, KD, NE])
        brb = small("brb", [P, NE])
        mx = small("mx", [P, 10])
        nmx = small("nmx", [P, 10])
        ssum = small("ssum", [P, 10])
        rsum = small("rsum", [P, 10])
        stats = small("stats", [P, 3, 4, 6])
        mv = small("mv", [P, 3, 2])
        rstd = small("rstd", [P, 3])
        shift = small("shift", [P, 3])
        lg = small("lg", [P, 3, NE])
        top8 = small("top8", [P, 3, 8])
        gt = at("gt", [P, 3, NE], rH + 8192)
        eq = at("eq", [P, 3, NE], rH + 8576)
        ceq = at("ceq", [P, 3, NE], rH + 8960)
        mask = small("mask", [P, 3, NE], BF16)
        nsel = small("nsel", [P, 3])
        ge = at("ge", [P, 3, NE], rH + 9344)
        gsum = small("gsum", [P, 3])
        gates = small("gates", [P, 3, NE])
        slotv = small("slotv", [P, 3, NE + 2])
        cmax = small("cmax", [1, 2])
        late = small("late", [1, PASSES - 1])
        npass = small("npass", [1, 1], I32)
        ps = ctx.enter_context(nc.psum_tensor("ps", [P, 8, 512], F32))

        slot_full = [sem(f"slot_full{i}") for i in range(RING)]
        spare_full = sem("spare_full0"), sem("spare_full1")
        slot_free = sem("slot_free")
        bank_full = [sem(f"bank_full{i}") for i in range(8)]
        bank_free = [sem(f"bank_free{i}") for i in range(8)]
        x_in, bias_in, vparam_in, const_in, ws_in, hist_in, ln_in, b1_in, b2_in = (sem(n) for n in (
            "x_in", "bias_in", "vparam_in", "const_in", "ws_in", "hist_in", "ln_in", "b1_in", "b2_in"))
        cv_out, mkv_out, pout_out, hist_out, y_out = (sem(n) for n in (
            "cv_out", "mkv_out", "pout_out", "hist_out", "y_out"))
        consts, ops_pool, ops_dve = sem("consts"), sem("ops_pool"), sem("ops_dve")
        w_high, w_low, x_high, mem_high, a_high, a_low, o_high, yb_high, h_high, h_low = (sem(n) for n in (
            "w_high", "w_low", "x_high", "mem_high", "a_high", "a_low", "o_high", "yb_high", "h_high", "h_low"))
        v_norm, wsT_ready, a_ready = (sem(n) for n in ("v_norm", "wsT_ready", "a_ready"))
        var_ready, std_ready, rstd_ready = sem("var_ready"), sem("std_ready"), sem("rstd_ready")
        sm_max, sm_done, qmask_ready, d_ready, h_added = (sem(n) for n in (
            "sm_max", "sm_done", "qmask_ready", "d_ready", "h_added"))
        x1_left, x1_right, y_left, y_right, right_normal = (sem(n) for n in (
            "x1_left", "x1_right", "y_left", "y_right", "right_normal"))
        lg_ready, ge_ready, mask_ready, ebias_ready, npass_ready = (sem(n) for n in (
            "lg_ready", "ge_ready", "mask_ready", "ebias_ready", "npass_ready"))
        slots_moved, pick_ready, sel_ready, pickg_ready, pickT_turned, pickT_ready = (sem(n) for n in (
            "slots_moved", "pick_ready", "sel_ready", "pickg_ready", "pickT_turned", "pickT_ready"))
        xg_done, xg_ready, up_done, gm_ready, lin_ready = (sem(n) for n in (
            "xg_done", "xg_ready", "up_done", "gm_ready", "lin_ready"))
        sg_ready, gs_ready, act_ready, act_turned, actT_ready = (sem(n) for n in (
            "sg_ready", "gs_ready", "act_ready", "act_turned", "actT_ready"))
        y_done, y_left_out, y_right_out, part_done, part_added, yacc_begun = (sem(n) for n in (
            "y_done", "y_left_out", "y_right_out", "part_done", "part_added", "yacc_begun"))

        def bank(*key):
            return ps[:, TILES[key] % 8, :]

        def full(*key):
            return bank_full[TILES[key] % 8], TILES[key] // 8 + 1

        def fills(*key):
            return bank_full[TILES[key] % 8], 1

        def frees(*key):
            return bank_free[TILES[key] % 8], 1

        def copied(*key):
            return bank_free[TILES[key] % 8], TILES[key] // 8 + 1

        def slot(*key):
            return ring[:, SLOTS[key] % HR, :]

        def loaded(*key):
            return slot_full[SLOTS[key] % HR], 16 * (SLOTS[key] // HR + 1)

        def parts(*key, k=KD):
            hi = w_hi[:, SPLITS.index(key) % 2, :]
            lo = ring_lo[:, SLOTS[key] % HR, :]
            return [v.rearrange("p (k n) -> p k n", k=k) for v in (hi, lo)]

        def last_use(kind, i):
            if kind == "wo":
                return (kind, i, 2) if i % 2 == 0 else (kind, i, 1)
            if kind in ("mk", "mv"):
                return kind, i
            return {"mem": ("mem", 3), "kc": ("kt", 1, 2 * i + 1), "vc": ("sv", i // 2), "wb": ("wb", 4 * i + 3),
                    "wm": ("wm", 4 * i + 3)}.get(kind, (kind, 2 * i + 1))

        def wcols(w, c0, k=KD, n=256):
            return w[:, c0:c0 + n].rearrange("(k p) n -> p k n", k=k)

        def rows(v):
            return v.unsqueeze(0).broadcast_to([P, v.shape[0]])

        OFF = {"u": 0, "v": D, "p": 2 * D, "q": 2 * D + 512, "gA": 3 * D, "gB": 4 * D, "gM": 5 * D}
        BIAS = {k: v // P for k, v in OFF.items()}
        LS_COL = 48

        def source(kind, i):
            if kind in OFF:
                return wcols(a["w_in"], OFF[kind] + 256 * i)
            if kind == "mem":
                return a["mem_prompt"].rearrange("(m p) d -> p m d", m=2)
            if kind in ("kc", "vc"):
                c = a["cache_mem_k" if kind == "kc" else "cache_mem_v"]
                return c[2 * i:2 * i + 2].rearrange("b (m p) h d -> p (b m) (h d)", m=2)
            if kind in ("wb", "wm"):
                return wcols(a["w_b_out" if kind == "wb" else "w_m_out"], 512 * i, 4, 512)
            w = {"mk": "w_mk", "mv": "w_mv", "wa": "w_a_out", "wo": "w_o"}[kind]
            return wcols(a[w], 256 * i)

        block = ctx.enter_context(nc.Block())

        def gate_used(n):
            return copied("wa", n) if n < KD else (h_added, n - KD + 1)

        GB, LB, XG, AT, YB, O0, ST = 0, 1, 2, 4, 5, 6, 7
        PAIRS = NE // 2

        HALF = D // 2

        def norm_half(link, buf, tt, side, g, b):
            r, c = slice(0, ROWS[tt]), slice(HALF * side, HALF * side + HALF)
            v = buf[r, tt, c]
            link(nc.vector.scalar_tensor_tensor(out=v, in0=v, scalar=mv[r, tt, 0:1], in1=g[r, c],
                                                op0=ALU.subtract, op1=ALU.mult))
            return nc.vector.scalar_tensor_tensor(out=v, in0=v, scalar=rstd[r, tt:tt + 1], in1=b[r, c],
                                                  op0=ALU.mult, op1=ALU.add)

        def turned(copy, tt, h):
            m = ROWS[tt]
            copy(x1T[:, 4 * h:4 * h + 4, P * tt:P * tt + m],
                 bank("x1T", tt, h)[:, 0:4 * m].rearrange("p (k t) -> p k t", k=4)).then_inc(*frees("x1T", tt, h))

        @block.sync
        def _(sp):
            slots = list(SLOTS)
            for m in range(2):
                sp.dma_start(x[:, m, :], a["x_prompt"][P * m:P * m + P, :]).then_inc(x_in, 16)
            sp.dma_start(x[0:64, 2, :], a["x_sample"]).then_inc(x_in, 16)
            for n, key in enumerate(slots):
                if n >= HR:
                    sp.wait_ge(*full(*last_use(*slots[n - HR])))
                src = source(*key)
                sp.dma_start(slot(*key).rearrange("p (k n) -> p k n", k=src.shape[1]), src)\
                    .then_inc(slot_full[n % HR], 16)

            def load(e, par, j):
                n = EXPERT_SLOTS[j]
                if j < KD:
                    src = a["w1"][e, j * P:(j + 1) * P, :].rearrange("e p n -> p (e n)")
                    dst = ring[:, n, :]
                else:
                    r0 = 2 * (j - KD) * P
                    src = a["w2"][e, r0:r0 + 2 * P, :].rearrange("e (k p) n -> p (e k) n", k=2)
                    dst = ring[:, n, :].rearrange("p (k n) -> p k n", k=2)
                full_sem = slot_full[n]
                if par and j >= RING - 2:
                    j -= RING - 2
                    dst, full_sem = spare[j][:, :].rearrange("p (k n) -> p k n", k=2), spare_full[j]
                sp.dma_start(dst, src).then_inc(full_sem, 16)

            def last_two(q, e, par):
                sp.wait_ge(y_done, q * NE + e - 1)
                for j in (RING - 2, RING - 1):
                    load(bass.ds(e, 1), par, j)

            def others(q, e, par):
                before = q * NE + e - 1
                for j in range(RING - 2):
                    if j == KD - 1:
                        sp.wait_ge(up_done, before + 1)
                    else:
                        sp.wait_ge(slot_free, before * (RING - 2) + (j if j < KD else j - 1) + 1)
                    load(bass.ds(e, 1), par, j)

            for j in range(RING):
                if j <= HR:
                    sp.wait_ge(*full(*last_use(*slots[min(NH - HR + j, NH - 1)])))
                load(slice(0, 1), 0, j)
            sp.wait_ge(ebias_ready, 1)
            for j in (RING - 2, RING - 1):
                load(slice(1, 2), 1, j)
            with sp.Fori(0, PAIRS - 2) as i:
                for par in (1, 0):
                    e = 2 * i + 2 - par
                    others(0, e, par)
                    last_two(0, (i + 1) * 2 + (1 - par), 1 - par)
            others(0, NE - 3, 1)
            last_two(0, NE - 2, 0)
            others(0, NE - 2, 0)
            others(0, NE - 1, 1)
            last_two(0, NE - 1, 1)
            sp.wait_ge(npass_ready, 1)
            passes = sp.value_load(npass[0:1, 0:1], min_val=1, max_val=PASSES)
            with sp.If(passes > 1):
                with sp.Fori(1, passes) as q:
                    with sp.Fori(1, PAIRS + 1) as i:
                        for par in range(2):
                            others(q, 2 * i - 2 + par, par)
                            last_two(q, 2 * i - 2 + par, par)
            for tt in range(3):
                sp.wait_ge(y_left, tt + 1)
                if tt < 2:
                    sp.wait_ge(y_right, tt + 1)
                dst = o["y_p"][P * tt:P * tt + P, :] if tt < 2 else o["y_s"]
                sp.dma_start(dst, yacc[0:ROWS[tt], tt, :]).then_inc(y_out, 16)
            sp.wait_ge(y_out, 48)

        @block.gpsimd
        def _(pool):
            n = [0]

            def link(ins):
                n[0] += 1
                ins.then_inc(ops_pool, 1)
                pool.wait_ge(ops_pool, n[0])

            def select(out, op, fill, base, pattern, mult):
                return pool.affine_select(out=out, in_=out, compare_op=op, fill=fill, base=base,
                                          pattern=pattern, channel_multiplier=mult)

            link(pool.memset(ident[:, :], 0.0))
            select(ident[:, :], ALU.not_equal, 1.0, 0, [[-1, P]], 1).then_inc(consts, 1)
            pool.memset(ones_f[:, :], 1.0).then_inc(consts, 1)
            link(pool.memset(upper_f[:, :], 1.0))
            select(upper_f[:, :], ALU.is_gt, 0.0, 0, [[1, P]], -1).then_inc(consts, 1)
            link(pool.memset(bdmask[:, :, :], 1.0))
            link(select(bdmask[:, :, :], ALU.is_ge, 0.0, 0, [[-LS, NB], [0, LS]], 1))
            select(bdmask[:, :, :], ALU.is_ge, 0.0, LS - 1, [[LS, NB], [0, LS]], -1).then_inc(consts, 1)
            link(pool.memset(rep8[:, :, :], 0.0))
            select(rep8[:, :, :], ALU.not_equal, 1.0, 0, [[0, NB], [-1, LS]], 1).then_inc(consts, 1)
            link(pool.memset(selcol[:, :], 0.0))
            for r in range(3):
                ins = select(selcol[:, 0:NE], ALU.not_equal, 1.0, -NE * r, [[-1, NE]], 1)
                if r < 2:
                    link(ins)
            ins.then_inc(consts, 1)
            pool.iota(slotj_i[:, :], [[1, CAP]], base=1, channel_multiplier=0).then_inc(consts, 1)
            pool.iota(pos_i[:, :], [[1, HIST + 1]], base=1, channel_multiplier=0).then_inc(consts, 1)
            for i in range(PASSES - 1):
                ins = pool.memset(thr[:, i:i + 1], float(CAP * (i + 1)))
            ins.then_inc(consts, 1)
            pool.memset(zeros32[:, :], 0.0).then_inc(consts, 1)

            pool.dma_start(o["pool_s"][:, 0:HIST - LS, :], a["state_pool"][:, LS:HIST, :]).then_inc(hist_out, 16)
            def lows(*keys):
                for key in keys:
                    pool.wait_ge(w_high, SPLITS.index(key) + 1)
                    pool.tensor_tensor(ring_lo[:, SLOTS[key] % HR, :], slot(*key),
                                       w_hi[:, SPLITS.index(key) % 2, :].bitcast(F32), ALU.subtract)\
                        .then_inc(w_low, 1)

            at_v, at_mk, at_mv, at_q, at_gate, at_b = (
                SPLITS.index((w, 0)) for w in ("v", "mk", "mv", "q", "gA", "gB"))
            lows(*SPLITS[at_v:at_mk])
            pool.wait_ge(*copied("ws", 0))
            pool.wait_ge(*copied("ws", 1))
            select(wsT[:, :, :], ALU.is_ge, 0.0, 0, [[0, GA], [1, P]], -1).then_inc(wsT_ready, 1)
            lows(*SPLITS[at_mk:at_mv])
            pool.wait_ge(v_norm, 3)
            pool.dma_start(o["cv"], vn[0:NB * LS, 2, :]).then_inc(cv_out, 16)
            pool.wait_ge(a_ready, GA)
            pool.dma_start(histr[:, :], a["state_pool"].rearrange("b t c -> (b t) c")).then_inc(hist_in, 16)
            lows(*SPLITS[at_mv:at_gate])
            for m in range(2):
                pool.wait_ge(*copied("mv", m))
            pool.dma_start(o["mv"].rearrange("(m p) c -> p m c", m=2), mvp[:, :, :]).then_inc(mkv_out, 16)
            for m in range(2):
                pool.wait_ge(*copied("mkp", m))
            pool.dma_start(o["mk"].rearrange("(m p) c -> p m c", m=2), mkp[:, :, :]).then_inc(mkv_out, 16)
            lows(*SPLITS[at_gate:at_gate + 2])
            pool.wait_ge(*copied("pout", 0))
            pool.dma_start(o["pool_p"], pout[49:64, :]).then_inc(pout_out, 16)
            pool.dma_start(o["pool_s"][:, HIST - LS:HIST, :], pout[64:P, :]).then_inc(pout_out, 16)
            lows(*SPLITS[at_gate + 2:at_b])
            pool.wait_ge(d_ready, PG)
            for i, w in enumerate(("ln1_g", "ln1_b", "ln2_g", "ln2_b")):
                pool.dma_start(lnb[:, i, :], rows(a[w])).then_inc(ln_in, 16)
            for r in range(3):
                pool.dma_start(b2x[r * NE:(r + 1) * NE, :], a["b2"]).then_inc(b2_in, 16)
            lows(*SPLITS[at_b:at_b + 2])
            pool.wait_ge(*full("yb", 0))
            for r in range(3):
                pool.dma_start(b1x[r * NE:(r + 1) * NE, :], a["b1"]).then_inc(b1_in, 16)
            lows(*SPLITS[at_b + 2:])

            def right_half(nth, buf, tt, g, b):
                r, c = slice(0, ROWS[tt]), slice(HALF, D)
                pool.wait_ge(right_normal, nth)
                link(pool.tensor_tensor(buf[r, tt, c], buf[r, tt, c], g[r, c], ALU.mult))
                return pool.tensor_tensor(buf[r, tt, c], buf[r, tt, c], b[r, c], ALU.add)

            for nth, tt in enumerate(TILE_ORDER):
                right_half(1 + nth, x, tt, lnb[:, 0, :], lnb[:, 1, :]).then_inc(x1_right, 1)
            for tt in range(2):
                right_half(4 + tt, yacc, tt, lnb[:, 2, :], lnb[:, 3, :]).then_inc(y_right, 1)
            pool.wait_ge(cv_out, 16)
            pool.wait_ge(mkv_out, 32)
            pool.wait_ge(pout_out, 32)
            pool.wait_ge(hist_out, 16)

        @block.scalar
        def _(act):
            act.dma_start(brow[0:48, :], a["b_in"].rearrange("(c p) -> c p", p=P)).then_inc(bias_in, 16)
            act.dma_start(brow[48:52, :], a["ls_pool"].rearrange("(c p) -> c p", p=P)).then_inc(bias_in, 16)
            for i, src in enumerate((a["ln_v_g"], a["ln_v_b"])):
                act.dma_start(bvb[:, i, :], rows(src))\
                    .then_inc(vparam_in, 16)
            act.dma_start(wsr[:, :, :], a["w_s"].rearrange("g t s -> t g s")).then_inc(ws_in, 16)
            act.dma_start(bsb[:, :, :].rearrange("p g t -> p (g t)"),
                          rows(a["b_s"].rearrange("g t -> (g t)"))).then_inc(const_in, 16)
            act.dma_start(wpool[:, :, :], a["w_pool"].rearrange("g c d -> c g d")).then_inc(const_in, 16)
            act.dma_start(wr[:, :, :], a["w_r"].rearrange("(k p) e -> p k e", k=KD)).then_inc(const_in, 16)
            act.dma_start(brb[:, :], rows(a["b_r"])).then_inc(const_in, 16)

            def high(*key):
                i = SPLITS.index(key)
                act.wait_ge(*loaded(*key))
                if i >= 2:
                    act.wait_ge(*full(*last_use(*SPLITS[i - 2])))
                act.copy(w_hi[:, i % 2, :], slot(*key)).then_inc(w_high, 1)

            def high_after(*key):
                high(*SPLITS[SPLITS.index(key) + 2])

            for k in range(KD):
                act.wait_ge(*full("xT", k))
                act.copy(xT_hi[:, k, :], bank("xT", k)[:, 0:T]).then_inc(x_high, 1)
            act.wait_ge(w_high, 1)
            high("v", 1)

            def root(nth, tt):
                r = slice(0, ROWS[tt])
                act.wait_ge(var_ready, nth)
                act.activation(rstd[r, tt:tt + 1], rstd[r, tt:tt + 1], ACT.Sqrt).then_inc(std_ready, 1)

            def normal_right(nth, buf, tt):
                r = slice(0, ROWS[tt])
                act.wait_ge(rstd_ready, nth)
                act.activation(buf[r, tt, HALF:D], buf[r, tt, HALF:D], ACT.Identity, bias=shift[r, tt:tt + 1],
                               scale=rstd[r, tt:tt + 1]).then_inc(right_normal, 1)

            act.wait_ge(*copied("bias", 0))
            for c in range(KD):
                act.wait_ge(*full("v", c))
                act.activation(vT[:, c, :], bank("v", c)[:, 0:T], ACT.Gelu_apprx_tanh,
                               bias=bT[:, BIAS["v"] + c:BIAS["v"] + c + 1]).then_inc(*frees("v", c))
                if c % 2:
                    high_after("v", c // 2)
            for c in range(KD):
                act.wait_ge(*full("u", c))
                act.activation(uT[:, c, :], bank("u", c)[:, 0:T], ACT.Gelu_apprx_tanh,
                               bias=bT[:, BIAS["u"] + c:BIAS["u"] + c + 1]).then_inc(*frees("u", c))
                if c % 2:
                    high_after("u", c // 2)
                if c == 1:
                    for nth, tt in enumerate(TILE_ORDER):
                        root(1 + nth, tt)
            for i in range(4):
                act.wait_ge(*full("mem", i))
                act.copy(memT_hi[:, 2 * i:2 * i + 2, :], bank("mem", i).rearrange("p (k m) -> p k m", k=2))\
                    .then_inc(mem_high, 1)
            for g in range(GA):
                act.wait_ge(a_ready, g + 1)
                act.copy(aT_hi[:, g, :], uT[:, g, :]).then_inc(a_high, 1)
            for i in range(2):
                act.wait_ge(*full("mk", i))
                act.copy(mkT[:, 2 * i:2 * i + 2, :], bank("mk", i).rearrange("p (h m) -> p h m", h=2))\
                    .then_inc(*frees("mk", i))
                high_after("mk", i)
            for i in range(2):
                high_after("mv", i)
            act.wait_ge(cv_out, 16)
            for i in range(2):
                act.wait_ge(*full("mkp", i))
                act.copy(mkp[:, i, :], bank("mkp", i)).then_inc(*frees("mkp", i))
            for h in range(HEADS):
                act.wait_ge(*full("q", h))
                act.activation(qT[:, h, :], bank("q", h)[:, 0:T], ACT.Identity,
                               bias=bT[:, BIAS["q"] + h:BIAS["q"] + h + 1]).then_inc(*frees("q", h))
                if h % 2:
                    high_after("q", h // 2)
            for g in range(PG):
                act.wait_ge(*full("p", g))
                act.activation(pcur[:, g, :], bank("p", g)[:, 0:T], ACT.Identity,
                               bias=bT[:, BIAS["p"] + g:BIAS["p"] + g + 1]).then_inc(*frees("p", g))
            for h in range(HEADS):
                act.wait_ge(sm_max, h + 1)
                for lt in range(2):
                    j = 2 * h + lt
                    ins = act.activation(Pp[:, h, lt, :], bank("sc", h)[:, lt * MEM:(lt + 1) * MEM], ACT.Exp,
                                         bias=nmx[:, j:j + 1], scale=SCALE, accum_out=ssum[:, j:j + 1])
                ins.then_inc(*frees("sc", h))
            for hp in range(2):
                for b in range(1, NB, 2):
                    act.wait_ge(*full("kt", hp, b))
                    act.copy(kTs[:, b, :, :], bank("kt", hp, b).rearrange("p (h m) -> p h m", h=2))\
                        .then_inc(*frees("kt", hp, b))
                act.wait_ge(sm_max, HEADS + hp + 1)
                act.activation(Ps[:, hp, :], bank("ss", hp)[:, 0:MEM], ACT.Exp, bias=nmx[:, 8 + hp:9 + hp],
                               scale=SCALE, accum_out=ssum[:, 8 + hp:9 + hp]).then_inc(*frees("ss", hp))
            for kind, h in (("pt", 0), ("pt", 1), ("o", 0), ("pt", 2), ("o", 1), ("pt", 3), ("o", 2), ("o", 3)):
                act.wait_ge(*full(kind, h))
                if kind == "pt":
                    act.copy(PT[:, h % 2, :, :], bank("pt", h).rearrange("p (m l) -> p m l", m=2))\
                        .then_inc(*frees("pt", h))
                else:
                    act.copy(oT_hi[:, h, 0:SEQ], bank("o", h)[:, 0:SEQ]).then_inc(o_high, 1)
            act.wait_ge(*full("sv", 0))
            act.copy(sov[:, 0, :], bank("sv", 0)).then_inc(*frees("sv", 0))
            for i in range(2):
                high_after("p", i)

            def gate(kind, c, n):
                act.wait_ge(*full(kind, c))
                if n >= 4:
                    act.wait_ge(*gate_used(n - 4))
                act.activation(gbuf[:, n % 4, :], bank(kind, c)[:, 0:T], ACT.Sigmoid,
                               bias=bT[:, BIAS[kind] + c:BIAS[kind] + c + 1]).then_inc(*frees(kind, c))

            for i in range(4):
                for c in (2 * i, 2 * i + 1):
                    gate("gA", c, c)
                high_after("gA", i)
                high_after("wa", i)
            for g in range(PG):
                act.wait_ge(*full("yb", g))
                act.activation(ybT_hi[:, g, :], bank("yb", g)[:, 0:T], ACT.Copy,
                               scale=bT[:, LS_COL + g:LS_COL + g + 1]).then_inc(yb_high, 1)
            for gk, wk, first in (("gB", "wb", KD), ("gM", "wm", 2 * KD)):
                for i in range(2):
                    for c in range(4 * i, 4 * i + 4):
                        gate(gk, c, first + c)
                        if c % 2:
                            high_after(gk, c // 2)
                    if wk == "wm":
                        for c in range(4 * i, 4 * i + 4):
                            act.wait_ge(h_added, KD + c + 1)
                            act.copy(hT_hi[:, c, :], hT[:, c, :]).then_inc(h_high, 1)
                    high_after(wk, i)
            for i in range(2):
                high_after("wo", i)
            for nth, tt in enumerate(TILE_ORDER):
                if tt == 1:
                    for h in range(2):
                        act.wait_ge(*full("x1T", 2, h))
                        turned(act.copy, 2, h)
                root(4 + nth, tt)
                normal_right(4 + nth, x, tt)
            for tt, h in ((0, 0), (0, 1), (1, 1)):
                act.wait_ge(*full("x1T", tt, h))
                turned(act.copy, tt, h)
            act.wait_ge(lg_ready, 1)
            act.activation(ge[:, :, :], ge[:, :, :], ACT.Exp).then_inc(ge_ready, 1)

            def gathered(g, h):
                act.wait_ge(xg_done, 2 * g + h + 1)
                act.copy(xg[:, 4 * h:4 * h + 4, :, :],
                         ps[:, XG + h, :].rearrange("p (k e c) -> p k e c", k=4, e=2)).then_inc(xg_ready, 1)

            def pair(q, i):
                for par in range(2):
                    e = (q * NE + 2 * i) + par
                    act.wait_ge(gm_ready, e + 1)
                    act.activation(sg[:, :], gm[:, :], ACT.Sigmoid, scale=SW_ALPHA).then_inc(sg_ready, 1)
                    if par == 1:
                        for h in range(2):
                            gathered(q * (PAIRS + 1) + i + 1, h)
                    act.wait_ge(act_turned, e + 1)
                    act.copy(actT[:, :, :, :], ps[:, AT, :].rearrange("p (c h s) -> p c h s", c=4, h=2))\
                        .then_inc(actT_ready, 1)
                    act.wait_ge(y_done, e + 1)
                    act.copy(ypair[CAP * par:CAP * par + CAP, 0:512], ps[0:CAP, YB, :]).then_inc(y_left_out, 1)

            for h in range(2):
                gathered(0, h)
            for nth, tt in enumerate(TILE_ORDER):
                r = slice(0, ROWS[tt])
                act.wait_ge(x1_left, nth + 1)
                act.wait_ge(x1_right, nth + 1)
                act.activation(yacc[r, tt, :], x[r, tt, :], ACT.Copy, scale=ALPHA).then_inc(yacc_begun, 1)
            with act.Fori(0, PAIRS) as i:
                pair(0, i)
            act.wait_ge(npass_ready, 1)
            passes = act.value_load(npass[0:1, 0:1], min_val=1, max_val=PASSES)
            with act.If(passes > 1):
                with act.Fori(1, passes) as q:
                    for h in range(2):
                        gathered(q * (PAIRS + 1), h)
                    with act.Fori(0, PAIRS) as i:
                        pair(q, i)
            root(7, 0)
            root(8, 1)
            normal_right(7, yacc, 0)
            root(9, 2)
            normal_right(8, yacc, 1)

        @block.vector
        def _(dve):
            n = [0]

            def link(ins):
                n[0] += 1
                ins.then_inc(ops_dve, 1)
                dve.wait_ge(ops_dve, n[0])

            def moments(tt, parts, nth):
                r = slice(0, ROWS[tt])
                link(dve.bn_aggr(mv[r, tt, :], stats[r, tt, 0:parts, :].rearrange("p c s -> p (c s)")))
                dve.tensor_scalar(rstd[r, tt:tt + 1], mv[r, tt, 1:2], EPS, None, ALU.add).then_inc(var_ready, 1)

            def inverse(tt, nth):
                r = slice(0, ROWS[tt])
                dve.wait_ge(std_ready, nth)
                link(dve.reciprocal(rstd[r, tt:tt + 1], rstd[r, tt:tt + 1]))
                dve.scalar_tensor_tensor(out=shift[r, tt:tt + 1], in0=mv[r, tt, 0:1], scalar=-1.0,
                                         in1=rstd[r, tt:tt + 1], op0=ALU.mult, op1=ALU.mult).then_inc(rstd_ready, 1)

            dve.wait_ge(*loaded("v", 0))
            dve.tensor_copy(w_hi[:, 0, :], slot("v", 0)).then_inc(w_high, 1)
            for k in range(KD):
                dve.wait_ge(*full("xT", k))
                dve.wait_ge(x_high, k + 1)
                dve.tensor_tensor(xT_lo[:, k, :], bank("xT", k)[:, 0:T], xT_hi[:, k, :].bitcast(F32), ALU.subtract)\
                   .then_inc(*frees("xT", k))
            dve.wait_ge(*full("bias", 0))
            dve.tensor_copy(bT[:, :], bank("bias", 0)[:, 0:52]).then_inc(*frees("bias", 0))
            dve.wait_ge(consts, 10)
            dve.tensor_copy(ones[:, :], ones_f[:, :])
            dve.tensor_copy(upper[:, :], upper_f[:, :])
            dve.tensor_copy(slotj[:, :], slotj_i[:, :])
            link(dve.tensor_copy(pos_f[:, :], pos_i[:, :]))
            for g, w in enumerate(WINDOWS):
                ins = dve.tensor_scalar(ratio[:, g, :], pos_f[:, :], float(w), None, ALU.min)
            link(ins)
            link(dve.reciprocal(ratio[:, :, :], ratio[:, :, :]))
            for g, w in enumerate(WINDOWS):
                dve.tensor_scalar(ratio[:, g, :], ratio[:, g, :], float(w), None, ALU.mult)
            dve.memset(slotv[:, :, :], -1.0)
            dve.memset(gates[:, :, :], 0.0)
            link(dve.memset(lg[:, :, :], 0.0))

            dve.wait_ge(vparam_in, 32)
            for nth, tt in enumerate(TILE_ORDER):
                r = slice(0, ROWS[tt])
                for h in range(2):
                    dve.wait_ge(*full("vt", tt, h))
                    dve.tensor_copy(vn[r, tt, HALF * h:HALF * h + HALF], bank("vt", tt, h)[r, :])\
                       .then_inc(*frees("vt", tt, h))
            for nth, tt in enumerate(TILE_ORDER):
                r = slice(0, ROWS[tt])
                for h in range(2):
                    dve.wait_ge(*copied("vt", tt, h))
                    ins = dve.bn_stats(stats[r, tt, h, :], vn[r, tt, HALF * h:HALF * h + HALF])
                link(ins)
                moments(tt, 2, 1 + nth)
            for nth, tt in enumerate(TILE_ORDER):
                inverse(tt, 1 + nth)
                norm_half(link, vn, tt, 0, bvb[:, 0, :], bvb[:, 1, :])
                norm_half(link, vn, tt, 1, bvb[:, 0, :], bvb[:, 1, :]).then_inc(v_norm, 1)

            for i in range(2):
                dve.wait_ge(*full("ws", i))
                dve.tensor_copy(wsT[:, 4 * i:4 * i + 4, :], bank("ws", i).rearrange("p (g t) -> p g t", g=4))\
                   .then_inc(*frees("ws", i))
            for i in range(4):
                dve.wait_ge(mem_high, i + 1)
                two = slice(2 * i, 2 * i + 2)
                dve.tensor_tensor(memT_lo[:, two, :], bank("mem", i).rearrange("p (k m) -> p k m", k=2),
                                  memT_hi[:, two, :].bitcast(F32), ALU.subtract).then_inc(*frees("mem", i))
            dve.wait_ge(*full("bd", 0))
            dve.tensor_tensor(bd[:, :, :], bank("bd", 0)[0:64, :].rearrange("p (g t) -> p g t", g=GA),
                              bdmask[:, :, :].rearrange("p b t -> p (b t)").unsqueeze(1)
                              .broadcast_to([NB * LS, GA, NB * LS]), ALU.mult).then_inc(*frees("bd", 0))
            dve.wait_ge(const_in, 64)

            def a_lower(g):
                dve.wait_ge(a_high, g + 1)
                dve.tensor_tensor(aT_lo[:, g, :], uT[:, g, :], aT_hi[:, g, :].bitcast(F32), ALU.subtract)\
                   .then_inc(a_low, 1)

            for g in range(GA):
                m, tmp = bank("mix", g), mtmp[:, g % 2, :]
                dve.wait_ge(*full("mix", g))
                if g >= 2:
                    dve.wait_ge(a_ready, g - 1)
                dve.tensor_tensor(tmp[:, 0:SEQ].rearrange("p (c t) -> p c t", c=2),
                                  m[:, 0:SEQ].rearrange("p (c t) -> p c t", c=2),
                                  bsb[:, g:g + 1, :].broadcast_to([P, 2, P]), ALU.add)
                dve.tensor_tensor(tmp[:, SEQ:T].rearrange("p (b t) -> p b t", b=NB),
                                  m[:, SEQ:T].rearrange("p (b t) -> p b t", b=NB),
                                  bsb[:, g:g + 1, 0:LS].broadcast_to([P, NB, LS]), ALU.add)\
                   .then_inc(*frees("mix", g))
                dve.wait_ge(*copied("mix", g))
                dve.wait_ge(*copied("u", g))
                dve.tensor_tensor(uT[:, g, :], uT[:, g, :], tmp, ALU.mult).then_inc(a_ready, 1)
                if g:
                    a_lower(g - 1)
            a_lower(GA - 1)

            for i in range(2):
                dve.wait_ge(*full("mv", i))
                dve.tensor_copy(mvp[:, :, 256 * i:256 * i + 256], bank("mv", i).rearrange("p (m n) -> p m n", m=2))\
                   .then_inc(*frees("mv", i))
            link(dve.memset(qmask[:, :, :], 0.0))

            def row_max(j, w, scores):
                link(dve.tensor_reduce(mx[:, j:j + w], scores, AX.X, ALU.max))
                dve.tensor_scalar(nmx[:, j:j + w], mx[:, j:j + w], -SCALE, None, ALU.mult).then_inc(sm_max, 1)

            def own_queries(hp):
                for hh in range(2):
                    dve.wait_ge(*copied("q", 2 * hp + hh))
                    ins = dve.tensor_copy(
                        qmask[:, hh, :].rearrange("p (b s) -> p b s", s=QSTEP)[:, :, 0:LS],
                        qT[:, 2 * hp + hh, SEQ:T].rearrange("p (b l) -> p b l", b=NB))
                ins.then_inc(qmask_ready, 1)

            def turned_keys(hp):
                for b in range(0, NB, 2):
                    dve.wait_ge(*full("kt", hp, b))
                    dve.tensor_copy(kTs[:, b, :, :], bank("kt", hp, b).rearrange("p (h m) -> p h m", h=2))\
                       .then_inc(*frees("kt", hp, b))

            def sample_max(hp):
                dve.wait_ge(*full("ss", hp))
                row_max(8 + hp, 1, bank("ss", hp)[:, 0:MEM])

            def o_lower(h):
                dve.wait_ge(o_high, h + 1)
                dve.tensor_tensor(oT_lo[:, h, 0:SEQ], bank("o", h)[:, 0:SEQ], oT_hi[:, h, 0:SEQ].bitcast(F32),
                                  ALU.subtract).then_inc(*frees("o", h))

            for h in range(HEADS):
                dve.wait_ge(*full("sc", h))
                row_max(2 * h, 2, bank("sc", h).rearrange("p (t m) -> p t m", t=2))
            own_queries(0)
            turned_keys(0)
            sample_max(0)
            own_queries(1)
            turned_keys(1)
            for h in range(HEADS):
                dve.wait_ge(*copied("sc", h))
                link(dve.reciprocal(rsum[:, 2 * h:2 * h + 2], ssum[:, 2 * h:2 * h + 2]))
                for lt in range(2):
                    ins = dve.tensor_scalar(Pp[:, h, lt, :], Pp[:, h, lt, :], rsum[:, 2 * h + lt:2 * h + lt + 1],
                                            None, ALU.mult)
                ins.then_inc(sm_done, 1)
            sample_max(1)
            for hp in range(2):
                dve.wait_ge(*copied("ss", hp))
                link(dve.reciprocal(rsum[:, 8 + hp:9 + hp], ssum[:, 8 + hp:9 + hp]))
                dve.tensor_scalar(Ps[:, hp, :], Ps[:, hp, :], rsum[:, 8 + hp:9 + hp], None, ALU.mult)\
                   .then_inc(sm_done, 1)
            for h in range(2):
                o_lower(h)
            for hp in range(2):
                dve.wait_ge(*full("pst", hp))
                for m in range(2):
                    ins = dve.tensor_copy(PTs[:, m, :, 2 * hp:2 * hp + 2, :].transpose([0, 2, 1, 3]),
                                          bank("pst", hp)[:, P * m:P * m + P]
                                          .rearrange("p (h b t) -> p h b t", h=2, b=NB))
                ins.then_inc(*frees("pst", hp))
            for h in (2, 3):
                o_lower(h)
            dve.wait_ge(*full("sv", 1))
            dve.tensor_copy(sov[:, 1, :], bank("sv", 1)).then_inc(*frees("sv", 1))

            e0, e1, e2 = ext

            def own(t, lo, hi):
                return t[:, :, HIST + SEQ:EXT].rearrange("p g (b s) -> p g b s", s=SEG)[:, :, :, lo:hi]

            dve.wait_ge(*full("hist", 0))
            dve.memset(e0[:, :, 0:HIST], 0.0)
            dve.tensor_copy(own(e0, 0, HIST),
                            bank("hist", 0)[:, 0:PG * NB * HIST].rearrange("p (g b t) -> p g b t", g=PG, b=NB))\
               .then_inc(*frees("hist", 0))
            for i in range(2):
                dve.wait_ge(*full("so", i))
                cols = slice(SEQ + 32 * i, SEQ + 32 * i + 32)

                def queries(h):
                    return bank("so", i)[:, P * h:P * h + P].rearrange("p (b c) -> p b c", b=4)\
                        [:, :, LS * h:LS * h + LS]

                for h in range(HEADS):
                    ins = dve.tensor_copy(oT_hi[:, h, cols].rearrange("p (b t) -> p b t", b=4), queries(h))
                link(ins)
                for h in range(HEADS):
                    ins = dve.tensor_tensor(oT_lo[:, h, cols].rearrange("p (b t) -> p b t", b=4), queries(h),
                                            oT_hi[:, h, cols].bitcast(F32).rearrange("p (b t) -> p b t", b=4),
                                            ALU.subtract)
                ins.then_inc(*frees("so", i))
            for g in range(PG):
                dve.wait_ge(*copied("p", g))
            dve.tensor_copy(e0[:, :, HIST:HIST + SEQ], pcur[:, :, 0:SEQ])
            link(dve.tensor_copy(own(e0, HIST, SEG), pcur[:, :, SEQ:T].rearrange("p g (b l) -> p g b l", b=NB)))
            dve.wait_ge(*full("pout", 0))
            dve.tensor_copy(pout[:, :], bank("pout", 0)).then_inc(*frees("pout", 0))
            sums = e0
            for step, out in enumerate((e1, e2, e1, e2)):
                w = 1 << step
                link(dve.tensor_tensor(out[:, step:PG, 2 * w - 1:EXT], sums[:, step:PG, 2 * w - 1:EXT],
                                       sums[:, step:PG, w - 1:EXT - w], ALU.add))
                sums = out
            for g in range(PG):
                s = (e1, e2)[g % 2][:, g, HIST:2 * HIST + 1]
                ins = dve.tensor_tensor(s, s, ratio[:, g, :], ALU.mult)
            link(ins)
            dve.wait_ge(mkv_out, 32)
            for g, w in enumerate(WINDOWS):
                s = (e1, e2)[g % 2]
                dve.scalar_tensor_tensor(out=dT[:, g, 0:SEQ], in0=s[:, g, HIST:HIST + SEQ], scalar=1.0 / w,
                                         in1=e0[:, g, HIST:HIST + SEQ], op0=ALU.mult, op1=ALU.subtract)
                dve.scalar_tensor_tensor(out=dT[:, g, SEQ:T].rearrange("p (b l) -> p b l", b=NB),
                                         in0=own(s, HIST, SEG)[:, g], scalar=1.0 / w,
                                         in1=own(e0, HIST, SEG)[:, g], op0=ALU.mult, op1=ALU.subtract)\
                   .then_inc(d_ready, 1)

            for c in range(KD):
                dve.wait_ge(*full("wa", c))
                dve.wait_ge(*copied("gA", c))
                dve.tensor_tensor(hT[:, c, :], bank("wa", c)[:, 0:T], gbuf[:, c % 4, :], ALU.mult)\
                   .then_inc(*frees("wa", c))
            for g in range(PG):
                dve.wait_ge(yb_high, g + 1)
                dve.scalar_tensor_tensor(out=ybT_lo[:, g, :], in0=bank("yb", g)[:, 0:T],
                                         scalar=bT[:, LS_COL + g:LS_COL + g + 1],
                                         in1=ybT_hi[:, g, :].bitcast(F32), op0=ALU.mult, op1=ALU.subtract)\
                   .then_inc(*frees("yb", g))

            def three_parts(three, b):
                for rest in (2 * NE, NE):
                    link(dve.tensor_copy(three[0:rest, :], b[0:rest, :]))
                    link(dve.tensor_tensor(b[0:rest, :], b[0:rest, :], three[0:rest, :], ALU.subtract))
                return dve.tensor_copy(three[:, :], b[:, :])

            def h_lower(c):
                dve.wait_ge(h_high, c + 1)
                dve.tensor_tensor(hT_lo[:, c, :], hT[:, c, :], hT_hi[:, c, :].bitcast(F32), ALU.subtract)\
                   .then_inc(h_low, 1)

            for g, w in (("gB", "wb"), ("gM", "wm")):
                if g == "gM":
                    dve.wait_ge(b2_in, 48)
                    three_parts(b2s, b2x)
                for c in range(KD):
                    dve.wait_ge(*full(w, c))
                    dve.wait_ge(*copied(g, c))
                    dve.tensor_tensor(gbuf[:, c % 4, :], bank(w, c)[:, 0:T], gbuf[:, c % 4, :], ALU.mult)\
                       .then_inc(*frees(w, c))
                    dve.wait_ge(*copied(w, c))
                    dve.tensor_tensor(hT[:, c, :], hT[:, c, :], gbuf[:, c % 4, :], ALU.add).then_inc(h_added, 1)
                    if g == "gM" and c:
                        h_lower(c - 1)
            h_lower(KD - 1)

            dve.wait_ge(ln_in, 64)
            for s, tt in TOKEN_ORDER:
                out = bank("wo", s, tt)
                r, n_slots = slice(0, ROWS[tt]), 2 if tt == 2 else 1
                dve.wait_ge(*full("wo", s, tt))
                cols = slice(256 * s, 256 * (s + n_slots))
                dve.scalar_tensor_tensor(out=x[r, tt, cols], in0=x[r, tt, cols], scalar=ALPHA,
                                         in1=out[r, 0:256 * n_slots], op0=ALU.mult, op1=ALU.add)\
                   .then_inc(*frees("wo", s, tt))
                if (s, tt) == (0, 0):
                    dve.wait_ge(b1_in, 48)
                    three_parts(b1s, b1x).then_inc(ebias_ready, 1)
                dve.wait_ge(*copied("wo", s, tt))
                for j in range(n_slots):
                    ins = dve.bn_stats(stats[r, tt, s + j, :], x[r, tt, 256 * (s + j):256 * (s + j + 1)])
                if s + n_slots == 4:
                    nth = TILE_ORDER.index(tt)
                    link(ins)
                    moments(tt, 4, 4 + nth)
                    inverse(tt, 4 + nth)
                    norm_half(link, x, tt, 0, lnb[:, 0, :], lnb[:, 1, :]).then_inc(x1_left, 1)

            for tt in TILE_ORDER:
                r = slice(0, ROWS[tt])
                if tt == 0:
                    dve.wait_ge(*full("x1T", 1, 0))
                    turned(dve.tensor_copy, 1, 0)
                dve.wait_ge(*full("rt", tt))
                dve.tensor_tensor(lg[r, tt, :], bank("rt", tt)[r, 0:NE], brb[r, :], ALU.add).then_inc(*frees("rt", tt))
                dve.wait_ge(*copied("rt", tt))
                ins = dve.max(out=top8[:, tt, :], in_=lg[:, tt, :])
            link(ins)
            fourth = top8[:, :, TOPK - 1:TOPK].broadcast_to([P, 3, NE])
            dve.tensor_tensor(ge[:, :, :], lg[:, :, :], top8[:, :, 0:1].broadcast_to([P, 3, NE]), ALU.subtract)\
               .then_inc(lg_ready, 1)
            dve.tensor_tensor(eq[:, :, :], lg[:, :, :], fourth, ALU.is_equal)
            link(dve.tensor_tensor(gt[:, :, :], lg[:, :, :], fourth, ALU.is_gt))
            link(dve.tensor_reduce(nsel[:, :], gt[:, :, :], AX.X, ALU.add))
            dve.tensor_scalar(nsel[:, :], nsel[:, :], -1.0, float(TOPK), ALU.mult, ALU.add)
            for tt in range(3):
                ins = dve.tensor_tensor_scan(ceq[:, tt, :], eq[:, tt, :], zeros32[:, :], 0.0, ALU.add, ALU.add)
            link(ins)
            link(dve.tensor_tensor(ceq[:, :, :], ceq[:, :, :], nsel[:, :].unsqueeze(2).broadcast_to([P, 3, NE]),
                                   ALU.is_le))
            link(dve.tensor_tensor(eq[:, :, :], eq[:, :, :], ceq[:, :, :], ALU.mult))
            dve.tensor_tensor(mask[:, :, :], gt[:, :, :], eq[:, :, :], ALU.add).then_inc(mask_ready, 1)
            dve.wait_ge(mask_ready, 1)
            dve.wait_ge(ge_ready, 1)
            link(dve.tensor_tensor(ge[:, :, :], ge[:, :, :], mask[:, :, :], ALU.mult))
            link(dve.tensor_reduce(gsum[:, :], ge[:, :, :], AX.X, ALU.add))
            link(dve.reciprocal(gsum[:, :], gsum[:, :]))
            dve.tensor_tensor(gates[:, :, 0:NE], ge[:, :, :], gsum[:, :].unsqueeze(2).broadcast_to([P, 3, NE]),
                              ALU.mult)
            rk = bank("rank", 0)[:, 0:4 * NE].rearrange("p (t e) -> p t e", t=4)
            dve.wait_ge(*full("rank", 0))
            dve.scalar_tensor_tensor(out=slotv[:, 0:2, 0:NE], in0=rk[:, 0:2, :], scalar=1.0, in1=mask[:, 0:2, :],
                                     op0=ALU.add, op1=ALU.mult)
            dve.scalar_tensor_tensor(out=slotv[0:64, 2, 0:NE], in0=rk[0:64, 2, :], scalar=1.0,
                                     in1=mask[0:64, 2, :], op0=ALU.add, op1=ALU.mult)
            dve.tensor_reduce(cmax[:, 0:1], rk[0:1, 3, :], AX.X, ALU.max).then_inc(*frees("rank", 0))
            dve.wait_ge(*copied("rank", 0))
            def picks(i):
                two = bass.ds(2 * i, 2)
                dve.tensor_tensor(pick[:, 0:2, :, :],
                                  slotj[:, :].unsqueeze(1).unsqueeze(1).broadcast_to([P, 2, 2, CAP]),
                                  slotv[:, 0:2, two].unsqueeze(3).broadcast_to([P, 2, 2, CAP]), ALU.is_equal)
                dve.tensor_tensor(pick[0:64, 2, :, :], slotj[0:64, :].unsqueeze(1).broadcast_to([64, 2, CAP]),
                                  slotv[0:64, 2, two].unsqueeze(2).broadcast_to([64, 2, CAP]), ALU.is_equal)\
                   .then_inc(pick_ready, 1)

            def choose(e, par):
                dve.tensor_copy(sel[:, par, :], selcol[:, bass.ds(e, 1)].broadcast_to([3 * NE, CAP]))\
                   .then_inc(sel_ready, 1)

            def right_output(e, par):
                row = CAP * par
                dve.wait_ge(y_done, e + 1)
                dve.tensor_copy(ypair[row:row + CAP, HALF:D], ps[CAP:2 * CAP, YB, :]).then_inc(y_right_out, 1)

            def pair(q, i):
                n = q * PAIRS + i
                dve.wait_ge(xg_done, 2 * (q * (PAIRS + 1) + i + 1))
                picks(i + 1)
                for par in range(2):
                    for tt in range(3):
                        r = slice(0, ROWS[tt])
                        ins = dve.tensor_scalar(pickg[r, tt, par, :], slotj[r, :],
                                                slotv[r, tt, bass.ds(2 * i + par, 1)],
                                                gates[r, tt, bass.ds(2 * i + par, 1)], ALU.is_equal, ALU.mult)
                ins.then_inc(pickg_ready, 1)
                for par in range(2):
                    e = 2 * n + par
                    dve.wait_ge(up_done, e + 1)
                    dve.tensor_scalar(gm[:, :], ps[:, GB, :], SW_LIMIT, None, ALU.min).then_inc(gm_ready, 1)
                    dve.tensor_scalar(lin[:, :], ps[:, LB, :], -SW_LIMIT, SW_LIMIT, ALU.max, ALU.min)\
                       .then_inc(lin_ready, 1)
                    dve.wait_ge(sg_ready, e + 1)
                    dve.tensor_tensor(gs[:, :], gm[:, :], sg[:, :], ALU.mult).then_inc(gs_ready, 1)
                    dve.wait_ge(gs_ready, e + 1)
                    dve.wait_ge(lin_ready, e + 1)
                    dve.scalar_tensor_tensor(out=act_s[:, :], in0=lin[:, :], scalar=1.0, in1=gs[:, :],
                                             op0=ALU.add, op1=ALU.mult).then_inc(act_ready, 1)
                    choose(2 * i + par + 2, par)
                    if par == 0:
                        right_output(e, 0)
                dve.wait_ge(pickT_turned, n + 1)
                dve.tensor_copy(pickT[:, :], ps[:, ST, 0:T]).then_inc(pickT_ready, 1)
                right_output(2 * n + 1, 1)
                for t in range(6):
                    tt, dh = t // 2, t % 2
                    y = yacc[0:ROWS[tt], tt, 512 * dh:512 * dh + 512]
                    dve.wait_ge(part_done, 6 * n + t + 1)
                    dve.tensor_tensor(y, ps[0:ROWS[tt], O0 + t % 2, :], y, ALU.add).then_inc(part_added, 1)

            dve.wait_ge(pout_out, 32)
            picks(0)
            for par in range(2):
                choose(par, par)
            link(dve.tensor_scalar(late[:, :], thr[:, :], cmax[:, 0:1], None, ALU.is_lt))
            link(dve.tensor_reduce(cmax[:, 1:2], late[:, :], AX.X, ALU.add))
            dve.tensor_scalar(npass[:, :], cmax[:, 1:2], 1.0, None, ALU.add).then_inc(npass_ready, 1)
            dve.wait_ge(npass_ready, 1)
            dve.wait_ge(yacc_begun, 3)
            with dve.Fori(0, PAIRS) as i:
                pair(0, i)
            passes = dve.value_load(npass[0:1, 0:1], min_val=1, max_val=PASSES)
            with dve.If(passes > 1):
                with dve.Fori(1, passes) as q:
                    dve.wait_ge(xg_done, q * (2 * PAIRS + 2))
                    dve.tensor_scalar(slotv[:, 0:2, 0:NE], slotv[:, 0:2, 0:NE], -float(CAP), None, ALU.add)
                    dve.tensor_scalar(slotv[0:64, 2, 0:NE], slotv[0:64, 2, 0:NE], -float(CAP), None, ALU.add)\
                       .then_inc(slots_moved, 1)
                    dve.wait_ge(slots_moved, q)
                    picks(0)
                    for par in range(2):
                        choose(par, par)
                    with dve.Fori(0, PAIRS) as i:
                        pair(q, i)

            dve.wait_ge(part_added, passes * (6 * PAIRS))
            for step in (0, 1, (0,), 2, (1,), (2,)):
                tt = step[0] if isinstance(step, tuple) else step
                r = slice(0, ROWS[tt])
                if step == tt:
                    for c in range(2):
                        ins = dve.bn_stats(stats[r, tt, c, :], yacc[r, tt, HALF * c:HALF * c + HALF])
                    link(ins)
                    moments(tt, 2, 7 + tt)
                else:
                    inverse(tt, 7 + tt)
                    ins = norm_half(link, yacc, tt, 0, lnb[:, 2, :], lnb[:, 3, :])
                    if tt == 2:
                        ins = norm_half(link, yacc, tt, 1, lnb[:, 2, :], lnb[:, 3, :])
                    ins.then_inc(y_left, 1)

        @block.tensor
        def _(pe):
            def opens(*key):
                if TILES[key] >= 8:
                    pe.wait_ge(bank_free[TILES[key] % 8], TILES[key] // 8)
                return bank(*key)

            def contract(out, pairs):
                last = len(pairs) - 1
                for k, (lhsT, rhs) in enumerate(pairs):
                    ins = pe.matmul(out, lhsT, rhs, start=(k == 0), stop=(k == last))
                return ins

            def to_channels(kind, c, rhs, nk=KD):
                per_slot = SLOT // nk // P
                key = kind, c // per_slot
                cols = slice(P * (c % per_slot), P * (c % per_slot) + P)
                hi, lo = parts(*key, k=nk)
                out = opens(kind, c)[:, 0:T]
                for step, (w, x_part) in enumerate(((hi, 0), (hi, 1), (lo, 0))):
                    pe.wait_ge(w_low if step == 2 else w_high, SPLITS.index(key) + 1)
                    for k in range(nk):
                        if (kind, c) == ("v", 0) and step < 2:
                            pe.wait_ge(*((x_high, k + 1), copied("xT", k))[step])
                        ins = pe.matmul(out, w[:, k, cols], rhs[x_part][:, k, :], start=(step + k == 0),
                                        stop=(step == 2 and k == nk - 1))
                ins.then_inc(*fills(kind, c))

            def to_tokens(kind, srcT, high, low):
                def product(out, tokens, s, k, step, **flags):
                    w = parts(kind, s)
                    src, w = ((srcT[0], w[0]), (srcT[1], w[0]), (srcT[0], w[1]))[step]
                    return pe.matmul(out, src[:, k, tokens], w[:, k, :], **flags)

                for s, tt in TOKEN_ORDER:
                    out = opens(kind, s, tt)
                    ss = (s,) if tt < 2 else (s, s + 1)
                    tokens = slice(P * tt, P * tt + ROWS[tt])
                    for j, sj in enumerate(ss):
                        for step in range(3):
                            pe.wait_ge(w_high if step < 2 else w_low, SPLITS.index((kind, sj)) + 1)
                            for k in range(KD):
                                if step < 2 and (s, tt) == (0, 0):
                                    pe.wait_ge((high, low)[step], k + 1)
                                ins = product(out[0:ROWS[tt], 256 * j:256 * j + 256], tokens, sj, k, step,
                                              start=(step + k == 0), stop=(step == 2 and k == KD - 1))
                    ins.then_inc(*fills(kind, s, tt))

            xT, aT, ybT, oT, hT_parts = (xT_hi, xT_lo), (aT_hi, aT_lo), (ybT_hi, ybT_lo), (oT_hi, oT_lo), (hT_hi, hT_lo)
            pe.wait_ge(consts, 10)
            pe.wait_ge(x_in, 48)
            for k in range(KD):
                out = opens("xT", k)
                for tt in range(3):
                    ins = pe.transpose(out[:, P * tt:P * tt + ROWS[tt]], x[0:ROWS[tt], tt, P * k:P * k + P],
                                       ident[0:ROWS[tt], 0:ROWS[tt]])
                ins.then_inc(*fills("xT", k))
            pe.wait_ge(bias_in, 32)
            pe.transpose(opens("bias", 0)[:, 0:52], brow[:, :], ident[0:52, 0:52]).then_inc(*fills("bias", 0))
            for c in range(KD):
                to_channels("v", c, xT)
            to_channels("u", 0, xT)
            for tt in TILE_ORDER:
                for h in range(2):
                    out, m = opens("vt", tt, h), ROWS[tt]
                    for k in range(4):
                        pe.wait_ge(*copied("v", 4 * h + k))
                        ins = pe.transpose(out[0:m, P * k:P * k + P], vT[:, 4 * h + k, P * tt:P * tt + m], ident[:, :])
                    ins.then_inc(*fills("vt", tt, h))
            for c in range(1, KD):
                to_channels("u", c, xT)

            pe.wait_ge(ws_in, 16)
            for i in range(2):
                out = opens("ws", i)
                for g in range(4):
                    ins = pe.transpose(out[:, P * g:P * g + P], wsr[:, 4 * i + g, :], ident[:, :])
                ins.then_inc(*fills("ws", i))
            pe.wait_ge(*loaded("mem", 0))
            memr = slot("mem", 0).rearrange("p (m d) -> p m d", m=2)
            for i in range(4):
                out = opens("mem", i)
                for k in (2 * i, 2 * i + 1):
                    for m in range(2):
                        c = MEM * (k % 2) + P * m
                        ins = pe.transpose(out[:, c:c + P], memr[:, m, P * k:P * k + P], ident[:, :])
                ins.then_inc(*fills("mem", i))

            pe.wait_ge(wsT_ready, 1)
            pe.matmul(opens("bd", 0)[0:64, :], rep8[:, :, :].rearrange("s b t -> s (b t)"),
                      wsT[0:LS, :, 0:LS].unsqueeze(2).broadcast_to([LS, GA, NB, LS]), start=True, stop=True)\
              .then_inc(*fills("bd", 0))
            pe.wait_ge(v_norm, 3)
            pe.wait_ge(*copied("bd", 0))
            for g in range(GA):
                out = opens("mix", g)
                for j in range(2):
                    pe.matmul(out[:, P * j:P * j + P], vn[:, j, P * g:P * g + P], wsT[:, g, :], start=True, stop=True)
                pe.matmul(out[:, SEQ:T], vn[0:64, 2, P * g:P * g + P], bd[:, g, :], start=True, stop=True)\
                  .then_inc(*fills("mix", g))

            for i in range(4):
                pe.wait_ge(*copied("mem", i))
            memT = memT_hi, memT_lo
            for i in range(2):
                w, out = parts("mk", i), opens("mk", i)
                for hh in range(2):
                    for step, (wp, mp) in enumerate(((0, 0), (0, 1), (1, 0))):
                        pe.wait_ge(w_low if wp else w_high, SPLITS.index(("mk", i)) + 1)
                        for k in range(KD):
                            ins = pe.matmul(out[:, MEM * hh:MEM * hh + MEM], w[wp][:, k, P * hh:P * hh + P],
                                            memT[mp][:, k, :], start=(step + k == 0), stop=(step == 2 and k == KD - 1))
                ins.then_inc(*fills("mk", i))
            for i in range(2):
                w, out = parts("mv", i), opens("mv", i)
                for m in range(2):
                    for step, (wp, mp) in enumerate(((0, 0), (0, 1), (1, 0))):
                        pe.wait_ge(w_low if wp else w_high, SPLITS.index(("mv", i)) + 1)
                        for k in range(KD):
                            ins = pe.matmul(out[:, 256 * m:256 * m + 256], memT[mp][:, k, P * m:P * m + P],
                                            w[wp][:, k, :], start=(step + k == 0), stop=(step == 2 and k == KD - 1))
                ins.then_inc(*fills("mv", i))
            for i in range(2):
                pe.wait_ge(*copied("mk", i))
            for m in range(2):
                out = opens("mkp", m)
                for h in range(HEADS):
                    ins = pe.transpose(out[:, P * h:P * h + P], mkT[:, h, P * m:P * m + P], ident[:, :])
                ins.then_inc(*fills("mkp", m))

            for h in range(HEADS):
                to_channels("q", h, xT)
            for g in range(PG):
                to_channels("p", g, xT)
            for h in range(HEADS):
                pe.wait_ge(*copied("q", h))
                out = opens("sc", h)
                for lt in range(2):
                    ins = pe.matmul(out[:, MEM * lt:MEM * lt + MEM], qT[:, h, P * lt:P * lt + P], mkT[:, h, :],
                                    start=True, stop=True)
                ins.then_inc(*fills("sc", h))

            def cache(kind, b):
                return slot(kind, b // 2).rearrange("p (c n) -> p c n", c=4)[:, 2 * (b % 2):2 * (b % 2) + 2, :]

            for hp in range(2):
                for b in range(NB):
                    pe.wait_ge(*loaded("kc", b // 2))
                    out = opens("kt", hp, b)
                    for hh in range(2):
                        for m in range(2):
                            c, h = MEM * hh + P * m, 2 * hp + hh
                            ins = pe.transpose(out[:, c:c + P], cache("kc", b)[:, m, P * h:P * h + P], ident[:, :])
                    ins.then_inc(*fills("kt", hp, b))
                for b in range(NB):
                    pe.wait_ge(*copied("kt", hp, b))
                pe.wait_ge(qmask_ready, hp + 1)
                out = opens("ss", hp)
                for b in range(4):
                    for hh in range(2):
                        for group in range(2):
                            row = 64 * hh + 32 * group
                            col = (4 * group + b) * QSTEP - LS * b
                            ins = pe.matmul(out[row:row + 32, 0:MEM], qmask[:, hh, col:col + 32],
                                            kTs[:, 4 * group + b, hh, :], start=(b == 0), stop=(b == 3))
                ins.then_inc(*fills("ss", hp))

            for kind, h in (("pt", 0), ("pt", 1), ("o", 0), ("pt", 2), ("o", 1), ("pt", 3), ("o", 2), ("o", 3)):
                out = opens(kind, h)
                if kind == "pt":
                    pe.wait_ge(sm_done, h + 1)
                    for m in range(2):
                        for lt in range(2):
                            c = SEQ * m + P * lt
                            ins = pe.transpose(out[:, c:c + P], Pp[:, h, lt, P * m:P * m + P], ident[:, :])
                    ins.then_inc(*fills("pt", h))
                else:
                    pe.wait_ge(*copied("pt", h))
                    for m in range(2):
                        pe.wait_ge(*copied("mv", m))
                    contract(out[:, 0:SEQ], [(mvp[:, m, P * h:P * h + P], PT[:, h % 2, m, :]) for m in range(2)])\
                        .then_inc(*fills("o", h))
            for hp in range(2):
                pe.wait_ge(sm_done, HEADS + hp + 1)
                out = opens("pst", hp)
                for m in range(2):
                    ins = pe.transpose(out[:, P * m:P * m + P], Ps[:, hp, P * m:P * m + P], ident[:, :])
                ins.then_inc(*fills("pst", hp))
            for hp in range(2):
                pe.wait_ge(*copied("pst", hp))
            for i in range(2):
                out = opens("sv", i)
                for m in range(2):
                    for j in range(4):
                        b = 4 * i + j
                        pe.wait_ge(*loaded("vc", b // 2))
                        ins = pe.matmul(out[32 * j:32 * j + 32, :], PTs[:, m, b, :, :].rearrange("p h t -> p (h t)"),
                                        cache("vc", b)[:, m, :], start=(m == 0), stop=(m == 1))
                ins.then_inc(*fills("sv", i))

            pe.wait_ge(hist_in, 16)
            out = opens("hist", 0)
            for g in range(PG):
                ins = pe.transpose(out[:, NB * HIST * g:NB * HIST * (g + 1)], histr[:, P * g:P * g + P],
                                   ident[0:NB * HIST, 0:NB * HIST])
            ins.then_inc(*fills("hist", 0))
            for i in range(2):
                pe.wait_ge(*copied("sv", i))
                out = opens("so", i)
                for h in range(HEADS):
                    ins = pe.transpose(out[:, P * h:P * h + P], sov[:, i, P * h:P * h + P], ident[:, :])
                ins.then_inc(*fills("so", i))
            for g in range(PG):
                pe.wait_ge(*copied("p", g))
            out = opens("pout", 0)
            for g in range(PG):
                ins = pe.transpose(out[:, P * g:P * g + P], pcur[:, g, T - P:T], ident[:, :])
            ins.then_inc(*fills("pout", 0))

            pe.wait_ge(a_low, GA)
            for i in range(4):
                for kind, rhs in (("gA", xT), ("wa", aT)):
                    for c in (2 * i, 2 * i + 1):
                        to_channels(kind, c, rhs)
            pe.wait_ge(const_in, 64)
            for g in range(PG):
                pe.wait_ge(d_ready, g + 1)
                pe.matmul(opens("yb", g)[:, 0:T], wpool[:, g, :], dT[:, g, :], start=True, stop=True)\
                  .then_inc(*fills("yb", g))
            for gk, wk, rhs in (("gB", "wb", ybT), ("gM", "wm", oT)):
                for i in range(2):
                    for c in range(4 * i, 4 * i + 4):
                        to_channels(gk, c, xT)
                    for key in (("yb", c) for c in range(PG)) if wk == "wb" else (
                            ("o", 0), ("o", 1), ("o", 2), ("o", 3), ("so", 0), ("so", 1)):
                        pe.wait_ge(*copied(*key))
                    for c in range(4 * i, 4 * i + 4):
                        to_channels(wk, c, rhs, 4)
            to_tokens("wo", hT_parts, h_high, h_low)

            for key in [key for key in TILES if key[0] in ("x1T", "rt")]:
                tt = key[1]
                m, nth = ROWS[tt], TILE_ORDER.index(tt) + 1
                out = opens(*key)
                if key[0] == "x1T":
                    pe.wait_ge((x1_left, x1_right)[key[2]], nth)
                    for k in range(4):
                        c = 512 * key[2] + P * k
                        ins = pe.transpose(out[:, m * k:m * k + m], x[0:m, tt, c:c + P], ident[0:m, 0:m])
                else:
                    for h in range(2):
                        pe.wait_ge(*copied("x1T", tt, h))
                    ins = contract(out[0:m, 0:NE], [(x1T[:, k, P * tt:P * tt + m], wr[:, k, :]) for k in range(KD)])
                ins.then_inc(*fills(*key))
            pe.wait_ge(mask_ready, 1)
            out = opens("rank", 0)
            for tt in range(4):
                m = ROWS[tt] if tt < 3 else P
                pairs = [(ones[0:ROWS[j], 0:m], mask[0:ROWS[j], j, :]) for j in range(tt)]
                if tt < 3:
                    pairs.append((upper[0:m, 0:m], mask[0:m, tt, :]))
                ins = contract(out[0:m, NE * tt:NE * tt + NE], pairs)
            ins.then_inc(*fills("rank", 0))
            for key, n in TILES.items():
                if n >= len(TILES) - 8:
                    pe.wait_ge(*copied(*key))

            def gather(g, h):
                pe.wait_ge(pick_ready, g + 1)
                for k in range(4):
                    c = 512 * h + P * k
                    ins = contract(ps[:, XG + h, P * k:P * k + P],
                                   [(x[0:ROWS[tt], tt, c:c + P],
                                     pick[0:ROWS[tt], tt, :, :].rearrange("p e s -> p (e s)")) for tt in range(3)])
                ins.then_inc(xg_done, 1)

            def pair(q, i):
                n = q * PAIRS + i
                g = q * (PAIRS + 1) + i
                for par in range(2):
                    e = 2 * n + par
                    if par == 0:
                        pe.wait_ge(xg_ready, 2 * g + 1)
                    pe.wait_ge(sel_ready, 2 * g + par + 1)
                    parts = [(GB, 0), (GB, 1), (LB, 0), (LB, 1)]
                    for p, (b, hh) in enumerate(parts):
                        pe.matmul(ps[CAP * hh:CAP * hh + CAP, b, :], sel[:, par, :], b1s[:, 512 * p:512 * p + 512],
                                  start=True, stop=False)
                    for k in range(KD):
                        w1_slot = EXPERT_SLOTS[k]
                        if k == KD // 2:
                            if par == 0:
                                pe.wait_ge(xg_ready, 2 * g + 2)
                            if par == 1:
                                pe.wait_ge(y_left_out, e)
                                pe.wait_ge(y_right_out, e)
                            for dh in range(2):
                                pe.matmul(ps[CAP * dh:CAP * dh + CAP, YB, :], sel[:, par, :],
                                          b2s[:, 512 * dh:512 * dh + 512], start=True, stop=False)
                        pe.wait_ge(slot_full[w1_slot], 16 * (e + HEAD_LOADS[w1_slot] + 1))
                        for p, (b, hh) in enumerate(parts):
                            ins = pe.matmul(ps[CAP * hh:CAP * hh + CAP, b, :], xg[:, k, par, :],
                                            ring[:, w1_slot, 512 * p:512 * p + 512], start=False, stop=(k == KD - 1))
                        ins.then_inc(slot_free if k < KD - 1 else up_done, 1)
                    gather(g + 1, par)
                    pe.wait_ge(act_ready, e + 1)
                    for c in range(4):
                        ins = pe.transpose(ps[:, AT, P * c:P * c + P], act_s[:, P * c:P * c + P], ident[:, :])
                    ins.then_inc(act_turned, 1)
                    if par == 1:
                        pe.wait_ge(pickg_ready, n + 1)
                        for tt in range(3):
                            ins = pe.transpose(ps[:, ST, P * tt:P * tt + ROWS[tt]],
                                               pickg[0:ROWS[tt], tt, :, :].rearrange("p e s -> p (e s)"),
                                               ident[0:ROWS[tt], 0:ROWS[tt]])
                        ins.then_inc(pickT_turned, 1)
                    pe.wait_ge(actT_ready, e + 1)
                    for j in range(KD, RING):
                        w2_slot, w2_spare = EXPERT_SLOTS[j], j - (RING - 2)
                        w = ring[:, w2_slot, :]
                        if w2_spare < 0:
                            pe.wait_ge(slot_full[w2_slot], 16 * (e + HEAD_LOADS[w2_slot] + 1))
                        elif par == 0:
                            pe.wait_ge(slot_full[w2_slot], 16 * (n + HEAD_LOADS[w2_slot] + 1))
                        else:
                            pe.wait_ge(spare_full[w2_spare], 16 * (n + 1))
                            w = spare[w2_spare][:, :]
                        w = w.rearrange("p (k n) -> p k n", k=2)
                        for kk in range(2):
                            f = 2 * (j - KD) + kk
                            for dh in range(2):
                                ins = pe.matmul(ps[CAP * dh:CAP * dh + CAP, YB, :], actT[:, f % 4, f // 4, :],
                                                w[:, kk, 512 * dh:512 * dh + 512], start=False, stop=(f == KD - 1))
                        ins.then_inc(slot_free if j < RING - 1 else y_done, 1)
                pe.wait_ge(pickT_ready, n + 1)
                pe.wait_ge(y_left_out, 2 * n + 2)
                pe.wait_ge(y_right_out, 2 * n + 2)
                for t in range(6):
                    tt, dh = t // 2, t % 2
                    if t >= 2:
                        pe.wait_ge(part_added, 6 * n + t - 1)
                    pe.matmul(ps[0:ROWS[tt], O0 + t % 2, :], pickT[:, P * tt:P * tt + ROWS[tt]],
                              ypair[:, 512 * dh:512 * dh + 512], start=True, stop=True).then_inc(part_done, 1)

            for h in range(2):
                gather(0, h)
            pe.wait_ge(ebias_ready, 1)
            with pe.Fori(0, PAIRS) as i:
                pair(0, i)
            pe.wait_ge(npass_ready, 1)
            passes = pe.value_load(npass[0:1, 0:1], min_val=1, max_val=PASSES)
            with pe.If(passes > 1):
                with pe.Fori(1, passes) as q:
                    for h in range(2):
                        gather(q * (PAIRS + 1), h)
                    with pe.Fori(0, PAIRS) as i:
                        pair(q, i)


_INS = ['x_prompt', 'x_sample', 'state_pool', 'cache_mem_k', 'cache_mem_v', 'mem_prompt', 'w_in', 'b_in', 'ln_v_g',
        'ln_v_b', 'w_s', 'b_s', 'w_a_out', 'w_pool', 'ls_pool', 'w_b_out', 'w_mk', 'w_mv', 'w_m_out', 'w_o', 'ln1_g',
        'ln1_b', 'w_r', 'b_r', 'w1', 'b1', 'w2', 'b2', 'ln2_g', 'ln2_b']
_OUTS = [('y_p', (SEQ, D), (1, SEQ, D)), ('y_s', (NB * LS, D), (NB, LS, D)),
         ('pool_p', (HIST, 512), (1, 1, HIST, 512)), ('pool_s', (NB, HIST, 512), (1, NB, HIST, 512)),
         ('mk', (MEM, 512), (1, 1, MEM, HEADS, P)), ('mv', (MEM, 512), (1, 1, MEM, HEADS, P)),
         ('cv', (NB * LS, D), (1, NB, LS, D))]


def kernel(**inputs):
    import numpy as _np
    import concourse.bacc as _bacc
    from concourse import mybir as _mybir
    from concourse.bass_utils import run_bass_kernel_spmd as _run

    nc = _bacc.Bacc("TRN2", target_bir_lowering=False, num_devices=1)
    arrays, ins, outs = {}, {}, {}
    for name in _INS:
        v = _np.ascontiguousarray(inputs[name])
        v = v.reshape(-1, D) if name == 'x_sample' else v.reshape(v.shape[1:])
        arrays[f"in_{name}"] = v
        ins[name] = nc.dram_tensor(f"in_{name}", v.shape, _mybir.dt.from_np(v.dtype), kind="ExternalInput").ap()
    for name, shape, _ in _OUTS:
        outs[name] = nc.dram_tensor(f"out_{name}", shape, F32, kind="ExternalOutput").ap()
    build(nc, ins, outs)
    r = _run(nc, [arrays], core_ids=[0])
    return tuple(_np.asarray(r.results[0][f"out_{name}"]).reshape(shape) for name, _, shape in _OUTS)
```
